# Optimizing a Trainium2 kernel written in Bass

```python
import math
import jax
import jax.numpy as jnp
from jax import lax
import numpy as np

D_MODEL = 1024
BATCH = 1
SEQ = 256
DEPTH = 1
DEC_BATCH = 8
DEC_SEQ = 8
PAST_LEN = 256
PAGE_SIZE = 128

PLE_DIM = 256
BRANCH_WIDTH = D_MODEL
A_WIDTH = BRANCH_WIDTH
A_GROUPS = 4
A_GROUP_WIDTH = A_WIDTH // A_GROUPS
CHUNK = 128
N_HEADS = 16
HEAD_DIM = BRANCH_WIDTH // N_HEADS
N_KV_HEADS = 4
HEADS_PER_KV = N_HEADS // N_KV_HEADS
CMP_LEN = 32
CMP_STRIDE = 16
CMP_HIDDEN = 256
SEL_LEN = 64
SEL_TOP = 16
SEL_QBLOCK = 64
WINDOW = 512
WIN_QBLOCK = 128
N_BUCKETS = 32
MAX_DISTANCE = 128
N_GROUPS = 4
EXPERTS_PER_GROUP = 8
N_EXPERTS = N_GROUPS * EXPERTS_PER_GROUP
TOP_K = 2
D_EXPERT = 512
MOE_BLOCK = 128
N_KV_SLOTS = 6
N_CACHE_SLOTS = 4
KV_COLS = N_KV_SLOTS * N_KV_HEADS * HEAD_DIM
NSA_GATE_COLS = 3 * N_HEADS
MERGE_GATE_COLS = 2 * D_MODEL
SPLIT_POINTS = (A_WIDTH, 2 * A_WIDTH, 2 * A_WIDTH + BRANCH_WIDTH,
                2 * A_WIDTH + BRANCH_WIDTH + KV_COLS,
                2 * A_WIDTH + BRANCH_WIDTH + KV_COLS + NSA_GATE_COLS)
IN_COLS = SPLIT_POINTS[-1] + MERGE_GATE_COLS
EPS = 1e-6
NEG = -1e30
FORCE = 1e9

kernel_name = 'hybrid_gmlp_nsa_hmoe_step'

def rms_norm(x, gain):
    xf = x.astype(jnp.float32)
    xf = xf * lax.rsqrt(jnp.mean(xf * xf, axis=-1, keepdims=True) + EPS)
    return (xf * gain.astype(jnp.float32)).astype(x.dtype)

def rel_bucket(dist):
    n = jnp.maximum(jnp.asarray(dist, jnp.int32), 0)
    max_exact = N_BUCKETS // 2
    nf = jnp.maximum(n, max_exact).astype(jnp.float32)
    large = max_exact + (jnp.log(nf / max_exact) / math.log(MAX_DISTANCE / max_exact)
                         * (N_BUCKETS - max_exact)).astype(jnp.int32)
    return jnp.where(n < max_exact, n, jnp.minimum(large, N_BUCKETS - 1))

def chunk_mlp(u, v, w_s, b_s):
    b, s = u.shape[:2]
    length = min(s, CHUNK)
    n_chunks = s // length
    causal = np.tril(np.ones((length, length), np.float32))
    w = w_s[:, :length, :length] * causal
    vg = v.reshape(b, n_chunks, length, A_GROUPS, A_GROUP_WIDTH)
    mixed = jnp.einsum('grs,bcsgw->bcrgw', w, vg) + b_s[:, :length].T[None, None, :, :, None]
    return u * mixed.reshape(b, s, A_WIDTH)

def compress(rows, pe, w1, w2):
    b, t = rows.shape[:2]
    n_cmp = (t - CMP_LEN) // CMP_STRIDE + 1
    idx = np.arange(n_cmp)[:, None] * CMP_STRIDE + np.arange(CMP_LEN)[None]
    blk = rows[:, idx] + pe[None, None, :, None, :]
    flat = blk.transpose(0, 1, 3, 2, 4).reshape(b, n_cmp, N_KV_HEADS, CMP_LEN * HEAD_DIM)
    return jax.nn.gelu(flat @ w1) @ w2

def cmp_sel_attn(q, hist, q_pos, rel_bias, pe_cmp, w_phi1, w_phi2):
    b, sq = q.shape[:2]
    t = hist.shape[1]
    scale = HEAD_DIM ** -0.5
    k_c = compress(hist[:, :, 0], pe_cmp[0], w_phi1[0], w_phi2[0])
    v_c = compress(hist[:, :, 1], pe_cmp[1], w_phi1[1], w_phi2[1])
    n_cmp = k_c.shape[1]
    c_start = np.arange(n_cmp) * CMP_STRIDE
    dist = q_pos[:, None] - (c_start + CMP_LEN - 1)[None]
    valid = dist >= 0
    bias = rel_bias[rel_bucket(dist)].reshape(sq, n_cmp, N_KV_HEADS, HEADS_PER_KV).transpose(2, 3, 0, 1)
    s = jnp.einsum('bqghd,bcgd->bghqc', q, k_c).astype(jnp.float32) * scale + bias
    p_cmp = jax.nn.softmax(jnp.where(valid, s, NEG), axis=-1) * valid
    o_cmp = jnp.einsum('bghqc,bcgd->bqghd', p_cmp.astype(v_c.dtype), v_c)
    n_sel = -(-t // SEL_LEN)
    s_start = np.arange(n_sel) * SEL_LEN
    overlap = ((c_start[:, None] < s_start[None] + SEL_LEN)
               & (c_start[:, None] + CMP_LEN > s_start[None])).astype(np.float32)
    importance = jnp.einsum('bghqc,cj->bgqj', p_cmp, overlap)
    q_blk = q_pos // SEL_LEN
    j = np.arange(n_sel)[None]
    forced = (j == 0) | (j == q_blk[:, None]) | (j == q_blk[:, None] - 1)
    causal_blk = j <= q_blk[:, None]
    score = jnp.where(forced, FORCE, jnp.where(causal_blk, importance, NEG))
    n_top = min(SEL_TOP, n_sel)
    sel = lax.top_k(score, n_top)[1].transpose(0, 2, 1, 3)
    pad = n_sel * SEL_LEN - t

    def to_blocks(r):
        r = jnp.pad(r, ((0, 0), (0, pad), (0, 0), (0, 0)))
        return r.reshape(b, n_sel, SEL_LEN, N_KV_HEADS, HEAD_DIM).transpose(0, 3, 1, 2, 4)

    k_s = to_blocks(hist[:, :, 2])
    v_s = to_blocks(hist[:, :, 3])
    rb_g = rel_bias.reshape(N_BUCKETS, N_KV_HEADS, HEADS_PER_KV).transpose(1, 0, 2)
    bi = jnp.arange(b)[:, None, None, None]
    gi = jnp.arange(N_KV_HEADS)[None, None, :, None]
    offs = jnp.arange(SEL_LEN)
    n_keys = n_top * SEL_LEN

    def select_block(args):
        q_b, sel_b, pos_b = args
        qb = q_b.shape[1]
        k_g = k_s[bi, gi, sel_b].reshape(b, qb, N_KV_HEADS, n_keys, HEAD_DIM)
        v_g = v_s[bi, gi, sel_b].reshape(b, qb, N_KV_HEADS, n_keys, HEAD_DIM)
        k_pos = (sel_b[..., None] * SEL_LEN + offs).reshape(b, qb, N_KV_HEADS, n_keys)
        d = pos_b[None, :, None, None] - k_pos
        bias_b = rb_g[gi, rel_bucket(d)]
        s_b = jnp.einsum('bqghd,bqgkd->bqghk', q_b, k_g).astype(jnp.float32) * scale
        s_b = s_b + jnp.swapaxes(bias_b, -1, -2)
        p_b = jax.nn.softmax(jnp.where((d >= 0)[:, :, :, None, :], s_b, NEG), axis=-1)
        return jnp.einsum('bqghk,bqgkd->bqghd', p_b.astype(v_g.dtype), v_g)

    qb = math.gcd(sq, SEL_QBLOCK)
    nqb = sq // qb
    o = lax.map(select_block, (
        jnp.moveaxis(q.reshape(b, nqb, qb, N_KV_HEADS, HEADS_PER_KV, HEAD_DIM), 1, 0),
        jnp.moveaxis(sel.reshape(b, nqb, qb, N_KV_HEADS, n_top), 1, 0),
        jnp.asarray(q_pos.reshape(nqb, qb), jnp.int32)))
    o_slc = jnp.moveaxis(o, 0, 1).reshape(b, sq, N_KV_HEADS, HEADS_PER_KV, HEAD_DIM)
    return o_cmp, o_slc

def window_attn(q, k, v, q_pos, k_pos, rel_bias):
    dist = q_pos[:, :, None] - k_pos[:, None, :]
    valid = (dist >= 0) & (dist < WINDOW) & (k_pos[:, None, :] >= 0)
    nb, qb, kw = dist.shape
    bias = rel_bias[rel_bucket(dist)].reshape(nb, qb, kw, N_KV_HEADS, HEADS_PER_KV).transpose(0, 3, 4, 1, 2)
    s = jnp.einsum('bnqghd,bnkgd->bnghqk', q, k).astype(jnp.float32) * HEAD_DIM ** -0.5 + bias
    p = jax.nn.softmax(jnp.where(valid[:, None, None], s, NEG), axis=-1)
    return jnp.einsum('bnghqk,bnkgd->bnqghd', p.astype(v.dtype), v)

def moe_ffn(h, w_rg, b_rg, w_re, b_re, w_gate, w_up, w_down):
    n, d = h.shape
    logit_g = (h @ w_rg).astype(jnp.float32) + b_rg.astype(jnp.float32)
    grp = jnp.argmax(logit_g, axis=-1)
    p_grp = jnp.take_along_axis(jax.nn.softmax(logit_g, axis=-1), grp[:, None], axis=-1)
    logit_e = ((h @ w_re).astype(jnp.float32) + b_re.astype(jnp.float32)).reshape(n, N_GROUPS, EXPERTS_PER_GROUP)
    logit_e = jnp.take_along_axis(logit_e, grp[:, None, None], axis=1)[:, 0]
    top_val, top_idx = lax.top_k(logit_e, TOP_K)
    weight = p_grp * jax.nn.softmax(top_val, axis=-1)
    expert = (grp[:, None] * EXPERTS_PER_GROUP + top_idx).reshape(-1).astype(jnp.int32)
    token = jnp.repeat(jnp.arange(n, dtype=jnp.int32), TOP_K)
    n_assign = n * TOP_K
    one_hot = jax.nn.one_hot(expert, N_EXPERTS, dtype=jnp.int32)
    counts = jnp.sum(one_hot, axis=0)
    rank = jnp.take_along_axis(jnp.cumsum(one_hot, axis=0), expert[:, None], axis=1)[:, 0] - 1
    padded = (counts + MOE_BLOCK - 1) // MOE_BLOCK * MOE_BLOCK
    pad_end = jnp.cumsum(padded)
    dest = (pad_end - padded)[expert] + rank
    n_blocks = -(-n_assign // MOE_BLOCK) + N_EXPERTS
    cap = n_blocks * MOE_BLOCK
    slot_tok = jnp.full((cap,), n, jnp.int32).at[dest].set(token)
    slot_w = jnp.zeros((cap,), h.dtype).at[dest].set(weight.reshape(-1).astype(h.dtype))
    block_expert = jnp.minimum(
        jnp.searchsorted(pad_end, jnp.arange(n_blocks, dtype=jnp.int32) * MOE_BLOCK, side='right'),
        N_EXPERTS - 1)
    h_pad = jnp.concatenate([h, jnp.zeros((1, d), h.dtype)], axis=0)

    def expert_block(args):
        tok, e, w = args
        xb = h_pad[tok]
        y = (jax.nn.silu(xb @ w_gate[e]) * (xb @ w_up[e])) @ w_down[e]
        return y * w[:, None]

    y = lax.map(expert_block, (slot_tok.reshape(n_blocks, MOE_BLOCK), block_expert,
                               slot_w.reshape(n_blocks, MOE_BLOCK)))
    out = jnp.zeros((n + 1, d), h.dtype).at[slot_tok].add(y.reshape(cap, d))
    return out[:n]

def layer_forward(x, pemb, past_kv, past_win, rel_bias, lp):
    (norm_mix, w_in, v_norm, w_spatial, b_spatial, pe_cmp, w_phi1, w_phi2, w_branch, w_out,
     norm_ffn, w_rg, b_rg, w_re, b_re, w_gate, w_up, w_down, norm_ple, w_ple_gate, w_ple_proj) = lp
    b, s, _ = x.shape
    past_len = 0 if past_kv is None else past_kv.shape[1]
    q_pos = past_len + np.arange(s)
    h = rms_norm(x, norm_mix)
    u, v, q, kv, g_nsa, g_merge = jnp.split(h @ w_in, SPLIT_POINTS, axis=-1)
    v_rows = rms_norm(jax.nn.gelu(v), v_norm)
    o_a = chunk_mlp(jax.nn.gelu(u), v_rows, w_spatial, b_spatial)
    q = q.reshape(b, s, N_KV_HEADS, HEADS_PER_KV, HEAD_DIM)
    kv = kv.reshape(b, s, N_KV_SLOTS, N_KV_HEADS, HEAD_DIM)
    kv_new = kv[:, :, :N_CACHE_SLOTS]
    kv_win = kv[:, :, N_CACHE_SLOTS:]
    hist = kv_new if past_kv is None else jnp.concatenate([past_kv, kv_new], axis=1)
    o_cmp, o_slc = cmp_sel_attn(q, hist, q_pos, rel_bias, pe_cmp, w_phi1, w_phi2)
    if past_win is None:
        qb = math.gcd(s, WIN_QBLOCK)
        nb = s // qb
        k_idx = np.arange(nb)[:, None] * qb + np.arange(WINDOW + qb)[None]
        win_pad = jnp.pad(kv_win, ((0, 0), (WINDOW, 0), (0, 0), (0, 0), (0, 0)))
        k_blk = win_pad[:, k_idx]
        k_pos = k_idx - WINDOW
        win_state = kv_win[:, s - min(WINDOW, s):]
    else:
        w_buf = past_win.shape[1]
        rows = jnp.concatenate([past_win, kv_win], axis=1)
        qb, nb = s, 1
        k_blk = rows[:, None]
        k_pos = (past_len - w_buf + np.arange(w_buf + s))[None]
        win_state = rows[:, s:]
    o_win = window_attn(q.reshape(b, nb, qb, N_KV_HEADS, HEADS_PER_KV, HEAD_DIM),
                        k_blk[:, :, :, 0], k_blk[:, :, :, 1], q_pos.reshape(nb, qb), k_pos,
                        rel_bias).reshape(b, s, N_KV_HEADS, HEADS_PER_KV, HEAD_DIM)
    gates = jax.nn.sigmoid(g_nsa).reshape(b, s, 3, N_KV_HEADS, HEADS_PER_KV, 1)
    o_b = (gates[:, :, 0] * o_cmp + gates[:, :, 1] * o_slc + gates[:, :, 2] * o_win).reshape(b, s, BRANCH_WIDTH)
    gm = jax.nn.sigmoid(g_merge).reshape(b, s, 2, D_MODEL)
    merged = gm[:, :, 0] * (o_a @ w_branch[0]) + gm[:, :, 1] * (o_b @ w_branch[1])
    x = x + merged @ w_out
    h2 = rms_norm(x, norm_ffn).reshape(b * s, D_MODEL)
    x = x + moe_ffn(h2, w_rg, b_rg, w_re, b_re, w_gate, w_up, w_down).reshape(b, s, D_MODEL)
    gate = jax.nn.sigmoid(rms_norm(x, norm_ple) @ w_ple_gate)
    x = x + gate * (pemb @ w_ple_proj)
    return x, kv_new, win_state, v_rows

def setup_inputs(seed: int = 0) -> dict:
    key = jax.random.key(seed)
    ks = jax.random.split(key, 32)

    def nrm(k, shape, scale):
        return jax.random.normal(k, shape, jnp.float32) * scale

    n_pages = PAST_LEN // PAGE_SIZE
    n_used = DEC_BATCH * n_pages
    n_pool = n_used + n_used // 4 + 1
    perm = jax.random.permutation(ks[0], n_pool)
    page_table = perm[:n_used].reshape(DEC_BATCH, n_pages).astype(jnp.int32)
    w_buf = min(WINDOW, PAST_LEN)
    return {
        'x_prompt': nrm(ks[1], (BATCH, SEQ, D_MODEL), 1.0),
        'x_sample': nrm(ks[2], (DEC_BATCH, DEC_SEQ, D_MODEL), 1.0),
        'cache_kv': nrm(ks[3], (DEPTH, n_pool, PAGE_SIZE, N_CACHE_SLOTS, N_KV_HEADS, HEAD_DIM), 1.0),
        'state_win_kv': nrm(ks[4], (DEPTH, DEC_BATCH, w_buf, 2, N_KV_HEADS, HEAD_DIM), 1.0),
        'page_table': page_table,
        'p_prompt': nrm(ks[5], (DEPTH, BATCH, SEQ, PLE_DIM), 1.0),
        'p_sample': nrm(ks[6], (DEPTH, DEC_BATCH, DEC_SEQ, PLE_DIM), 1.0),
        'rel_bias': nrm(ks[7], (N_BUCKETS, N_HEADS), 0.5),
        'norm_mix': 1.0 + nrm(ks[8], (DEPTH, D_MODEL), 0.02),
        'w_in': nrm(ks[9], (DEPTH, D_MODEL, IN_COLS), D_MODEL ** -0.5),
        'v_norm': 1.0 + nrm(ks[10], (DEPTH, A_WIDTH), 0.02),
        'w_spatial': nrm(ks[11], (DEPTH, A_GROUPS, CHUNK, CHUNK), CHUNK ** -0.5),
        'b_spatial': 1.0 + nrm(ks[12], (DEPTH, A_GROUPS, CHUNK), 0.1),
        'pe_cmp': nrm(ks[13], (DEPTH, 2, CMP_LEN, HEAD_DIM), 0.1),
        'w_phi1': nrm(ks[14], (DEPTH, 2, CMP_LEN * HEAD_DIM, CMP_HIDDEN), (CMP_LEN * HEAD_DIM) ** -0.5),
        'w_phi2': nrm(ks[15], (DEPTH, 2, CMP_HIDDEN, HEAD_DIM), CMP_HIDDEN ** -0.5),
        'w_branch': nrm(ks[16], (DEPTH, 2, BRANCH_WIDTH, D_MODEL), BRANCH_WIDTH ** -0.5),
        'w_out': nrm(ks[17], (DEPTH, D_MODEL, D_MODEL), D_MODEL ** -0.5),
        'norm_ffn': 1.0 + nrm(ks[18], (DEPTH, D_MODEL), 0.02),
        'w_router_group': nrm(ks[19], (DEPTH, D_MODEL, N_GROUPS), D_MODEL ** -0.5),
        'b_router_group': nrm(ks[20], (DEPTH, N_GROUPS), 0.01),
        'w_router_expert': nrm(ks[21], (DEPTH, D_MODEL, N_EXPERTS), D_MODEL ** -0.5),
        'b_router_expert': nrm(ks[22], (DEPTH, N_EXPERTS), 0.01),
        'w_exp_gate': nrm(ks[23], (DEPTH, N_EXPERTS, D_MODEL, D_EXPERT), D_MODEL ** -0.5),
        'w_exp_up': nrm(ks[24], (DEPTH, N_EXPERTS, D_MODEL, D_EXPERT), D_MODEL ** -0.5),
        'w_exp_down': nrm(ks[25], (DEPTH, N_EXPERTS, D_EXPERT, D_MODEL), D_EXPERT ** -0.5),
        'norm_ple': 1.0 + nrm(ks[26], (DEPTH, D_MODEL), 0.02),
        'w_ple_gate': nrm(ks[27], (DEPTH, D_MODEL, D_MODEL), D_MODEL ** -0.5),
        'w_ple_proj': nrm(ks[28], (DEPTH, PLE_DIM, D_MODEL), PLE_DIM ** -0.5),
        'final_norm': 1.0 + nrm(ks[29], (D_MODEL,), 0.02),
    }

def reference(x_prompt, x_sample, cache_kv, state_win_kv, page_table, p_prompt, p_sample, rel_bias,
              norm_mix, w_in, v_norm, w_spatial, b_spatial, pe_cmp, w_phi1, w_phi2, w_branch, w_out,
              norm_ffn, w_router_group, b_router_group, w_router_expert, b_router_expert,
              w_exp_gate, w_exp_up, w_exp_down, norm_ple, w_ple_gate, w_ple_proj, final_norm):
    x_p, x_s = x_prompt, x_sample
    kv_p, kv_s, win_p, win_s, v_s = [], [], [], [], []
    for i in range(DEPTH):
        lp = (norm_mix[i], w_in[i], v_norm[i], w_spatial[i], b_spatial[i], pe_cmp[i], w_phi1[i], w_phi2[i],
              w_branch[i], w_out[i], norm_ffn[i], w_router_group[i], b_router_group[i],
              w_router_expert[i], b_router_expert[i], w_exp_gate[i], w_exp_up[i], w_exp_down[i],
              norm_ple[i], w_ple_gate[i], w_ple_proj[i])
        x_p, kv_new_p, win_new_p, _ = layer_forward(x_p, p_prompt[i], None, None, rel_bias, lp)
        kv_p.append(kv_new_p)
        win_p.append(win_new_p)
        past_kv = cache_kv[i][page_table].reshape(page_table.shape[0], -1, N_CACHE_SLOTS, N_KV_HEADS, HEAD_DIM)
        x_s, kv_new_s, win_new_s, v_rows_s = layer_forward(x_s, p_sample[i], past_kv, state_win_kv[i], rel_bias, lp)
        kv_s.append(kv_new_s)
        win_s.append(win_new_s)
        v_s.append(v_rows_s)
    y_prompt = rms_norm(x_p, final_norm)
    y_sample = rms_norm(x_s, final_norm)
    kv_rows_prompt = jnp.stack(kv_p)
    kv_rows_sample = jnp.stack(kv_s)
    win_prompt = jnp.stack(win_p)
    win_sample = jnp.stack(win_s)
    chunk_v_sample = jnp.stack(v_s)
    return (y_prompt, y_sample, kv_rows_prompt, kv_rows_sample, win_prompt, win_sample, chunk_v_sample)


_drawn_inputs = setup_inputs


def setup_inputs(seed=0):
    import zlib

    import numpy as np

    out = dict(_drawn_inputs(seed))
    spreads = {}
    factors = {'norm_mix': 2.914,
     'v_norm': 8.609,
     'pe_cmp': 2.791,
     'b_router_group': 19.239,
     'b_router_expert': 31.275,
     'norm_ple': 64.0,
     'final_norm': 8.516,
     'norm_ffn': 4.776}
    for name, (base, spread) in spreads.items():
        noise = np.random.default_rng([zlib.crc32(name.encode()), seed]).standard_normal(out[name].shape)
        drawn = base * np.exp(spread * noise) if base else spread * noise
        out[name] = jnp.asarray(drawn.astype(out[name].dtype))
    for name, factor in factors.items():
        out[name] = (out[name] * factor).astype(out[name].dtype)
    return out
```

```python
from contextlib import ExitStack

import numpy as np

import concourse.bass as bass
from concourse import mybir

F32 = mybir.dt.float32
I32 = mybir.dt.int32
U32 = mybir.dt.uint32
ALU = mybir.AluOpType
ACT = mybir.ActivationFunctionType
AX = mybir.AxisListType

D = 1024
KT = D // 128
NP, NS, NB = 256, 64, 8
NQ = NS // NB
N = NP + NS
PAST = 256
H, G, HPG, DH = 16, 4, 4, 64
NC = 15
NSEQ = 1 + NB
XROWS = G * NSEQ + 1
BUCKETS, MAX_DISTANCE = 32, 128
MAXD = PAST + NQ - 1
TABN = MAXD + 1 + 127
NE, EPG, NG, DE = 32, 8, 4, 512
SLOTS = 64
EXTRA = N // SLOTS - 1
MORE = N - SLOTS
EPS = 1e-6
NEG = -1e30
TILES = ((0, 128), (128, 128), (256, 64))
CU, CV_, CQ, CKV, CGN, CGM = 0, 1024, 2048, 3072, 4608, 4656

K_ID, K_UP, K_BLK, K_REP, K_IOTA, K_E, K_VALID = 0, 128, 256, 320, 384, 704, 736
K_ALL = 737


def shape_constants():
    c = np.zeros((128, K_ALL), np.float32)
    r = np.arange(128)
    c[:, K_ID:K_ID + 128] = np.eye(128)
    c[:, K_UP:K_UP + 128] = r[:, None] <= r[None, :]
    s = np.arange(64)
    c[:64, K_BLK:K_BLK + 64] = s[:, None] // NQ == s[None, :] // NQ
    c[:NQ, K_REP:K_REP + 64] = np.arange(NQ)[:, None] == s[None, :] % NQ
    c[:, K_IOTA:K_IOTA + N] = np.arange(N)
    c[:, K_E:K_E + NE] = np.arange(NE)
    c[:, K_VALID] = r >= 31
    dist = MAXD - np.arange(TABN)
    n = np.maximum(dist, 0)
    half = BUCKETS // 2
    nf = np.maximum(n, half).astype(np.float32)
    big = half + (np.log(nf / half) / np.float32(np.log(MAX_DISTANCE / half)) * half).astype(np.int32)
    bucket = np.where(n < half, n, np.minimum(big, BUCKETS - 1))
    hot = np.zeros((BUCKETS + 1, TABN), np.float32)
    hot[bucket, np.arange(TABN)] = dist >= 0
    hot[BUCKETS] = dist < 0
    other = np.where(np.arange(NB)[:, None] == s[None, :] // NQ, 0.0, NEG).astype(np.float32)
    return c, hot, other


def psum_plan():
    jobs = [("cols", 1), ("tab", 1)]
    jobs += [(("hT", k), 1) for k in range(KT)]
    jobs += [(("kv", c, s), 1) for c in range(3) for s in range(3)]
    jobs += [("gates", 2), (("ktp", 0), 1), (("ktp", 1), 1), ("ktn", 1)]
    jobs += [(("xt", s, kv), 1) for s in range(NSEQ) for kv in range(2)]
    jobs += [(("h1", kv, hid, half), 1 + (half == 1) + (kv == 1)) for kv in range(2) for hid in range(2) for half in (1, 0)]
    jobs += [(("kc", half), 2) for half in range(2)] + [("vcs", 1), ("vcp", 1)]
    jobs += [(("q", m), 2) for m in range(KT)]
    jobs += [(("sc", qt, par), 1) for qt in range(2) for par in range(2)] + [("scs", 1)]
    jobs += [(("pct", 0), 1), (("pct", 1), 1), ("pcts", 1)]
    for i in range(34):
        if i < 32:
            jobs.append((("s", i), 1))
        if 1 <= i <= 32:
            jobs.append((("pt", i - 1), 1))
        if i >= 2 and i % 2 == 0:
            jobs.append((("o", (i - 2) // 2), 1))
    for b in range(NB + 1):
        if b < NB:
            jobs += [(("ktb", b, 0), 1), (("ktb", b, 1), 1)]
        if b >= 1:
            jobs += [(("pts", b - 1, 0), 2), (("pts", b - 1, 1), 2)]
        if b < NB:
            jobs += [(("ss", b), 1), (("sn", b), 1)]
        if b >= 1:
            jobs += [(("os", b - 1), 2)]
    jobs += [(("v", c, t), 1) for c in range(2) for t in range(3)]
    jobs += [("ws", 1), ("wss", 1)]
    jobs += [(("u", m), 1) for m in range(KT)]
    jobs += [(("gm", m), 1) for m in range(2 * KT)]
    jobs += [(("mx", m), 2) for m in range(KT)]
    jobs += [(("br", j, m), 1) for j in range(2) for m in range(KT)]
    jobs += [(("xo", c, t), 1) for c in range(2) for t in range(3)]
    jobs += [(("hT2", k), 1) for k in range(KT)] + [("router", 2)]
    jobs += [(("ppT", k), 1) for k in range(2)]
    jobs += [(("pp", c, t), 1) for c in range(2) for t in range(3)] + [("rank", 1)]
    tail = [(("hT3", k), 1) for k in range(KT)] + [(("pg", c, t), 1) for c in range(2) for t in range(3)]
    plan, full, read = {}, [0] * 8, [0] * 8
    for n, (name, releases) in enumerate(jobs + tail):
        bank = n % 8
        full[bank] += 1
        plan[name] = (bank, full[bank], read[bank], read[bank] + releases)
        read[bank] += releases
        if n == len(jobs) - 1:
            plan["expert loop"] = list(read)
    return plan


def ring_plan():
    e = [(("kv", 0), 0, ("kv", 0, 2)), (("kv", 1), 1, ("kv", 1, 2)), (("kv", 2), 2, ("kv", 2, 2)),
         (("w1", 0), 3, ("h1", 0, 1, 0)), (("w1", 1), 0, ("h1", 1, 1, 0)),
         (("q", 0), 1, ("q", 3)), (("q", 1), 2, ("q", 7)),
         (("v", 0), 3, ("v", 0, 2)), (("v", 1), 0, ("v", 1, 2)),
         (("u", 0), 1, ("u", 3)), (("u", 1), 2, ("u", 7)),
         (("gm", 0), 4, ("gm", 3)), (("gm", 1), 5, ("gm", 7)), (("gm", 2), 3, ("gm", 11)), (("gm", 3), 0, ("gm", 15)),
         (("br", 0, 0), 1, ("br", 0, 3)), (("br", 0, 1), 2, ("br", 0, 7)),
         (("br", 1, 0), 4, ("br", 1, 3)), (("br", 1, 1), 5, ("br", 1, 7)),
         (("xo", 0), 3, ("xo", 0, 2)), (("xo", 1), 0, ("xo", 1, 2)),
         ("pp", 1, ("pp", 1, 2))]
    return e


def build(nc, x_prompt, x_sample, cache_kv, state_win_kv, page_table, p_prompt, p_sample, rel_bias,
          norm_mix, w_in, v_norm, w_spatial, b_spatial, pe_cmp, w_phi1, w_phi2, w_branch, w_out,
          norm_ffn, w_router_group, b_router_group, w_router_expert, b_router_expert,
          w_exp_gate, w_exp_up, w_exp_down, norm_ple, w_ple_gate, w_ple_proj, final_norm,
          consts, hot, other,
          y_prompt, y_sample, kv_rows_prompt, kv_rows_sample, win_prompt, win_sample, chunk_v_sample):
    plan = psum_plan()
    ring_entries = ring_plan()
    n_pages = cache_kv.shape[1]

    def at(ap, offset, pattern):
        return bass.AP(tensor=ap.tensor, offset=offset, ap=pattern)

    with ExitStack() as ctx:
        def sb(name, shape, dt=F32):
            return ctx.enter_context(nc.sbuf_tensor(name, shape, dt))

        def sem(name):
            return ctx.enter_context(nc.semaphore(name))

        def scratch(name, shape, dt=F32):
            return nc.dram_tensor(name, shape, dt, kind="Internal").ap()

        ps = ctx.enter_context(nc.psum_tensor("ps", [128, 8, 512], F32))
        ring = sb("ring", [128, 4, 4096])
        late = sb("late", [128, 2, 4096])
        hT = sb("hT", [128, KT, N])
        reg_x = sb("reg_x", [128, 9472])
        reg_k = sb("reg_k", [128, 4608])
        x = sb("x", [128, 3, D])
        cst = sb("cst", [128, K_ALL])
        rows56 = sb("rows56", [56, 128])
        cols = sb("cols", [128, 56])
        stat = sb("stat", [128, 5, 4, 3])
        gates = sb("gates", [128, 3, 48])
        gsamp = sb("gsamp", [128, NB, 3])
        wgn = sb("wgn", [128, KT, 48])
        wr = sb("wr", [128, KT, 36])
        biasr = sb("biasr", [128, 36])
        w2 = sb("w2", [128, 2, 2, DH])
        b1 = sb("b1", [128, 4])
        kcT = sb("kcT", [128, 2, NSEQ, NC])
        vcs = sb("vcs", [128, 8, DH])
        vcp = sb("vcp", [128, G, DH])
        reg_kt = sb("reg_kt", [128, 1024])
        obT = sb("obT", [128, KT, N])
        reg_pc = sb("reg_pc", [128, 1024])
        bs = sb("bs", [128, PAST + NQ])
        bsn = sb("bsn", [128, NB, 64])
        small = sb("small", [128, 96])
        page_sb = sb("page_sb", [1, 16], I32)

        slots = [ring[:, s, :] for s in range(4)] + [late[:, s, :] for s in range(2)]
        xt = reg_x[:, 0:2 * XROWS * 128].rearrange("p (k r t) -> p k r t", k=2, r=XROWS)
        qT = reg_x[:, 0:2560].rearrange("p (m n) -> p m n", m=KT)
        qs = reg_x[:, 2560:3584].rearrange("p (b g n) -> p b g n", b=NB, g=G)
        tz = reg_x[:, 3584:7680].rearrange("p (h e) -> p h e", h=H)
        s_ring = [reg_x[:, 7680 + 640 * i:7680 + 640 * (i + 1)] for i in range(2)]
        pcsm = reg_x[:, 8960:9216].rearrange("p (b c) -> p b c", b=NB)
        scm = reg_x[:, 9216:9456].rearrange("p (h c) -> p h c", h=H)
        gmT = reg_x[:, 0:5120].rearrange("p (m n) -> p m n", m=2 * KT)
        v = reg_x[:, 5120:8192].rearrange("p (t n) -> p t n", t=3)
        mergedT = reg_x[:, 5120:7680].rearrange("p (m n) -> p m n", m=KT)
        xn2 = reg_x[:, 0:3072].rearrange("p (t n) -> p t n", t=3)
        xe = [reg_x[:, 5120 + 512 * i:5632 + 512 * i].rearrange("p (k n) -> p k n", k=KT) for i in range(2)]
        he = [reg_x[:, 6144 + 256 * i:6400 + 256 * i].rearrange("p (m n) -> p m n", m=4) for i in range(2)]
        sg = reg_x[64:128, 6656:7168]
        ye = [reg_x[:, 7168 + 512 * i:7680 + 512 * i] for i in range(2)]
        sel = [reg_x[:, 8960 + 192 * i:9152 + 192 * i].rearrange("p (t n) -> p t n", t=3) for i in range(2)]
        xn = reg_k[:, 0:3072].rearrange("p (t n) -> p t n", t=3)
        kvc = reg_k[:, 0:1024].rearrange("p (s g l d) -> p s g l d", s=2, g=G, l=2)
        kvp = reg_k[:, 1024:3072].rearrange("p (l s n) -> p l s n", l=2, s=2)
        kvs = reg_k[:, 3072:4608]
        pc = reg_k[:, 0:1024].rearrange("p (q h c) -> p q h c", q=2, h=H)
        uT = reg_k[:, 0:2560].rearrange("p (m n) -> p m n", m=KT)
        bmix = reg_k[:, 2560:3840].rearrange("p (g n) -> p g n", g=4)
        wsT = reg_k[:, 3840:4352].rearrange("p (g n) -> p g n", g=4)
        wssT = reg_k[:, 4352:4608].rearrange("p (g n) -> p g n", g=4)
        pp = reg_k[:, 0:3072].rearrange("p (t n) -> p t n", t=3)
        early = late[:, :, :].rearrange("p s n -> p (s n)")
        cst_in = [early[:, 1024 * i:1024 * i + 1024].rearrange("p (a l d) -> p a l d", a=8, l=2) for i in range(2)]
        h1k = early[:, 2048:3128].rearrange("p (h r c) -> p h r c", h=2, r=36)
        h1v = early[:, 3200:6272].rearrange("p (h r c) -> p h r c", h=2, r=48)
        hot_sb = early[0:BUCKETS + 1, 7168:7168 + TABN]
        rel_sb = early[0:BUCKETS + 1, 7600:7600 + H]
        tab_sb = early[0:H, 7680:7680 + TABN]
        slc_in = [early[:, 1024 * i:1024 * i + 1024].rearrange("p (l n) -> p l n", l=2) for i in range(2)]
        win_in = [early[:, 2048 + 1024 * i:3072 + 1024 * i].rearrange("p (l n) -> p l n", l=2) for i in range(2)]
        ktb = [early[:, 4096 + 1024 * i:5120 + 1024 * i].rearrange("p (g s l t) -> p g s l t", g=2, s=2, l=2) for i in range(2)]
        pcts = early[:, 7680:7936].rearrange("p (a n) -> p a n", a=2)
        ktn = early[:, 7936:8192].rearrange("p (g s t) -> p g s t", g=2, s=2)
        pts = [early[:, 6144 + 768 * i:6912 + 768 * i] for i in range(2)]
        ktp = reg_kt[:, :].rearrange("p (g s l t) -> p g s l t", g=2, s=2, l=2)
        gain_v = reg_kt[:, :]
        pct = reg_pc[:, :].rearrange("p (q g n) -> p q g n", q=2, g=G)
        ws_in = reg_pc[:, 0:512].rearrange("p (g n) -> p g n", g=4)
        p_in = reg_pc[:, 0:768].rearrange("p (t n) -> p t n", t=3)
        pT = obT[:, 0:2, :]
        gath = [[slots[3 + k][:, 1024 * t:1024 * t + 1024] for t in range(3)] for k in range(2)]
        gain_f = slots[5][:, 0:1024]
        ysb = slots[5][:, 1024:4096].rearrange("p (t n) -> p t n", t=3)
        pgate = reg_x[:, 3072:6144].rearrange("p (t n) -> p t n", t=3)
        mix_tmp = reg_x[:, 8192:8192 + N]
        route = reg_kt

        ident = cst[:, K_ID:K_ID + 128]
        upper = cst[:, K_UP:K_UP + 128]
        iota = cst[:, K_IOTA:K_IOTA + N]

        tab = scratch("tab", (H, 128, TABN))
        gate_rows = scratch("gate_rows", (H, NS, 3))
        y_rows = scratch("y_rows", (NE * SLOTS, D))
        y_more = scratch("y_more", (NE * MORE, D))

        bank_full = [sem(f"bank_full{i}") for i in range(8)]
        bank_read = [sem(f"bank_read{i}") for i in range(8)]
        chunk_in = [sem(f"chunk_in{i}") for i in range(6)]
        x_in, cst_sem, rows_in, hot_in, rel_in = sem("x_in"), sem("cst_in"), sem("rows_in"), sem("hot_in"), sem("rel_in")
        rel_row, small_w = sem("rel_row"), sem("small_w")
        br_in, w2_in, pg_in = sem("br_in"), sem("w2_in"), sem("pg_in")
        hist_in = [sem(f"hist_in{i}") for i in range(2)]
        stage_in = [sem(f"stage_in{i}") for i in range(2)]
        tab_out, bias_in, mask_in, gate_out, gate_in = sem("tab_out"), sem("bias_in"), sem("mask_in"), sem("gate_out"), sem("gate_in")
        kv_out, out_done = sem("kv_out"), sem("out_done")
        stat_init, sq_done, var_ready, rms_ready, rstd_ready = sem("stat_init"), sem("sq_done"), sem("var_ready"), sem("rms_ready"), sem("rstd_ready")
        xn_dve, xn_act, normed = sem("xn_dve"), sem("xn_act"), sem("normed")
        pe_row, h1_pad, b1_ready = sem("pe_row"), sem("h1_pad"), sem("b1_ready")
        qs_zero, csub, cexp, pc_ready = sem("qs_zero"), sem("csub"), sem("cexp"), sem("pc_ready")
        pv_done, v_out = sem("pv_done"), sem("v_out")
        neg_max, exp_done, p_ready, bsn_ready = sem("neg_max"), sem("exp_done"), sem("p_ready"), sem("bsn_ready")
        gain_v_in, ws_in_s, bmix_in, bmix_ready, v_ready = sem("gain_v_in"), sem("ws_in"), sem("bmix_in"), sem("bmix_ready"), sem("v_ready")
        p_in_s, xn2_pad = sem("p_in"), sem("xn2_pad")
        gexp_in, gexp, dexp_in, dexp, assigned, ranked = sem("gexp_in"), sem("gexp"), sem("dexp_in"), sem("dexp"), sem("assigned"), sem("ranked")
        sel_ready, gathered, xe_ready, up_done, silu_done, sg_ready, turned, he_ready, down_done, ye_ready, ye_out = (
            sem("sel_ready"), sem("gathered"), sem("xe_ready"), sem("up_done"), sem("silu_done"), sem("sg_ready"),
            sem("turned"), sem("he_ready"),
            sem("down_done"), sem("ye_ready"),
            [sem(f"ye_out{i}") for i in range(2)])
        ov = {n: sem("more_" + n) for n in ("chunk0", "chunk1", "chunk2", "sel", "gathered", "xe", "up", "silu", "sg", "turned", "he",
                                            "down", "ye", "stored", "out", "rows", "added")}
        rows_back = [sem(f"rows_back{i}") for i in range(6)]
        gain_f_in, x2_done, pg_sig, y_done = sem("gain_f_in"), sem("x2_done"), sem("pg_sig"), sem("y_done")
        act_chain, dve_chain, pool_chain = sem("act_chain"), sem("dve_chain"), sem("pool_chain")

        block = ctx.enter_context(nc.Block())

        def filled(eng, job):
            bank, full, _, _ = plan[job]
            eng.wait_ge(bank_full[bank], full)
            return ps[:, bank, :]

        def release(ins, job):
            ins.then_inc(bank_read[plan[job][0]], 1)

        def evacuated(eng, job):
            bank, _, _, read = plan[job]
            eng.wait_ge(bank_read[bank], read)

        def chunk_count(chunk):
            seen = [0] * 6
            for name, slot, _ in ring_entries:
                seen[slot] += 16
                if name == chunk:
                    return slot, seen[slot]
            raise KeyError(chunk)

        def chunk(eng, name):
            slot, count = chunk_count(name)
            eng.wait_ge(chunk_in[slot], count)
            return slots[slot]

        uses = [sum(slot == s for _, slot, _ in ring_entries) for s in range(6)]
        last_use = {slot: job for _, slot, job in ring_entries}

        @block.sync
        def _(sp):
            sp.dma_start(x[:, 0:2, :], x_prompt.rearrange("a (t p) n -> p (a t) n", p=128)).then_inc(x_in, 16)
            sp.dma_start(x[0:NS, 2, :], x_sample.rearrange("a b n -> (a b) n")).then_inc(x_in, 16)
            win = w_in.rearrange("a (k p) n -> p (a k) n", p=128)
            sources = {}
            for c in range(3):
                sources[("kv", c)] = win[:, :, CKV + 512 * c:CKV + 512 * c + 512]
            for c in range(2):
                sources[("q", c)] = win[:, :, CQ + 512 * c:CQ + 512 * c + 512]
                sources[("v", c)] = win[:, :, CV_ + 512 * c:CV_ + 512 * c + 512]
                sources[("u", c)] = win[:, :, CU + 512 * c:CU + 512 * c + 512]
                sources[("w1", c)] = w_phi1[0, c].rearrange("(j p) n -> p j n", p=128)
                sources[("xo", c)] = w_out[0].rearrange("(k p) n -> p k n", p=128)[:, :, 512 * c:512 * c + 512]
                for j in range(2):
                    sources[("br", j, c)] = w_branch[0, j].rearrange("(k p) n -> p k n", p=128)[:, :, 512 * c:512 * c + 512]
            for c in range(4):
                sources[("gm", c)] = win[:, :, CGM + 512 * c:CGM + 512 * c + 512]
            sources["pp"] = w_ple_proj[0].rearrange("(k p) n -> p k n", p=128)
            before = {}
            for name, slot, job in ring_entries:
                if slot in before:
                    filled(sp, before[slot])
                elif slot >= 4:
                    filled(sp, ("os", NB - 1))
                before[slot] = job
                src = sources[name]
                k, n = src.shape[1], src.shape[2]
                sp.dma_start(slots[slot][:, 0:k * n].rearrange("p (k n) -> p k n", k=k), src).then_inc(chunk_in[slot], 16)

            exp_src = (w_exp_gate, w_exp_up, w_exp_down)

            def load_expert(e, par, first):
                for j in range(3):
                    slot = 3 * par + j
                    if first:
                        filled(sp, last_use[slot])
                    elif j == 0:
                        sp.wait_ge(up_done, e - 1)
                    elif j == 2:
                        sp.wait_ge(down_done, e - 1)
                    k = (8, 8, 4)[j]
                    src = exp_src[j][0, bass.ds(e, 1)].rearrange("a (k p) n -> p (a k) n", p=128)
                    sp.dma_start(slots[slot].rearrange("p (k n) -> p k n", k=k), src).then_inc(chunk_in[slot], 16)

            load_expert(0, 0, True)
            load_expert(1, 1, True)
            with sp.Fori(1, NE // 2) as i:
                for par in range(2):
                    load_expert(i * 2 + par, par, False)
            sp.wait_ge(ranked, 1)
            most = sp.value_load(route[:, :].bitcast(I32)[0:1, 1019:1020], min_val=0, max_val=N)
            with sp.If(most > SLOTS):
                sp.wait_ge(down_done, NE)
                with sp.Fori(0, NE) as e:
                    sp.wait_ge(ov["down"], e * EXTRA + 1)
                    for j in range(3):
                        k = (8, 8, 4)[j]
                        src = exp_src[j][0, bass.ds(e, 1)].rearrange("a (k p) n -> p (a k) n", p=128)
                        sp.dma_start(slots[j].rearrange("p (k n) -> p k n", k=k), src).then_inc(ov[f"chunk{j}"], 16)
                sp.wait_ge(ov["down"], NE * EXTRA + 1)
            sp.wait_ge(down_done, NE)
            for c in range(2):
                src = w_ple_gate[0].rearrange("(k p) n -> p k n", p=128)[:, :, 512 * c:512 * c + 512]
                sp.dma_start(slots[c].rearrange("p (k n) -> p k n", k=8), src).then_inc(pg_in, 16)

        @block.tensor
        def _(pe):
            def begin(job):
                bank, _, read, _ = plan[job]
                if read:
                    pe.wait_ge(bank_read[bank], read)
                return ps[:, bank, :]

            def finish(ins, job):
                ins.then_inc(bank_full[plan[job][0]], 1)

            def transposed(names, src):
                for k in range(KT):
                    out = begin((names, k))
                    for t, (t0, rows) in enumerate(TILES):
                        last = pe.transpose(out[:, t0:t0 + rows], src[0:rows, t, 128 * k:128 * k + 128],
                                            ident[0:rows, 0:rows])
                    finish(last, (names, k))

            def by_channel(job, w, m, moving, n_k=KT):
                out = begin(job)
                for k in range(n_k):
                    last = pe.matmul(out[:, 0:N], w[:, k, 128 * m:128 * m + 128], moving[:, k, :],
                                     start=(k == 0), stop=(k == n_k - 1))
                finish(last, job)

            def by_token(job, stationary, w, t, n_k=KT, cols_=slice(0, 512)):
                t0, rows = TILES[t]
                out = begin(job)
                for k in range(n_k):
                    last = pe.matmul(out[0:rows, 0:512], stationary[:, k, t0:t0 + rows], w[:, k, cols_],
                                     start=(k == 0), stop=(k == n_k - 1))
                finish(last, job)

            def chunk_k(name, k=8):
                return chunk(pe, name)[:, 0:4096].rearrange("p (k n) -> p k n", k=k)

            pe.wait_ge(cst_sem, 16)
            pe.wait_ge(rows_in, 64)
            out = begin("cols")
            finish(pe.transpose(out[:, 0:56], rows56[:, :], ident[0:56, 0:56]), "cols")
            pe.wait_ge(hot_in, 16)
            pe.wait_ge(rel_in, 16)
            pe.wait_ge(rel_row, 1)
            out = begin("tab")
            finish(pe.matmul(out[0:H, 0:TABN], rel_sb, hot_sb, start=True, stop=True), "tab")
            pe.wait_ge(xn_dve, 2)
            pe.wait_ge(xn_act, 1)
            transposed("hT", xn)
            for k in range(KT):
                evacuated(pe, ("hT", k))
            for c in range(3):
                w = chunk_k(("kv", c))
                for s in range(3):
                    out = begin(("kv", c, s))
                    rows = (128, 128, 64)[s]
                    for k in range(KT):
                        lhs = hT[:, k, s:NP:2] if s < 2 else hT[:, k, NP:N]
                        last = pe.matmul(out[0:rows, :], lhs, w[:, k, :], start=(k == 0), stop=(k == KT - 1))
                    finish(last, ("kv", c, s))
            pe.wait_ge(small_w, 16)
            out = begin("gates")
            for t, (t0, rows) in enumerate(TILES):
                for k in range(KT):
                    last = pe.matmul(out[0:rows, 48 * t:48 * t + 48], hT[:, k, t0:t0 + rows], wgn[:, k, :],
                                     start=(k == 0), stop=(k == KT - 1))
            finish(last, "gates")
            for c in (1, 2):
                for s in range(3):
                    evacuated(pe, ("kv", c, s))
            for gp in range(2):
                out = begin(("ktp", gp))
                for s in range(2):
                    for l in range(2):
                        last = pe.transpose(out[:, (2 * s + l) * 128:(2 * s + l) * 128 + 128],
                                            kvp[:, l, s, 128 * gp:128 * gp + 128], ident)
                finish(last, ("ktp", gp))
            out = begin("ktn")
            for gp in range(2):
                for s in range(2):
                    last = pe.transpose(out[:, (2 * gp + s) * 64:(2 * gp + s) * 64 + 64],
                                        kvs[0:64, 512 + 512 * s + 128 * gp:512 + 512 * s + 128 * gp + 128],
                                        ident[0:64, 0:64])
            finish(last, "ktn")
            for s in range(NSEQ):
                if s == 0:
                    evacuated(pe, ("kv", 0, 0))
                    evacuated(pe, ("kv", 0, 1))
                else:
                    pe.wait_ge(hist_in[(s - 1) % 2], 64 * ((s - 1) // 2 + 1))
                for kv in range(2):
                    out = begin(("xt", s, kv))
                    for g in range(G):
                        src = kvc[:, kv, g, :, :].rearrange("p l d -> p (l d)") if s == 0 else \
                            cst_in[(s - 1) % 2][:, 4 * kv + g, :, :].rearrange("p l d -> p (l d)")
                        last = pe.transpose(out[:, 128 * g:128 * g + 128], src, ident)
                    finish(last, ("xt", s, kv))
            pe.wait_ge(pe_row, 2)
            for s in range(NSEQ):
                for kv in range(2):
                    evacuated(pe, ("xt", s, kv))
            for kv in range(2):
                w = chunk_k(("w1", kv), 16)
                for hid in range(2):
                    for half in (1, 0):
                        r0, nr = (18, 19) if half else (0, 18)
                        out = begin(("h1", kv, hid, half))
                        for j in range(16):
                            last = pe.matmul(out[:, 0:nr * NC], w[:, j, 128 * hid:128 * hid + 128],
                                             xt[:, kv, r0:r0 + nr, j:j + 8 * NC - 7:8],
                                             start=(j == 0), stop=(j == 15))
                        finish(last, ("h1", kv, hid, half))
            pe.wait_ge(w2_in, 16)
            for hid in range(2):
                for half in range(2):
                    evacuated(pe, ("h1", 0, hid, half))
                    evacuated(pe, ("h1", 1, hid, half))
            for half in range(2):
                out = begin(("kc", half))
                for hid in range(2):
                    last = pe.matmul(out[0:DH, 0:18 * NC], w2[:, 0, hid, :],
                                     h1k[:, hid, 18 * half:18 * half + 18, :].rearrange("p r c -> p (r c)"),
                                     start=(hid == 0), stop=(hid == 1))
                finish(last, ("kc", half))
            for job, first, n in (("vcs", 0, 8), ("vcp", 8, 4)):
                out = begin(job)
                for blk in range(n):
                    r = 4 * (first + blk)
                    for hid in range(2):
                        last = pe.matmul(out[:, DH * blk:DH * blk + DH],
                                         h1v[:, hid, r:r + 4, :].rearrange("p r c -> p (r c)"), w2[:, 1, hid, :],
                                         start=(hid == 0), stop=(hid == 1))
                finish(last, job)
            for c in range(2):
                w = chunk_k(("q", c))
                for m in range(4):
                    by_channel(("q", 4 * c + m), w, m, hT)
            for m in range(KT):
                evacuated(pe, ("q", m))
            for half in range(2):
                evacuated(pe, ("kc", half))
            for qt in range(2):
                n = 7 if qt == 0 else NC
                for par in range(2):
                    out = begin(("sc", qt, par))
                    for j in range(8):
                        last = pe.matmul(out[:, 16 * j:16 * j + n], qT[64 * par:64 * par + 64, j, 128 * qt:128 * qt + 128],
                                         kcT[64 * par:64 * par + 64, j // 4, 0, 0:n], start=True, stop=True)
                    finish(last, ("sc", qt, par))
            out = begin("scs")
            for b in range(NB):
                for g in range(G):
                    last = pe.matmul(out[32 * g:32 * g + 32, 16 * b:16 * b + NC], qs[:, b, g, :],
                                     kcT[:, g // 2, 1 + b, :], start=True, stop=True)
            finish(last, "scs")
            for qt in range(2):
                pe.wait_ge(pc_ready, qt + 1)
                out = begin(("pct", qt))
                for g in range(G):
                    last = pe.transpose(out[:, 128 * g:128 * g + 128],
                                        pc[:, qt, 4 * g:4 * g + 4, :].rearrange("p h c -> p (h c)"), ident)
                finish(last, ("pct", qt))
            pe.wait_ge(pc_ready, 3)
            out = begin("pcts")
            for j in range(2):
                last = pe.transpose(out[:, 128 * j:128 * j + 128],
                                    pcsm[:, 4 * j:4 * j + 4, :].rearrange("p b c -> p (b c)"), ident)
            finish(last, "pcts")

            def step(i):
                hp, qt, par = i // 4, (i // 2) % 2, i % 2
                h = 2 * hp + par
                return h, h // HPG, h % HPG, qt, 64 * (qt + 1)

            evacuated(pe, ("ktp", 0))
            evacuated(pe, ("ktp", 1))
            evacuated(pe, "vcp")
            evacuated(pe, ("pct", 0))
            evacuated(pe, ("pct", 1))
            for i in range(34):
                if i < 32:
                    h, g, hh, qt, w_ = step(i)
                    base = 64 * (g % 2)
                    out = begin(("s", i))
                    rhs = ktp[base:base + 64, g // 2, :, :, 0:w_].rearrange("p s l t -> p (s l) t")
                    finish(pe.matmul(out[:, 0:4 * w_], qT[base:base + 64, 4 * (g // 2) + hh, 128 * qt:128 * qt + 128],
                                     rhs, start=True, stop=True), ("s", i))
                if 1 <= i <= 32:
                    h, g, hh, qt, w_ = step(i - 1)
                    pe.wait_ge(p_ready, i)
                    out = begin(("pt", i - 1))
                    for j in range(4):
                        last = pe.transpose(out[0:w_, 128 * j:128 * j + 128],
                                            s_ring[(i - 1) % 2][:, w_ * j:w_ * j + w_], ident)
                    finish(last, ("pt", i - 1))
                if i >= 2:
                    h, g, hh, qt, w_ = step(i - 2)
                    par = (i - 2) % 2
                    evacuated(pe, ("pt", i - 2))
                    if par == 0:
                        out_o = begin(("o", (i - 2) // 2))
                    dst = out_o[64 * par:64 * par + 64, 0:128]
                    for j in range(4):
                        s, l = j // 2, j % 2
                        pe.matmul(dst, kvp[0:w_, l, s, 256 + DH * g:256 + DH * g + DH],
                                  pts[i % 2][0:w_, 128 * j:128 * j + 128], start=(j == 0), stop=False)
                    last = pe.matmul(dst, vcp[32 * hh:32 * hh + 32, g, :], pct[32 * hh:32 * hh + 32, qt, g, :],
                                     start=False, stop=True)
                    if par == 1:
                        finish(last, ("o", (i - 2) // 2))
                    else:
                        last.then_inc(pv_done, 1)

            evacuated(pe, "ktn")
            evacuated(pe, "vcs")
            evacuated(pe, "pcts")
            for b in range(NB + 1):
                if b < NB:
                    pe.wait_ge(stage_in[b % 2], 48 * (b // 2 + 1))
                    for gp in range(2):
                        out = begin(("ktb", b, gp))
                        for s, stage in enumerate((slc_in, win_in)):
                            for l in range(2):
                                last = pe.transpose(out[:, (2 * s + l) * 128:(2 * s + l) * 128 + 128],
                                                    stage[b % 2][:, l, 128 * gp:128 * gp + 128], ident)
                        finish(last, ("ktb", b, gp))
                if b >= 1:
                    pe.wait_ge(p_ready, 32 + b)
                    src = s_ring[(b - 1) % 2]
                    for s in range(2):
                        out = begin(("pts", b - 1, s))
                        for l in range(2):
                            pe.transpose(out[:, 128 * l:128 * l + 128], src[:, 320 * s + 128 * l:320 * s + 128 * l + 128], ident)
                        finish(pe.transpose(out[0:64, 256:384], src[:, 320 * s + 256:320 * s + 320], ident), ("pts", b - 1, s))
                if b < NB:
                    evacuated(pe, ("ktb", b, 0))
                    evacuated(pe, ("ktb", b, 1))
                    out = begin(("ss", b))
                    for g in range(G):
                        last = pe.matmul(out[32 * g:32 * g + 32, 0:512], qs[:, b, g, :],
                                         ktb[b % 2][:, g // 2, :, :, :].rearrange("p s l t -> p (s l t)"),
                                         start=True, stop=True)
                    finish(last, ("ss", b))
                    out = begin(("sn", b))
                    for g in range(G):
                        last = pe.matmul(out[32 * g:32 * g + 32, 0:128], qs[:, b, g, :],
                                         ktn[:, g // 2, :, :].rearrange("p s t -> p (s t)"), start=True, stop=True)
                    finish(last, ("sn", b))
                if b >= 1:
                    c = b - 1
                    evacuated(pe, ("pts", c, 0))
                    evacuated(pe, ("pts", c, 1))
                    out = begin(("os", c))
                    for g in range(G):
                        dst = out[0:64, 32 * g:32 * g + 32]
                        for s, stage in enumerate((slc_in, win_in)):
                            for l in range(2):
                                pe.matmul(dst, stage[c % 2][:, l, 256 + DH * g:256 + DH * g + DH],
                                          pts[c % 2][:, 384 * s + 128 * l + 32 * g:384 * s + 128 * l + 32 * g + 32],
                                          start=(s == 0 and l == 0), stop=False)
                        for s in range(2):
                            pe.matmul(dst, kvs[0:64, 768 + 512 * s + DH * g:768 + 512 * s + DH * g + DH],
                                      pts[c % 2][0:64, 384 * s + 256 + 32 * g:384 * s + 256 + 32 * g + 32],
                                      start=False, stop=False)
                        r = 32 * (c % 4)
                        last = pe.matmul(dst, vcs[r:r + 32, 2 * g + c // 4, :], pcts[r:r + 32, c // 4, 32 * g:32 * g + 32],
                                         start=False, stop=True)
                    finish(last, ("os", c))

            for c in range(2):
                w = chunk_k(("v", c))
                for t in range(3):
                    by_token(("v", c, t), hT, w, t)
            pe.wait_ge(ws_in_s, 16)
            out = begin("ws")
            for g in range(4):
                last = pe.transpose(out[:, 128 * g:128 * g + 128], ws_in[:, g, :], ident)
            finish(last, "ws")
            evacuated(pe, "ws")
            out = begin("wss")
            finish(pe.matmul(out[0:64, 0:256], cst[0:NQ, K_REP:K_REP + 64],
                             wsT[0:NQ, :, 0:NQ].unsqueeze(2).broadcast_to([NQ, 4, NB, NQ]), start=True, stop=True), "wss")
            for c in range(2):
                w = chunk_k(("u", c))
                for m in range(4):
                    by_channel(("u", 4 * c + m), w, m, hT)
            for c in range(4):
                w = chunk_k(("gm", c))
                for m in range(4):
                    by_channel(("gm", 4 * c + m), w, m, hT)
            evacuated(pe, "wss")
            pe.wait_ge(v_ready, 3)
            for m in range(KT):
                out = begin(("mx", m))
                g = m // 2
                for t, (t0, rows) in enumerate(TILES):
                    rhs = wsT[:, g, :] if t < 2 else wssT[0:64, g, :]
                    last = pe.matmul(out[:, t0:t0 + rows], v[0:rows, t, 128 * m:128 * m + 128], rhs, start=True, stop=True)
                finish(last, ("mx", m))
            for m in range(KT):
                evacuated(pe, ("mx", m))
            for b in range(NB):
                evacuated(pe, ("os", b))
            for j in range(2):
                for c in range(2):
                    w = chunk_k(("br", j, c))
                    for m in range(4):
                        by_channel(("br", j, 4 * c + m), w, m, uT if j == 0 else obT)
            pe.wait_ge(normed, KT)
            for c in range(2):
                w = chunk_k(("xo", c))
                for t in range(3):
                    by_token(("xo", c, t), mergedT, w, t)
            pe.wait_ge(xn_dve, 4)
            pe.wait_ge(xn_act, 2)
            transposed("hT2", xn2)
            for k in range(KT):
                evacuated(pe, ("hT2", k))
            pe.wait_ge(br_in, 64)
            out = begin("router")
            for t, (t0, rows) in enumerate(TILES):
                for k in range(KT):
                    last = pe.matmul(out[0:rows, 36 * t:36 * t + 36], hT[:, k, t0:t0 + rows], wr[:, k, :],
                                     start=(k == 0), stop=(k == KT - 1))
            finish(last, "router")
            pe.wait_ge(p_in_s, 32)
            for k in range(2):
                out = begin(("ppT", k))
                for t, (t0, rows) in enumerate(TILES):
                    last = pe.transpose(out[:, t0:t0 + rows], p_in[0:rows, t, 128 * k:128 * k + 128], ident[0:rows, 0:rows])
                finish(last, ("ppT", k))
            evacuated(pe, ("ppT", 0))
            evacuated(pe, ("ppT", 1))
            w = chunk_k("pp", 4)
            for c in range(2):
                for t in range(3):
                    by_token(("pp", c, t), pT, w, t, 2, slice(512 * c, 512 * c + 512))
            pe.wait_ge(assigned, 1)
            out = begin("rank")
            ones = cst[:, K_UP + 127:K_UP + 128]
            a_all = route[:, 576:672].rearrange("p (t e) -> p t e", t=3)
            for t in range(4):
                for j in range(min(t, 2) + 1):
                    full_sum = j < t
                    lhs = ones.broadcast_to([128, 128]) if full_sum else upper
                    last = pe.matmul(out[:, 32 * t:32 * t + 32], lhs, a_all[:, j, :], start=(j == 0), stop=(j == min(t, 2)))
            finish(last, "rank")

            def gather(bufs, out, s_ready, count, s_done):
                pe.wait_ge(s_ready, count)
                for k in range(KT):
                    for t in range(3):
                        for half in range(2):
                            c0 = 128 * k + 64 * half
                            last = pe.matmul(out[64 * half:64 * half + 64, SLOTS * k:SLOTS * k + SLOTS], xn2[:, t, c0:c0 + 64],
                                             bufs[:, t, :], start=(t == 0), stop=(t == 2))
                last.then_inc(s_done, 1)

            def gate_up(w_gate, w_up, xb, out):
                ws_ = [w.rearrange("p (k n) -> p k n", k=8) for w in (w_gate, w_up)]
                for k in range(KT):
                    for part in range(2):
                        last = pe.matmul(out[64 * part:64 * part + 64, :], xb[:, k, :], ws_[part][:, k, :],
                                         start=(k == 0), stop=(k == KT - 1))
                return last

            def turn(out):
                for m in range(4):
                    last = pe.matmul(out[:, SLOTS * m:SLOTS * m + SLOTS], sg[:, 128 * m:128 * m + 128],
                                     ident[64:128, 64:128], start=True, stop=True)
                return last

            def down(w_down, hb, out):
                w = w_down.rearrange("p (k n) -> p k n", k=4)
                for m in range(4):
                    for c in range(2):
                        last = pe.matmul(out[64 * c:64 * c + 64, :], hb[:, m, :], w[:, m, 512 * c:512 * c + 512],
                                         start=(m == 0), stop=(m == 3))
                return last

            for bank in range(8):
                pe.wait_ge(bank_read[bank], plan["expert loop"][bank])
            pe.wait_ge(xn2_pad, 1)
            gather(sel[0], ps[:, 0, :], sel_ready, 1, gathered)

            def expert(i, par, last_one=False):
                e = i * 2 + par
                pe.wait_ge(xe_ready, e + 1)
                for slot in (3 * par, 3 * par + 1):
                    pe.wait_ge(chunk_in[slot], (i + uses[slot] + 1) * 16)
                gate_up(slots[3 * par], slots[3 * par + 1], xe[par], ps[:, 2 + par, :]).then_inc(up_done, 1)
                if not last_one:
                    gather(sel[1 - par], ps[:, 1 - par, :], sel_ready, e + 2, gathered)
                pe.wait_ge(sg_ready, e + 1)
                turn(ps[:, 6, :]).then_inc(turned, 1)
                pe.wait_ge(he_ready, e + 1)
                pe.wait_ge(ye_ready, e + 1)
                pe.wait_ge(chunk_in[3 * par + 2], (i + uses[3 * par + 2] + 1) * 16)
                down(slots[3 * par + 2], he[par], ps[:, 4 + par, :]).then_inc(down_done, 1)

            with pe.Fori(0, NE // 2 - 1) as i:
                expert(i, 0)
                expert(i, 1)
            expert(NE // 2 - 1, 0)
            expert(NE // 2 - 1, 1, True)
            pe.wait_ge(ranked, 1)
            most = pe.value_load(route[:, :].bitcast(I32)[0:1, 1019:1020], min_val=0, max_val=N)
            with pe.If(most > SLOTS):
                pe.sem_inc(ov["down"], 1)
                pe.wait_ge(ye_ready, NE + 2)
                with pe.Fori(0, NE) as e:
                    for blk in range(EXTRA):
                        n = e * EXTRA + blk + 1
                        gather(sel[0], ps[:, 0, :], ov["sel"], n, ov["gathered"])
                        if blk == 0:
                            pe.wait_ge(ov["chunk0"], (e + 1) * 16)
                            pe.wait_ge(ov["chunk1"], (e + 1) * 16)
                            pe.wait_ge(ov["chunk2"], (e + 1) * 16)
                        pe.wait_ge(ov["xe"], n)
                        gate_up(slots[0], slots[1], xe[0], ps[:, 2, :]).then_inc(ov["up"], 1)
                        pe.wait_ge(ov["sg"], n)
                        turn(ps[:, 6, :]).then_inc(ov["turned"], 1)
                        pe.wait_ge(ov["he"], n)
                        pe.wait_ge(ov["ye"], n)
                        down(slots[2], he[0], ps[:, 4, :]).then_inc(ov["down"], 1)
                pe.wait_ge(ov["ye"], NE * EXTRA + 1)
            pe.wait_ge(ye_ready, NE + 2)
            pe.wait_ge(xn_dve, 6)
            pe.wait_ge(xn_act, 3)
            transposed("hT3", xn2)
            for k in range(KT):
                evacuated(pe, ("hT3", k))
            pe.wait_ge(pg_in, 32)
            for c in range(2):
                for t in range(3):
                    by_token(("pg", c, t), hT, slots[c].rearrange("p (k n) -> p k n", k=8), t)

        @block.scalar
        def _(act):
            chain = [0]

            def link(ins):
                chain[0] += 1
                ins.then_inc(act_chain, 1)
                act.wait_ge(act_chain, chain[0])

            act.dma_start(cst[:, :], consts).then_inc(cst_sem, 16)
            for n, src in enumerate((norm_mix, norm_ffn, norm_ple)):
                act.dma_start(rows56[8 * n:8 * n + 8, :], src.rearrange("a (k p) -> (a k) p", p=128)).then_inc(rows_in, 16)
            act.dma_start(rows56[24:56, :], pe_cmp[0].rearrange("k (j l) d -> (k j) (l d)", l=2)).then_inc(rows_in, 16)
            act.dma_start(hot_sb, hot).then_inc(hot_in, 16)
            act.dma_start(rel_sb[0:BUCKETS, :], rel_bias).then_inc(rel_in, 16)
            act.dma_start(wgn[:, :, :], w_in[0].rearrange("(k p) n -> p k n", p=128)[:, :, CGN:CGN + 48]).then_inc(small_w, 16)
            act.dma_start(w2[:, :, :, :], w_phi2[0].rearrange("k (h p) d -> p k h d", p=128)).then_inc(w2_in, 16)
            act.dma_start(wr[:, :, 0:4], w_router_group[0].rearrange("(k p) n -> p k n", p=128)).then_inc(br_in, 16)
            act.dma_start(wr[:, :, 4:36], w_router_expert[0].rearrange("(k p) n -> p k n", p=128)).then_inc(br_in, 16)
            act.dma_start(biasr[:, 0:4], at(b_router_group, 0, [[0, 128], [1, 4]])).then_inc(br_in, 16)
            act.dma_start(biasr[:, 4:36], at(b_router_expert, 0, [[0, 128], [1, 32]])).then_inc(br_in, 16)

            def squares(n, src, junk):
                act.wait_ge(stat_init, 1)
                for t, (_, rows) in enumerate(TILES):
                    act.activation(junk[0:rows, t, :], src[0:rows, t, :], ACT.Square,
                                   accum_out=stat[0:rows, n, 0, t:t + 1]).then_inc(sq_done, 1)
                act.wait_ge(var_ready, n + 1)
                act.activation(stat[:, n, 2, :], stat[:, n, 1, :], ACT.Sqrt).then_inc(rms_ready, 1)

            def scaled(n, src, dst):
                act.wait_ge(rstd_ready, n + 1)
                act.activation(dst[:, 1, :], src[:, 1, :], ACT.Copy, scale=stat[:, n, 3, 1:2]).then_inc(xn_act, 1)

            act.wait_ge(x_in, 32)
            squares(0, x, xn)
            scaled(0, x, xn)
            evacuated(act, "cols")
            for k in range(1, KT, 2):
                src = filled(act, ("hT", k))
                release(act.activation(hT[:, k, :], src[:, 0:N], ACT.Copy, scale=cols[:, k:k + 1]), ("hT", k))
            src = filled(act, ("kv", 0, 1))
            release(act.activation(kvc[:, :, :, 1, :], src.rearrange("p (s g d) -> p s g d", s=2, g=G), ACT.Copy), ("kv", 0, 1))
            for c in (1, 2):
                src = filled(act, ("kv", c, 1))
                release(act.activation(kvp[:, 1, c - 1, :], src, ACT.Copy), ("kv", c, 1))
            src = filled(act, "gates")
            release(act.activation(gates[:, 0:2, :], src[:, 0:96].rearrange("p (t n) -> p t n", t=2), ACT.Sigmoid), "gates")
            release(act.activation(gates[0:64, 2, :], src[0:64, 96:144], ACT.Sigmoid), "gates")
            src = filled(act, ("ktp", 1))
            release(act.activation(ktp[:, 1].rearrange("p s l t -> p (s l t)"), src, ACT.Copy), ("ktp", 1))
            for s in range(NSEQ):
                src = filled(act, ("xt", s, 1))
                release(act.activation(xt[:, 1, s:s + 3 * NSEQ + 1:NSEQ, :], src.rearrange("p (g t) -> p g t", g=G), ACT.Copy), ("xt", s, 1))
            act.wait_ge(h1_pad, 1)
            for kv in range(2):
                for hid in range(2):
                    for half in (1, 0):
                        job = ("h1", kv, hid, half)
                        src = filled(act, job)[:, 0:18 * NC]
                        act.wait_ge(b1_ready, 2 * kv + hid + 1)
                        bias = b1[:, 2 * kv + hid:2 * kv + hid + 1]
                        if kv == 0:
                            release(act.activation(h1k[:, hid, 18 * half:18 * half + 18, :],
                                                   src.rearrange("p (r c) -> p r c", c=NC), ACT.Gelu_apprx_tanh, bias=bias), job)
                            continue
                        rows = src.rearrange("p (g s c) -> p g s c", g=2, s=NSEQ)
                        out = h1v[:, hid, 16 * half:16 * half + 16, 0:NC].rearrange("p (g s) c -> p g s c", g=2)
                        release(act.activation(out, rows[:, :, 1:NSEQ, :], ACT.Gelu_apprx_tanh, bias=bias), job)
                        out = h1v[:, hid, 32 + 8 * half:40 + 8 * half, 0:NC].rearrange("p (g r) c -> p g r c", g=2)
                        release(act.activation(out, rows[:, :, 0:1, :].broadcast_to([128, 2, 4, NC]),
                                               ACT.Gelu_apprx_tanh, bias=bias), job)
            act.wait_ge(qs_zero, 1)
            for m in range(KT):
                src = filled(act, ("q", m))
                g, hh = m // 2, 2 * (m % 2) + 1
                base = 64 * (g % 2)
                act.activation(qT[base:base + 64, 4 * (g // 2) + hh, :], src[64:128, 0:N], ACT.Copy, scale=0.125)
                release(act.activation(qs[base:base + 64, :, g, hh * NQ:hh * NQ + NQ],
                                       src[64:128, NP:N].rearrange("p (b t) -> p b t", b=NB), ACT.Copy, scale=0.125), ("q", m))
            for n in range(3):
                act.wait_ge(csub, n + 1)
                if n < 2:
                    c = 7 if n == 0 else NC
                    act.activation(scm[:, :, 0:c], scm[:, :, 0:c], ACT.Exp).then_inc(cexp, 1)
                else:
                    act.activation(scm[:, 0:NB, :], scm[:, 0:NB, :], ACT.Exp).then_inc(cexp, 1)
            for i in range(34):
                if i < 32:
                    w_ = 64 * ((i // 2) % 2 + 1)
                    act.wait_ge(neg_max, i + 1)
                    for s in range(2):
                        p_ = s_ring[i % 2][:, 2 * w_ * s:2 * w_ * s + 2 * w_]
                        last = act.activation(p_, p_, ACT.Exp, bias=small[:, 8 * (i % 2) + s:8 * (i % 2) + s + 1],
                                              accum_out=small[:, 8 * (i % 2) + 2 + s:8 * (i % 2) + 3 + s])
                    last.then_inc(exp_done, 1)
                if 1 <= i <= 32:
                    w_ = 64 * (((i - 1) // 2) % 2 + 1)
                    src = filled(act, ("pt", i - 1))
                    if i >= 3:
                        if (i - 3) % 2:
                            filled(act, ("o", (i - 3) // 2))
                        else:
                            act.wait_ge(pv_done, (i - 3) // 2 + 1)
                    release(act.activation(pts[(i - 1) % 2][0:w_, 0:512], src[0:w_, :], ACT.Copy), ("pt", i - 1))
            for b in range(NB + 1):
                if b < NB:
                    src = filled(act, ("ktb", b, 1))
                    if b >= 2:
                        filled(act, ("ss", b - 2))
                    release(act.activation(ktb[b % 2][:, 1].rearrange("p s l t -> p (s l t)"), src, ACT.Copy), ("ktb", b, 1))
                if b >= 1:
                    src = filled(act, ("pts", b - 1, 0))
                    if b >= 3:
                        filled(act, ("os", b - 3))
                    else:
                        filled(act, ("o", 15))
                    release(act.activation(pts[(b - 1) % 2][:, 0:256], src[:, 0:256], ACT.Copy), ("pts", b - 1, 0))
                    release(act.activation(pts[(b - 1) % 2][0:64, 256:384], src[0:64, 256:384], ACT.Copy), ("pts", b - 1, 0))
                if b < NB:
                    act.wait_ge(neg_max, 33 + b)
                    for s in range(2):
                        p_ = s_ring[b % 2][:, 320 * s:320 * s + 320]
                        last = act.activation(p_, p_, ACT.Exp, bias=small[:, 8 * (b % 2) + s:8 * (b % 2) + s + 1],
                                              accum_out=small[:, 8 * (b % 2) + 2 + s:8 * (b % 2) + 3 + s])
                    last.then_inc(exp_done, 1)
            for c in range(2):
                for t, (_, rows) in enumerate(TILES):
                    src = filled(act, ("v", c, t))
                    release(act.activation(v[0:rows, t, 512 * c:512 * c + 512], src[0:rows, :], ACT.Gelu_apprx_tanh), ("v", c, t))
            for m in range(KT):
                src = filled(act, ("u", m))
                release(act.activation(uT[:, m, :], src[:, 0:N], ACT.Gelu_apprx_tanh), ("u", m))
            for c in range(2):
                for t in range(3):
                    evacuated(act, ("v", c, t))
            squares(1, v, gmT[:, 0:10, :].rearrange("p a b -> p (a b)")[:, 0:3072].rearrange("p (t n) -> p t n", t=3))
            for m in range(2 * KT):
                src = filled(act, ("gm", m))
                release(act.activation(gmT[:, m, :], src[:, 0:N], ACT.Sigmoid), ("gm", m))
            for c in range(2):
                for t in range(3):
                    evacuated(act, ("xo", c, t))
            squares(2, x, xn2)
            scaled(2, x, xn2)
            for k in range(1, KT, 2):
                src = filled(act, ("hT2", k))
                release(act.activation(hT[:, k, :], src[:, 0:N], ACT.Copy, scale=cols[:, 8 + k:9 + k]), ("hT2", k))
            act.wait_ge(gexp_in, 1)
            lg = route[:, 864:876].rearrange("p (t g) -> p t g", t=3)
            act.activation(lg, lg, ACT.Exp).then_inc(gexp, 1)
            act.wait_ge(dexp_in, 1)
            dl = route[:, 880:883]
            act.activation(dl, dl, ACT.Exp).then_inc(dexp, 1)
            for c in range(2):
                for t in range(3):
                    src = filled(act, ("pp", c, t))
                    rows = TILES[t][1]
                    release(act.activation(pp[0:rows, t, 512 * c:512 * c + 512], src[0:rows, :], ACT.Copy), ("pp", c, t))

            def expert(i, par, first=False):
                e = i * 2 + par
                act.wait_ge(up_done, e + 1)
                act.activation(sg, ps[0:64, 2 + par, :], ACT.Silu).then_inc(silu_done, 1)
                act.wait_ge(down_done, e + 1)
                if not first:
                    act.wait_ge(ye_out[par], i * 16)
                act.activation(ye[par], ps[:, 4 + par, :], ACT.Copy).then_inc(ye_ready, 1)

            act.sem_inc(ye_ready, 2)
            expert(0, 0, True)
            expert(0, 1, True)
            with act.Fori(1, NE // 2) as i:
                expert(i, 0)
                expert(i, 1)
            act.wait_ge(ranked, 1)
            most = act.value_load(route[:, :].bitcast(I32)[0:1, 1019:1020], min_val=0, max_val=N)
            with act.If(most > SLOTS):
                for par in range(2):
                    act.wait_ge(ye_out[par], NE // 2 * 16)
                act.sem_inc(ov["ye"], 1)
                with act.Fori(0, NE) as e:
                    for blk in range(EXTRA):
                        n = e * EXTRA + blk + 1
                        act.wait_ge(ov["up"], n)
                        act.activation(sg, ps[0:64, 2, :], ACT.Silu).then_inc(ov["silu"], 1)
                        act.wait_ge(ov["down"], n + 1)
                        act.wait_ge(ov["out"], n)
                        act.activation(ye[0], ps[:, 4, :], ACT.Copy).then_inc(ov["ye"], 1)
                act.wait_ge(ov["ye"], NE * EXTRA + 1)
            act.wait_ge(x2_done, 3)
            squares(3, x, xn2)
            scaled(3, x, xn2)
            for k in range(1, KT, 2):
                src = filled(act, ("hT3", k))
                release(act.activation(hT[:, k, :], src[:, 0:N], ACT.Copy, scale=cols[:, 16 + k:17 + k]), ("hT3", k))
            for c in range(2):
                for t in range(3):
                    rows = TILES[t][1]
                    src = filled(act, ("pg", c, t))
                    act.activation(pgate[0:rows, t, 512 * c:512 * c + 512], src[0:rows, :], ACT.Sigmoid).then_inc(pg_sig, 1)
            act.wait_ge(y_done, 6)
            squares(4, x, ysb)

        @block.vector
        def _(dve):
            chain = [0]

            def link(ins):
                chain[0] += 1
                ins.then_inc(dve_chain, 1)
                dve.wait_ge(dve_chain, chain[0])

            def rstd(n):
                dve.wait_ge(sq_done, 3 * (n + 1))
                dve.tensor_scalar(stat[:, n, 1, :], stat[:, n, 0, :], 1.0 / D, EPS, ALU.mult, ALU.add).then_inc(var_ready, 1)
                dve.wait_ge(rms_ready, n + 1)
                dve.reciprocal(stat[:, n, 3, :], stat[:, n, 2, :]).then_inc(rstd_ready, 1)
                dve.wait_ge(rstd_ready, n + 1)

            def scaled(n, src, dst):
                for t in (0, 2):
                    rows = TILES[t][1]
                    dve.tensor_scalar(dst[0:rows, t, :], src[0:rows, t, :], stat[0:rows, n, 3, t:t + 1], None,
                                      ALU.mult).then_inc(xn_dve, 1)

            dve.memset(stat[:, :, 0, :], 1.0).then_inc(stat_init, 1)
            dve.memset(rel_sb[BUCKETS:BUCKETS + 1, :], NEG).then_inc(rel_row, 1)
            src = filled(dve, "cols")
            release(dve.tensor_copy(cols[:, :], src[:, 0:56]), "cols")
            src = filled(dve, "tab")
            release(dve.tensor_copy(tab_sb, src[0:H, 0:TABN]), "tab")
            rstd(0)
            scaled(0, x, xn)
            evacuated(dve, "cols")
            for k in range(0, KT, 2):
                src = filled(dve, ("hT", k))
                release(dve.tensor_scalar(hT[:, k, :], src[:, 0:N], cols[:, k:k + 1], None, ALU.mult), ("hT", k))
            link(dve.memset(xt[:, :, XROWS - 1, :], 0.0))
            for kv in range(2):
                dve.tensor_copy(xt[:, kv, XROWS - 1, 0:16], cols[:, 24 + 16 * kv:40 + 16 * kv]).then_inc(pe_row, 1)
            dve.memset(h1v[:, :, :, :].rearrange("p h r c -> p (h r c)"), 0.0).then_inc(h1_pad, 1)
            for c in range(3):
                src = filled(dve, ("kv", c, 0))
                if c == 0:
                    release(dve.tensor_copy(kvc[:, :, :, 0, :], src.rearrange("p (s g d) -> p s g d", s=2, g=G)), ("kv", 0, 0))
                else:
                    release(dve.tensor_copy(kvp[:, 0, c - 1, :], src), ("kv", c, 0))
                src = filled(dve, ("kv", c, 2))
                release(dve.tensor_copy(kvs[0:64, 512 * c:512 * c + 512], src[0:64, :]), ("kv", c, 2))
            src = filled(dve, ("ktp", 0))
            release(dve.tensor_copy(ktp[:, 0].rearrange("p s l t -> p (s l t)"), src), ("ktp", 0))
            src = filled(dve, "ktn")
            dve.wait_ge(tab_out, 16)
            release(dve.tensor_copy(ktn[:, :, :, :].rearrange("p g s t -> p (g s t)"), src[:, 0:256]), "ktn")
            for s in range(NSEQ):
                src = filled(dve, ("xt", s, 0))
                release(dve.tensor_copy(xt[:, 0, s:s + 3 * NSEQ + 1:NSEQ, :], src.rearrange("p (g t) -> p g t", g=G)), ("xt", s, 0))
            for kv in range(2):
                for hid in range(2):
                    job = ("h1", kv, hid, 1)
                    src = filled(dve, job)
                    dve.tensor_copy(b1[:, 2 * kv + hid:2 * kv + hid + 1], src[:, 18 * NC:18 * NC + 1]).then_inc(b1_ready, 1)
                    dve.wait_ge(b1_ready, 2 * kv + hid + 1)
                    dve.sem_inc(bank_read[plan[job][0]], 1)
            for half in range(2):
                src = filled(dve, ("kc", half))[0:64, 0:18 * NC].rearrange("p (g s c) -> p g s c", g=2, s=NSEQ)
                for par in range(2):
                    release(dve.tensor_copy(kcT[64 * par:64 * par + 64, half, :, :], src[:, par, :, :]), ("kc", half))
            src = filled(dve, "vcs")
            release(dve.tensor_copy(vcs[:, :, :].rearrange("p a d -> p (a d)"), src), "vcs")
            src = filled(dve, "vcp")
            release(dve.tensor_copy(vcp[:, :, :].rearrange("p a d -> p (a d)"), src[:, 0:256]), "vcp")
            dve.memset(qs.rearrange("p b g n -> p (b g n)"), 0.0).then_inc(qs_zero, 1)
            dve.wait_ge(qs_zero, 1)
            for m in range(KT):
                src = filled(dve, ("q", m))
                g, hh = m // 2, 2 * (m % 2)
                base = 64 * (g % 2)
                dve.tensor_scalar(qT[base:base + 64, 4 * (g // 2) + hh, :], src[0:64, 0:N], 0.125, None, ALU.mult)
                release(dve.tensor_scalar(qs[base:base + 64, :, g, hh * NQ:hh * NQ + NQ],
                                          src[0:64, NP:N].rearrange("p (b t) -> p b t", b=NB), 0.125, None, ALU.mult), ("q", m))
            dve.wait_ge(kv_out, 16 * 6)
            link(dve.memset(pc.rearrange("p q h c -> p (q h c)"), 0.0))
            dve.memset(pcsm.rearrange("p b c -> p (b c)"), 0.0)
            dve.wait_ge(bias_in, 32)
            for qt in range(2):
                n = 7 if qt == 0 else NC
                e0 = 31 + 128 - 128 * qt
                for par in range(2):
                    job = ("sc", qt, par)
                    src = filled(dve, job)[:, 0:128].rearrange("p (g h c) -> p g h c", g=2, h=4)[:, :, :, 0:n]
                    out = scm.rearrange("p (g r h) c -> p g r h c", g=2, r=2)[:, :, par, :, 0:n]
                    bias = tz.rearrange("p (g r h) e -> p g r h e", g=2, r=2)[:, :, par, :, e0:e0 + 16 * n - 15:16]
                    ins = dve.tensor_tensor(out, src, bias, ALU.add)
                    release(ins, job)
                    evacuated(dve, job)
                sc_ = scm[:, :, 0:n]
                link(dve.tensor_reduce(small[:, 16:32], sc_, AX.X, ALU.max))
                dve.tensor_tensor(sc_, sc_, small[:, 16:32].unsqueeze(2).broadcast_to([128, H, n]), ALU.subtract).then_inc(csub, 1)
                dve.wait_ge(cexp, qt + 1)
                link(dve.tensor_reduce(small[:, 32:48], sc_, AX.X, ALU.add))
                link(dve.reciprocal(small[:, 48:64], small[:, 32:48]))
                link(dve.tensor_tensor(small[:, 48:64], small[:, 48:64], gates[:, qt, 0:16], ALU.mult))
                if qt == 0:
                    link(dve.tensor_scalar(small[:, 48:64], small[:, 48:64], cst[:, K_VALID:K_VALID + 1], None, ALU.mult))
                dve.tensor_tensor(pc[:, qt, :, 0:n], sc_, small[:, 48:64].unsqueeze(2).broadcast_to([128, H, n]),
                                  ALU.mult).then_inc(pc_ready, 1)
                dve.wait_ge(pc_ready, qt + 1)
            src = filled(dve, "scs")[:, 0:128].rearrange("p (b c) -> p b c", b=NB)[:, :, 0:NC]
            bias = bs[:, 31:31 + 16 * NC - 15:16].unsqueeze(1).broadcast_to([128, NB, NC])
            sc_ = scm[:, 0:NB, :]
            release(dve.tensor_tensor(sc_, src, bias, ALU.add), "scs")
            evacuated(dve, "scs")
            link(dve.tensor_reduce(small[:, 16:24], sc_, AX.X, ALU.max))
            dve.tensor_tensor(sc_, sc_, small[:, 16:24].unsqueeze(2).broadcast_to([128, NB, NC]), ALU.subtract).then_inc(csub, 1)
            dve.wait_ge(cexp, 3)
            link(dve.tensor_reduce(small[:, 32:40], sc_, AX.X, ALU.add))
            link(dve.reciprocal(small[:, 48:56], small[:, 32:40]))
            dve.wait_ge(gate_in, 16 * NB)
            link(dve.tensor_tensor(small[:, 48:56], small[:, 48:56], gsamp[:, :, 0], ALU.mult))
            dve.tensor_tensor(pcsm[:, :, 0:NC], sc_, small[:, 48:56].unsqueeze(2).broadcast_to([128, NB, NC]),
                              ALU.mult).then_inc(pc_ready, 1)
            dve.wait_ge(pc_ready, 3)
            dve.wait_ge(mask_in, 16)
            bn = bsn[:, :, :].rearrange("p b (c t) -> p (b c) t", t=NQ)
            dve.tensor_tensor(bn, bn, bs[:, PAST:PAST + NQ].unsqueeze(1).broadcast_to([128, NB * NB, NQ]), ALU.add).then_inc(bsn_ready, 1)
            dve.wait_ge(bsn_ready, 1)
            for qt in range(2):
                src = filled(dve, ("pct", qt))
                release(dve.tensor_copy(pct[:, qt].rearrange("p g n -> p (g n)"), src), ("pct", qt))
            src = filled(dve, "pcts")
            release(dve.tensor_copy(pcts[:, :, :].rearrange("p a n -> p (a n)"), src[:, 0:256]), "pcts")

            def maxima(buf, n, view):
                o = 8 * buf
                link(dve.tensor_reduce(small[:, o + 4:o + 6], view, AX.X, ALU.max))
                dve.tensor_scalar(small[:, o:o + 2], small[:, o + 4:o + 6], -1.0, None, ALU.mult).then_inc(neg_max, 1)

            def weighted(n, buf, view, gate, width):
                o = 8 * buf
                dve.wait_ge(exp_done, n + 1)
                link(dve.reciprocal(small[:, o + 6:o + 8], small[:, o + 2:o + 4]))
                link(dve.tensor_tensor(small[:, o + 6:o + 8], small[:, o + 6:o + 8], gate, ALU.mult))
                dve.tensor_tensor(view, view, small[:, o + 6:o + 8].unsqueeze(2).broadcast_to([128, 2, width]),
                                  ALU.mult).then_inc(p_ready, 1)

            for i in range(35):
                if i < 32:
                    h, qt = 2 * (i // 4) + i % 2, (i // 2) % 2
                    w_ = 64 * (qt + 1)
                    src = filled(dve, ("s", i))
                    if i >= 2:
                        filled(dve, ("pt", i - 2))
                    e0 = 128 - 128 * qt
                    bias = tz[:, h, e0:e0 + 2 * w_].rearrange("p (t l) -> p l t", l=2).unsqueeze(1).broadcast_to([128, 2, 2, w_])
                    out = s_ring[i % 2][:, 0:4 * w_]
                    release(dve.tensor_tensor(out.rearrange("p (s l t) -> p s l t", s=2, l=2),
                                              src[:, 0:4 * w_].rearrange("p (s l t) -> p s l t", s=2, l=2), bias, ALU.add), ("s", i))
                    evacuated(dve, ("s", i))
                    maxima(i % 2, i, out.rearrange("p (s n) -> p s n", s=2))
                if 1 <= i <= 32:
                    j = i - 1
                    h, qt = 2 * (j // 4) + j % 2, (j // 2) % 2
                    w_ = 64 * (qt + 1)
                    weighted(j, j % 2, s_ring[j % 2][:, 0:4 * w_].rearrange("p (s n) -> p s n", s=2),
                             gates[:, qt, 16 + h:48:16], 2 * w_)
                if i >= 3 and i % 2 == 0:
                    j = (i - 4) // 2
                    src = filled(dve, ("o", j))
                    release(dve.tensor_copy(obT[:, j // 2, 128 * (j % 2):128 * (j % 2) + 128], src[:, 0:128]), ("o", j))
            for b in range(NB + 1):
                if b < NB:
                    src = filled(dve, ("ktb", b, 0))
                    if b >= 2:
                        filled(dve, ("ss", b - 2))
                    release(dve.tensor_copy(ktb[b % 2][:, 0].rearrange("p s l t -> p (s l t)"), src), ("ktb", b, 0))
                if b >= 1:
                    c = b - 1
                    weighted(32 + c, c % 2, s_ring[c % 2].rearrange("p (s n) -> p s n", s=2), gsamp[:, c, 1:3], 320)
                    src = filled(dve, ("pts", c, 1))
                    filled(dve, ("os", b - 3) if b >= 3 else ("o", 15))
                    release(dve.tensor_copy(pts[c % 2][:, 384:640], src[:, 0:256]), ("pts", c, 1))
                    release(dve.tensor_copy(pts[c % 2][0:64, 640:768], src[0:64, 256:384]), ("pts", c, 1))
                if b < NB:
                    src = filled(dve, ("ss", b))
                    buf = s_ring[b % 2].rearrange("p (s n) -> p s n", s=2)
                    bias = bs[:, 0:PAST].rearrange("p (t l) -> p l t", l=2).unsqueeze(1).broadcast_to([128, 2, 2, 128])
                    release(dve.tensor_tensor(buf[:, :, 0:256].rearrange("p s (l t) -> p s l t", l=2),
                                              src.rearrange("p (s l t) -> p s l t", s=2, l=2), bias, ALU.add), ("ss", b))
                    src = filled(dve, ("sn", b))
                    release(dve.tensor_tensor(buf[:, :, 256:320], src[:, 0:128].rearrange("p (s t) -> p s t", s=2),
                                              bsn[:, b, :].unsqueeze(1).broadcast_to([128, 2, 64]), ALU.add), ("sn", b))
                    evacuated(dve, ("ss", b))
                    evacuated(dve, ("sn", b))
                    maxima(b % 2, 32 + b, buf)
                if b >= 1:
                    c = b - 1
                    src = filled(dve, ("os", c))[0:64, 0:128].rearrange("p (m r t) -> p m r t", m=KT, r=2)
                    for par in range(2):
                        release(dve.tensor_copy(obT[64 * par:64 * par + 64, :, NP + NQ * c:NP + NQ * c + NQ], src[:, :, par, :]), ("os", c))
            src = filled(dve, "ws")
            release(dve.tensor_tensor(wsT, src.rearrange("p (g n) -> p g n", g=4),
                                      upper.unsqueeze(1).broadcast_to([128, 4, 128]), ALU.mult), "ws")
            src = filled(dve, "wss")
            release(dve.tensor_tensor(wssT[0:64], src[0:64, 0:256].rearrange("p (g n) -> p g n", g=4),
                                      cst[0:64, K_BLK:K_BLK + 64].unsqueeze(1).broadcast_to([64, 4, 64]), ALU.mult), "wss")
            dve.wait_ge(bmix_in, 16)
            dve.tensor_copy(bmix[:, :, 128:256], bmix[:, :, 0:128]).then_inc(bmix_ready, 1)
            dve.tensor_copy(bmix[:, :, 256:320].rearrange("p g (b t) -> p g b t", b=NB),
                            bmix[:, :, 0:NQ].unsqueeze(2).broadcast_to([128, 4, NB, NQ])).then_inc(bmix_ready, 1)
            rstd(1)
            dve.wait_ge(gain_v_in, 16)
            for t, (_, rows) in enumerate(TILES):
                dve.scalar_tensor_tensor(out=v[0:rows, t, :], in0=v[0:rows, t, :], scalar=stat[0:rows, 1, 3, t:t + 1],
                                         in1=gain_v[0:rows, :], op0=ALU.mult, op1=ALU.mult).then_inc(v_ready, 1)
            dve.wait_ge(bmix_ready, 2)
            for m in range(KT):
                src = filled(dve, ("mx", m))
                job = ("mx", m)
                ins = dve.tensor_tensor(mix_tmp, src[:, 0:N], bmix[:, m // 2, :], ALU.add)
                release(ins, job)
                bank, _, read, _ = plan[job]
                dve.wait_ge(bank_read[bank], read + 1)
                evacuated(dve, ("u", m))
                release(dve.tensor_tensor(uT[:, m, :], uT[:, m, :], mix_tmp, ALU.mult), job)
                evacuated(dve, job)
            dve.wait_ge(v_out, 16)
            for m in range(KT):
                src = filled(dve, ("br", 0, m))
                evacuated(dve, ("gm", m))
                release(dve.tensor_tensor(mergedT[:, m, :], src[:, 0:N], gmT[:, m, :], ALU.mult), ("br", 0, m))
            for m in range(KT):
                src = filled(dve, ("br", 1, m))
                evacuated(dve, ("gm", KT + m))
                evacuated(dve, ("br", 0, m))
                release(dve.tensor_tensor(gmT[:, KT + m, :], src[:, 0:N], gmT[:, KT + m, :], ALU.mult), ("br", 1, m))
                evacuated(dve, ("br", 1, m))
                dve.tensor_tensor(mergedT[:, m, :], mergedT[:, m, :], gmT[:, KT + m, :], ALU.add).then_inc(normed, 1)
            for c in range(2):
                for t, (_, rows) in enumerate(TILES):
                    src = filled(dve, ("xo", c, t))
                    xs = x[0:rows, t, 512 * c:512 * c + 512]
                    release(dve.tensor_tensor(xs, xs, src[0:rows, :], ALU.add), ("xo", c, t))
            rstd(2)
            scaled(2, x, xn2)
            dve.memset(xn2[64:128, 2, :], 0.0).then_inc(xn2_pad, 1)
            for k in range(0, KT, 2):
                src = filled(dve, ("hT2", k))
                release(dve.tensor_scalar(hT[:, k, :], src[:, 0:N], cols[:, 8 + k:9 + k], None, ALU.mult), ("hT2", k))
            def r3(a, n):
                return route[:, a:a + 3 * n].rearrange("p (t n) -> p t n", t=3)
            logits, g8, gtop, gidx = r3(0, 36), r3(108, 8), r3(132, 8), route[:, :].bitcast(U32)[:, 156:180].rearrange("p (t n) -> p t n", t=3)
            ohg, prod, se8, stop_, sidx = r3(180, 4), r3(192, 32), r3(288, 8), r3(312, 8), route[:, :].bitcast(U32)[:, 336:360].rearrange("p (t n) -> p t n", t=3)
            a1, a2, aa = r3(360, 32), r3(456, 32), r3(576, 32)
            ranks, tmp = r3(672, 32), r3(768, 32)
            lg4, dl = r3(864, 4), route[:, 880:883]
            gf, e1, e2, i1, pg, w1_, w2_, den = (route[:, 884 + 3 * j:887 + 3 * j] for j in range(8))
            dest = route[:, 908:914]
            desti = route[:, :].bitcast(U32)[:, 914:920]
            rank_a = route[:, 920:1016].rearrange("p (e t) -> p e t", e=NE)
            rank12, w_more, dest_more = route[:, 108:114], route[:, 114:120], route[:, 120:126]
            mostf = route[:, 1018:1019]
            iota_e = cst[:, K_E:K_E + NE]

            def bc(ap, n):
                return ap.unsqueeze(2).broadcast_to([128, 3, n])

            link(dve.memset(logits, 0.0))
            link(dve.memset(g8, -3e38))
            src = filled(dve, "router")
            dve.wait_ge(br_in, 64)
            release(dve.tensor_tensor(logits[:, 0:2, :], src[:, 0:72].rearrange("p (t n) -> p t n", t=2),
                                      biasr[:, :].unsqueeze(1).broadcast_to([128, 2, 36]), ALU.add), "router")
            release(dve.tensor_tensor(logits[0:64, 2, :], src[0:64, 72:108], biasr[0:64, :], ALU.add), "router")
            evacuated(dve, "router")
            for k in range(2):
                src = filled(dve, ("ppT", k))
                release(dve.tensor_copy(pT[:, k, :], src[:, 0:N]), ("ppT", k))
            link(dve.tensor_copy(g8[:, :, 0:4], logits[:, :, 0:4]))
            for t in range(3):
                link(dve.max(out=gtop[:, t, :], in_=g8[:, t, :]))
                link(dve.max_index(out=gidx[:, t, :], in_max=gtop[:, t, :], in_values=g8[:, t, :]))
            dve.tensor_tensor(lg4, g8[:, :, 0:4], bc(gtop[:, :, 0], 4), ALU.subtract).then_inc(gexp_in, 1)
            link(dve.tensor_copy(gf, gidx[:, :, 0]))
            link(dve.tensor_tensor(ohg, iota_e[:, 0:4].unsqueeze(1).broadcast_to([128, 3, 4]), bc(gf, 4), ALU.is_equal))
            for t in range(3):
                ins = dve.tensor_tensor(prod[:, t, :].rearrange("p (g j) -> p g j", g=4),
                                        logits[:, t, 4:36].rearrange("p (g j) -> p g j", g=4),
                                        ohg[:, t, :].unsqueeze(2).broadcast_to([128, 4, 8]), ALU.mult)
            link(ins)
            link(dve.tensor_reduce(se8, prod.rearrange("p t (g j) -> p t j g", g=4), AX.X, ALU.add))
            for t in range(3):
                link(dve.max(out=stop_[:, t, :], in_=se8[:, t, :]))
                link(dve.max_index(out=sidx[:, t, :], in_max=stop_[:, t, :], in_values=se8[:, t, :]))
            dve.tensor_tensor(dl, stop_[:, :, 1], stop_[:, :, 0], ALU.subtract).then_inc(dexp_in, 1)
            for k, (e_, a_) in enumerate(((e1, a1), (e2, a2))):
                link(dve.tensor_copy(i1, sidx[:, :, k]))
                link(dve.scalar_tensor_tensor(out=e_, in0=gf, scalar=float(EPG), in1=i1, op0=ALU.mult, op1=ALU.add))
                link(dve.tensor_tensor(a_, iota_e.unsqueeze(1).broadcast_to([128, 3, NE]), bc(e_, NE), ALU.is_equal))
                link(dve.memset(a_[64:128, 2, :], 0.0))
            dve.tensor_tensor(aa, a1, a2, ALU.add).then_inc(assigned, 1)
            dve.wait_ge(gexp, 1)
            link(dve.tensor_reduce(den, lg4, AX.X, ALU.add))
            link(dve.reciprocal(pg, den))
            dve.wait_ge(dexp, 1)
            link(dve.tensor_scalar(den, dl, 1.0, None, ALU.add))
            link(dve.reciprocal(den, den))
            link(dve.tensor_tensor(w1_, pg, den, ALU.mult))
            link(dve.tensor_tensor(w2_, w1_, dl, ALU.mult))
            src = filled(dve, "rank")
            dve.tensor_reduce(mostf, src[:, 96:128], AX.X, ALU.max)
            release(dve.tensor_copy(ranks, src[:, 0:96].rearrange("p (t e) -> p t e", t=3)), "rank")
            evacuated(dve, "rank")
            link(dve.tensor_tensor(tmp, aa, ranks, ALU.mult))
            link(dve.tensor_scalar(rank_a.rearrange("p e t -> p t e"), tmp, -1.0, None, ALU.add))
            dve.tensor_copy(route[:, :].bitcast(I32)[:, 1019:1020], mostf).then_inc(ranked, 1)
            for k, (e_, a_) in enumerate(((e1, a1), (e2, a2))):
                link(dve.tensor_tensor(tmp, a_, ranks, ALU.mult))
                link(dve.tensor_reduce(i1, tmp, AX.X, ALU.add))
                rk, wm, wk = rank12[:, 3 * k:3 * k + 3], w_more[:, 3 * k:3 * k + 3], (w1_, w2_)[k]
                link(dve.tensor_scalar(rk, i1, -1.0, None, ALU.add))
                link(dve.tensor_scalar(i1, rk, float(SLOTS - 1), None, ALU.min))
                dve.scalar_tensor_tensor(out=dest[:, 3 * k:3 * k + 3], in0=e_, scalar=float(SLOTS), in1=i1, op0=ALU.mult, op1=ALU.add)
                link(dve.tensor_scalar(wm, rk, float(SLOTS), None, ALU.is_ge))
                link(dve.tensor_tensor(wm, wm, wk, ALU.mult))
                link(dve.tensor_tensor(wk, wk, wm, ALU.subtract))
                link(dve.tensor_scalar(i1, rk, -float(SLOTS), 0.0, ALU.add, ALU.max))
                link(dve.scalar_tensor_tensor(out=dest_more[:, 3 * k:3 * k + 3], in0=e_, scalar=float(MORE), in1=i1, op0=ALU.mult, op1=ALU.add))
            link(dve.tensor_copy(route[:, :].bitcast(U32)[:, 126:132], dest_more))
            dve.tensor_copy(desti, dest).then_inc(ranked, 1)
            dve.wait_ge(ranked, 2)

            def select(e, buf, first):
                return dve.tensor_tensor(buf, iota[:, first:first + SLOTS].unsqueeze(1).broadcast_to([128, 3, SLOTS]),
                                         rank_a[:, bass.ds(e, 1), :].rearrange("p a t -> p (a t)").unsqueeze(2).broadcast_to([128, 3, SLOTS]),
                                         ALU.is_equal)

            gain = cols[:, 8:16].unsqueeze(2).broadcast_to([128, KT, SLOTS])

            select(0, sel[0], 0).then_inc(sel_ready, 1)

            def expert_steps(i, par, last_one=False):
                e = i * 2 + par
                if not last_one:
                    dve.wait_ge(gathered, e + 1)
                    select(e + 1, sel[1 - par], 0).then_inc(sel_ready, 1)
                dve.wait_ge(gathered, e + 1)
                dve.tensor_tensor(xe[par], ps[:, par, :].rearrange("p (k n) -> p k n", k=KT), gain, ALU.mult).then_inc(xe_ready, 1)
                dve.wait_ge(silu_done, e + 1)
                dve.wait_ge(up_done, e + 1)
                dve.tensor_tensor(sg, sg, ps[64:128, 2 + par, :], ALU.mult).then_inc(sg_ready, 1)
                dve.wait_ge(turned, e + 1)
                dve.tensor_copy(he[par].rearrange("p m n -> p (m n)"), ps[:, 6, 0:256]).then_inc(he_ready, 1)

            with dve.Fori(0, NE // 2 - 1) as i:
                expert_steps(i, 0)
                expert_steps(i, 1)
            expert_steps(NE // 2 - 1, 0)
            expert_steps(NE // 2 - 1, 1, True)
            most = dve.value_load(route[:, :].bitcast(I32)[0:1, 1019:1020], min_val=0, max_val=N)
            with dve.If(most > SLOTS):
                dve.wait_ge(ye_ready, NE + 2)
                with dve.Fori(0, NE) as e:
                    for blk in range(EXTRA):
                        n = e * EXTRA + blk + 1
                        select(e, sel[0], SLOTS * (blk + 1)).then_inc(ov["sel"], 1)
                        dve.wait_ge(ov["gathered"], n)
                        dve.tensor_tensor(xe[0], ps[:, 0, :].rearrange("p (k n) -> p k n", k=KT), gain, ALU.mult).then_inc(ov["xe"], 1)
                        dve.wait_ge(ov["silu"], n)
                        dve.tensor_tensor(sg, sg, ps[64:128, 2, :], ALU.mult).then_inc(ov["sg"], 1)
                        dve.wait_ge(ov["turned"], n)
                        dve.tensor_copy(he[0].rearrange("p m n -> p (m n)"), ps[:, 6, 0:256]).then_inc(ov["he"], 1)
                        dve.wait_ge(ov["down"], n + 1)
                dve.wait_ge(ov["rows"], 96)
                for t, (_, rows) in enumerate(TILES):
                    for k in range(2):
                        dve.scalar_tensor_tensor(out=x[0:rows, t, :], in0=gath[k][t][0:rows, :],
                                                 scalar=w_more[0:rows, 3 * k + t:3 * k + t + 1],
                                                 in1=x[0:rows, t, :], op0=ALU.mult, op1=ALU.add).then_inc(ov["added"], 1)
                        dve.wait_ge(ov["added"], 2 * t + k + 1)
            for t, (_, rows) in enumerate(TILES):
                for k, w_ in enumerate((w1_, w2_)):
                    dve.wait_ge(rows_back[2 * t + k], 16)
                    ins = dve.scalar_tensor_tensor(out=x[0:rows, t, :], in0=gath[k][t][0:rows, :], scalar=w_[0:rows, t:t + 1],
                                                   in1=x[0:rows, t, :], op0=ALU.mult, op1=ALU.add)
                    if k == 0:
                        link(ins)
                ins.then_inc(x2_done, 1)
            rstd(3)
            scaled(3, x, xn2)
            for k in range(0, KT, 2):
                src = filled(dve, ("hT3", k))
                release(dve.tensor_scalar(hT[:, k, :], src[:, 0:N], cols[:, 16 + k:17 + k], None, ALU.mult), ("hT3", k))
            for c in range(2):
                for t, (_, rows) in enumerate(TILES):
                    n = 3 * c + t
                    part = pgate[0:rows, t, 512 * c:512 * c + 512]
                    xs = x[0:rows, t, 512 * c:512 * c + 512]
                    dve.wait_ge(pg_sig, n + 1)
                    evacuated(dve, ("pp", c, t))
                    link(dve.tensor_tensor(part, part, pp[0:rows, t, 512 * c:512 * c + 512], ALU.mult))
                    dve.tensor_tensor(xs, xs, part, ALU.add).then_inc(y_done, 1)
            rstd(4)
            dve.wait_ge(gain_f_in, 16)
            for t, (_, rows) in enumerate(TILES):
                dve.scalar_tensor_tensor(out=ysb[0:rows, t, :], in0=x[0:rows, t, :], scalar=stat[0:rows, 4, 3, t:t + 1],
                                         in1=gain_f[0:rows, :], op0=ALU.mult, op1=ALU.mult).then_inc(y_done, 1)

        @block.gpsimd
        def _(pool):
            pool.dma_start(page_sb[:, :], page_table.rearrange("b p -> (b p)").unsqueeze(0)).then_inc(pool_chain, 16)
            pool.dma_start(bsn[:, :, :], at(other, 0, [[0, 128], [64, NB], [1, 64]])).then_inc(mask_in, 16)
            evacuated(pool, "tab")
            pool.dma_start(tab, tab_sb.unsqueeze(1).broadcast_to([H, 128, TABN])).then_inc(tab_out, 16)
            pool.wait_ge(pool_chain, 16)
            hist = cache_kv[0].rearrange("a (t l) s g d -> a t l (s g) d", l=2)

            def page_rows(b, half):
                page = pool.value_load(page_sb[0:1, 2 * b + half:2 * b + half + 1], min_val=0, max_val=n_pages - 1)
                return hist[bass.ds(page, 1)].rearrange("a t l s d -> (a t) l s d")

            for b in range(NB):
                if b >= 2:
                    filled(pool, ("xt", b - 1, 1))
                for half in range(2):
                    src = page_rows(b, half)
                    for l in range(2):
                        pool.dma_start(cst_in[b % 2][64 * half:64 * half + 64, :, l, :], src[:, l, 0:8, :]).then_inc(hist_in[b % 2], 16)
                if b == 0:
                    pool.wait_ge(tab_out, 16)
                    pool.dma_start(bs[:, :], at(tab, NQ - 1, [[128 * TABN, H], [TABN - 1, NQ], [1, PAST + NQ]])).then_inc(bias_in, 16)
            for c in range(3):
                for s in range(3):
                    evacuated(pool, ("kv", c, s))
            rows = kv_rows_prompt.rearrange("a b (t l) s g d -> (a b t) l (s g d)", l=2)
            for l in range(2):
                pool.dma_start(rows[:, l, 0:512].rearrange("t (a d) -> t a d", d=DH),
                               kvc[:, :, :, l, :].rearrange("p s g d -> p (s g) d")).then_inc(kv_out, 16)
            pool.dma_start(rows[:, :, 512:1024], kvp[:, :, 0, :]).then_inc(kv_out, 16)
            pool.dma_start(win_prompt.rearrange("a b (t l) s g d -> (a b t) l (s g d)", l=2), kvp[:, :, 1, :]).then_inc(kv_out, 16)
            pool.dma_start(kv_rows_sample.rearrange("a b t s g d -> (a b t) (s g d)"), kvs[0:64, 0:1024]).then_inc(kv_out, 16)
            wnew = win_sample.rearrange("a b t s g d -> (a b) t (s g d)")
            pool.dma_start(wnew[:, PAST - NQ:PAST, :], kvs[0:64, 1024:1536]).then_inc(kv_out, 16)
            evacuated(pool, "gates")
            for br in range(3):
                pool.dma_start(at(gate_rows, br, [[3, NS], [3 * NS, H]]), gates[0:64, 2, H * br:H * br + H],
                               allow_slow_non_contiguous=True).then_inc(gate_out, 16)
            filled(pool, ("h1", 1, 1, 0))
            pool.dma_start(tz, at(tab, MAXD - 128, [[TABN - 1, 128], [128 * TABN, H], [1, 256]])).then_inc(bias_in, 16)
            pool.wait_ge(gate_out, 48)
            for b in range(NB):
                pool.dma_start(gsamp[:, b, :], at(gate_rows, 3 * NQ * b, [[3 * NS, H], [3, NQ], [1, 3]])).then_inc(gate_in, 16)
            filled(pool, "vcp")
            for b in range(NB):
                if b >= 2:
                    filled(pool, ("os", b - 2))
                for half in range(2):
                    pool.dma_start(slc_in[b % 2][64 * half:64 * half + 64].rearrange("p l (a d) -> p l a d", d=DH),
                                   page_rows(b, half)[:, :, 8:16, :]).then_inc(stage_in[b % 2], 16)
                pool.dma_start(win_in[b % 2], state_win_kv[0, b].rearrange("(t l) s g d -> t l (s g d)", l=2)).then_inc(stage_in[b % 2], 16)
            wold = state_win_kv.rearrange("a b t s g d -> (a b) t (s g d)")
            pool.dma_start(wnew[:, 0:PAST - NQ, :], wold[:, NQ:PAST, :]).then_inc(out_done, 16)
            filled(pool, ("o", 15))
            pool.dma_start(gain_v, at(v_norm, 0, [[0, 128], [1, D]])).then_inc(gain_v_in, 16)
            filled(pool, ("os", NB - 1))
            pool.dma_start(ws_in, w_spatial[0].rearrange("g r s -> r g s")).then_inc(ws_in_s, 16)
            pool.dma_start(bmix[:, :, 0:128], at(b_spatial, 0, [[0, 128], [128, 4], [1, 128]])).then_inc(bmix_in, 16)
            filled(pool, "ws")
            pool.dma_start(p_in[:, 0:2, :], p_prompt.rearrange("a b (t p) n -> p (a b t) n", p=128)).then_inc(p_in_s, 16)
            pool.dma_start(p_in[0:64, 2, :], p_sample.rearrange("a b t n -> (a b t) n")).then_inc(p_in_s, 16)
            pool.wait_ge(v_ready, 3)
            pool.dma_start(chunk_v_sample.rearrange("a b t n -> (a b t) n"), v[0:64, 2, :]).then_inc(v_out, 16)

            first_rows = y_rows.rearrange("(e r) n -> e r n", e=NE)
            more_rows = y_more.rearrange("(e r) n -> e r n", e=NE)

            def halves(rows_dram):
                return rows_dram.rearrange("r (c n) -> c r n", c=2)

            def gather_rows(rows_dram, first_col, sems):
                idx = route[:, :].bitcast(U32)[:, first_col:first_col + 6]
                for t, (_, rows) in enumerate(TILES):
                    for k in range(2):
                        pool.indirect_dma_start(gath[k][t][0:rows, :], None, rows_dram,
                                                bass.IndirectOffsetOnAxis(ap=idx[0:rows, 3 * k + t:3 * k + t + 1], axis=0)
                                                ).then_inc(sems[2 * t + k], 16)

            with pool.Fori(0, NE // 2) as i:
                for par in range(2):
                    pool.wait_ge(ye_ready, i * 2 + par + 3)
                    dst = first_rows[bass.ds(i * 2 + par, 1)].rearrange("a r n -> (a r) n")
                    pool.dma_start(halves(dst), ye[par]).then_inc(ye_out[par], 16)
            for par in range(2):
                pool.wait_ge(ye_out[par], NE // 2 * 16)
            pool.wait_ge(ranked, 2)
            most = pool.value_load(route[:, :].bitcast(I32)[0:1, 1019:1020], min_val=0, max_val=N)
            with pool.If(most > SLOTS):
                pool.sem_inc(ov["out"], 1)
                with pool.Fori(0, NE) as e:
                    for blk in range(EXTRA):
                        n = e * EXTRA + blk + 1
                        pool.wait_ge(ov["ye"], n + 1)
                        dst = more_rows[bass.ds(e, 1), SLOTS * blk:SLOTS * (blk + 1)].rearrange("a r n -> (a r) n")
                        pool.dma_start(halves(dst), ye[0]).then_inc(ov["stored"], 16)
                        pool.wait_ge(ov["stored"], n * 16)
                        pool.sem_inc(ov["out"], 1)
                gather_rows(y_more, 126, [ov["rows"]] * 6)
                pool.wait_ge(ov["added"], 6)
            pool.wait_ge(down_done, NE)
            gather_rows(y_rows, 914, rows_back)
            pool.dma_start(gain_f, at(final_norm, 0, [[0, 128], [1, D]])).then_inc(gain_f_in, 16)
            pool.wait_ge(y_done, 8)
            pool.dma_start(y_prompt.rearrange("a (t p) n -> p (a t) n", p=128), ysb[:, 0:2, :]).then_inc(out_done, 16)
            pool.wait_ge(y_done, 9)
            pool.dma_start(y_sample.rearrange("a b n -> (a b) n"), ysb[0:64, 2, :]).then_inc(out_done, 16)
            pool.wait_ge(out_done, 48)
            pool.wait_ge(v_out, 16)
            pool.wait_ge(kv_out, 16 * 6)


_INS = ['x_prompt', 'x_sample', 'cache_kv', 'state_win_kv', 'page_table', 'p_prompt', 'p_sample', 'rel_bias',
        'norm_mix', 'w_in', 'v_norm', 'w_spatial', 'b_spatial', 'pe_cmp', 'w_phi1', 'w_phi2', 'w_branch', 'w_out',
        'norm_ffn', 'w_router_group', 'b_router_group', 'w_router_expert', 'b_router_expert',
        'w_exp_gate', 'w_exp_up', 'w_exp_down', 'norm_ple', 'w_ple_gate', 'w_ple_proj', 'final_norm']
_OUTS = [('y_prompt', (1, NP, D)), ('y_sample', (NB, NQ, D)), ('kv_rows_prompt', (1, 1, NP, 4, G, DH)),
         ('kv_rows_sample', (1, NB, NQ, 4, G, DH)), ('win_prompt', (1, 1, NP, 2, G, DH)),
         ('win_sample', (1, NB, PAST, 2, G, DH)), ('chunk_v_sample', (1, NB, NQ, D))]


def kernel(**inputs):
    import concourse.bacc as bacc
    from concourse.bass_utils import run_bass_kernel_spmd

    nc = bacc.Bacc("TRN2", target_bir_lowering=False, num_devices=1)
    consts, hot, other = shape_constants()
    arrays, args = {}, []
    for name, a in [(n, inputs[n]) for n in _INS] + [("consts", consts), ("hot", hot), ("other", other)]:
        a = np.ascontiguousarray(a)
        arrays[f"in_{name}_dram"] = a
        args.append(nc.dram_tensor(f"in_{name}_dram", a.shape, mybir.dt.from_np(a.dtype), kind="ExternalInput").ap())
    for name, shape in _OUTS:
        args.append(nc.dram_tensor(f"out_{name}_dram", shape, F32, kind="ExternalOutput").ap())
    build(nc, *args)
    r = run_bass_kernel_spmd(nc, [arrays], core_ids=[0])
    return tuple(r.results[0][f"out_{name}_dram"] for name, _ in _OUTS)
```

```python
from contextlib import ExitStack

import numpy as np

import concourse.bass as bass
from concourse import mybir

F32 = mybir.dt.float32
I32 = mybir.dt.int32
U32 = mybir.dt.uint32
ALU = mybir.AluOpType
ACT = mybir.ActivationFunctionType
AX = mybir.AxisListType

D = 1024
KT = D // 128
NP, NS, NB = 256, 64, 8
NQ = NS // NB
N = NP + NS
PAST = 256
H, G, HPG, DH = 16, 4, 4, 64
NC = 15
NSEQ = 1 + NB
XROWS = G * NSEQ + 1
BUCKETS, MAX_DISTANCE = 32, 128
MAXD = PAST + NQ - 1
TABN = MAXD + 1 + 127
NE, EPG, NG, DE = 32, 8, 4, 512
SLOTS = 64
EXTRA = N // SLOTS - 1
MORE = N - SLOTS
EPS = 1e-6
NEG = -1e30
TILES = ((0, 128), (128, 128), (256, 64))
CU, CV_, CQ, CKV, CGN, CGM = 0, 1024, 2048, 3072, 4608, 4656

K_ID, K_UP, K_BLK, K_REP, K_IOTA, K_E, K_VALID = 0, 128, 256, 320, 384, 704, 736
K_ALL = 737


def shape_constants():
    c = np.zeros((128, K_ALL), np.float32)
    r = np.arange(128)
    c[:, K_ID:K_ID + 128] = np.eye(128)
    c[:, K_UP:K_UP + 128] = r[:, None] <= r[None, :]
    s = np.arange(64)
    c[:64, K_BLK:K_BLK + 64] = s[:, None] // NQ == s[None, :] // NQ
    c[:NQ, K_REP:K_REP + 64] = np.arange(NQ)[:, None] == s[None, :] % NQ
    c[:, K_IOTA:K_IOTA + N] = np.arange(N)
    c[:, K_E:K_E + NE] = np.arange(NE)
    c[:, K_VALID] = r >= 31
    dist = MAXD - np.arange(TABN)
    n = np.maximum(dist, 0)
    half = BUCKETS // 2
    nf = np.maximum(n, half).astype(np.float32)
    big = half + (np.log(nf / half) / np.float32(np.log(MAX_DISTANCE / half)) * half).astype(np.int32)
    bucket = np.where(n < half, n, np.minimum(big, BUCKETS - 1))
    hot = np.zeros((BUCKETS + 1, TABN), np.float32)
    hot[bucket, np.arange(TABN)] = dist >= 0
    hot[BUCKETS] = dist < 0
    other = np.where(np.arange(NB)[:, None] == s[None, :] // NQ, 0.0, NEG).astype(np.float32)
    return c, hot, other


def psum_plan():
    jobs = [("cols", 1)]
    jobs += [(("hT", k), 1) for k in range(KT)]
    jobs += [(("kv", 0, s), 1 + (s == 2)) for s in range(3)] + [("tab", 1)]
    jobs += [(("kv", c, s), 1 + (s == 2)) for c in (1, 2) for s in range(3)]
    jobs += [("gates", 2), (("ktp", 0), 1), (("ktp", 1), 1), ("ktn", 1)]
    jobs += [(("xt", s, kv), 1) for s in range(NSEQ) for kv in range(2)]
    jobs += [(("h1", kv, hid, half), 1 + (half == 1) + (kv == 1)) for kv in range(2) for hid in range(2) for half in (1, 0)]
    jobs += [(("kc", half), 2) for half in range(2)] + [("vcs", 1), ("vcp", 1)]
    jobs += [(("q", m), 2) for m in range(KT)]
    jobs += [(("sc", qt, par), 1) for qt in range(2) for par in range(2)] + [("scs", 1)]
    jobs += [(("pct", 0), 1), (("pct", 1), 1), ("pcts", 1)]
    before, jobs = jobs, []
    for i in range(35):
        if i < 32:
            jobs.append((("s", i), 1))
        if 2 <= i <= 33:
            jobs.append((("pt", i - 2), 1))
        if i >= 3 and i % 2 == 1:
            jobs.append((("o", (i - 3) // 2), 1))
    for b in range(NB + 1):
        if b < NB:
            jobs += [(("ktb", b, 0), 1), (("ktb", b, 1), 1)]
        if b >= 1:
            jobs += [(("pts", b - 1, 0), 2), (("pts", b - 1, 1), 2)]
        if b < NB:
            jobs += [(("ss", b), 1), (("sn", b), 1)]
        if b >= 1:
            jobs += [(("os", b - 1), 2)]
    attention, jobs = jobs, []
    between = [(("v", c, t), 1 + (t == 2)) for c in range(2) for t in range(3)] + [(("gm", m), 1) for m in range(2 * KT)]
    between += [(("u", m), 1) for m in range(2)]
    jobs += [("ws", 1)] + [(("u", m), 1) for m in (2, 3)] + [("wss", 1)] + [(("u", m), 1) for m in range(4, KT)]
    jobs += [(("mx", m), 2) for m in range(KT)]
    jobs += [(("br", j, m), 1) for j in range(2) for m in range(KT)]
    jobs += [(("xo", c, t), 1 + (t == 2)) for t in range(3) for c in range(2)]
    jobs += [(("hT2", k), 1) for k in range(KT)] + [("router", 2)]
    jobs += [("rank", 1)]
    tail = [(("ppT", k), 1) for k in range(2)] + [(("pp", c, t), 1) for c in range(2) for t in range(3)]
    tail += [(("hT3", k), 1) for k in range(KT)] + [(("pg", c, t), 1 + (t == 2)) for t in range(3) for c in range(2)]
    plan, full, read = {}, [0] * 8, [0] * 8

    def assign(some, banks):
        for n, (name, releases) in enumerate(some):
            bank = banks[n % len(banks)]
            full[bank] += 1
            plan[name] = (bank, full[bank], read[bank], read[bank] + releases)
            read[bank] += releases

    assign(before, range(8))
    assign(attention, range(6))
    assign(between, (6, 7))
    assign(jobs, range(8))
    plan["expert loop"] = list(read)
    assign(tail, range(8))
    return plan


def ring_plan():
    e = [(("kv", 0), 0, ("kv", 0, 2)), (("kv", 1), 1, ("kv", 1, 2)), (("kv", 2), 2, ("kv", 2, 2)),
         (("w1", 0), 3, ("h1", 0, 1, 0)), (("w1", 1), 0, ("h1", 1, 1, 0)),
         (("q", 0), 1, ("q", 3)), (("q", 1), 2, ("q", 7)),
         (("v", 0), 3, ("v", 0, 2)), (("v", 1), 0, ("v", 1, 2)),
         (("gm", 0), 1, ("gm", 3)), (("gm", 1), 2, ("gm", 7)), (("gm", 2), 3, ("gm", 11)), (("gm", 3), 0, ("gm", 15)),
         (("u", 0), 1, ("u", 3)), (("u", 1), 2, ("u", 7)),
         (("br", 0, 0), 3, ("br", 0, 3)), (("br", 0, 1), 0, ("br", 0, 7)),
         (("br", 1, 0), 1, ("br", 1, 3)), (("br", 1, 1), 2, ("br", 1, 7)),
         (("xo", 0), 3, ("xo", 1, 2)), (("xo", 1), 4, ("xo", 1, 2))]
    return e


def build(nc, x_prompt, x_sample, cache_kv, state_win_kv, page_table, p_prompt, p_sample, rel_bias,
          norm_mix, w_in, v_norm, w_spatial, b_spatial, pe_cmp, w_phi1, w_phi2, w_branch, w_out,
          norm_ffn, w_router_group, b_router_group, w_router_expert, b_router_expert,
          w_exp_gate, w_exp_up, w_exp_down, norm_ple, w_ple_gate, w_ple_proj, final_norm,
          consts, hot, other,
          y_prompt, y_sample, kv_rows_prompt, kv_rows_sample, win_prompt, win_sample, chunk_v_sample):
    plan = psum_plan()
    ring_entries = ring_plan()
    n_pages = cache_kv.shape[1]

    def at(ap, offset, pattern):
        return bass.AP(tensor=ap.tensor, offset=offset, ap=pattern)

    with ExitStack() as ctx:
        def sb(name, shape, dt=F32):
            return ctx.enter_context(nc.sbuf_tensor(name, shape, dt))

        def sem(name):
            return ctx.enter_context(nc.semaphore(name))

        def scratch(name, shape, dt=F32):
            return nc.dram_tensor(name, shape, dt, kind="Internal").ap()

        ps = ctx.enter_context(nc.psum_tensor("ps", [128, 8, 512], F32))
        ring = sb("ring", [128, 4, 4096])
        late = sb("late", [128, 2, 4096])
        hT = sb("hT", [128, KT, N])
        reg_x = sb("reg_x", [128, 9472])
        reg_k = sb("reg_k", [128, 4608])
        x = sb("x", [128, 3, D])
        cst = sb("cst", [128, K_ALL])
        rows56 = sb("rows56", [56, 128])
        cols = sb("cols", [128, 56])
        stat = sb("stat", [128, 5, 4, 3])
        gates = sb("gates", [128, 3, 48])
        gsamp = sb("gsamp", [128, NB, 3])
        wgn = sb("wgn", [128, KT, 48])
        wr = sb("wr", [128, KT, 36])
        biasr = sb("biasr", [128, 36])
        w2 = sb("w2", [128, 2, 2, DH])
        b1 = sb("b1", [128, 4])
        kcT = sb("kcT", [128, 2, NSEQ, NC])
        vcs = sb("vcs", [128, 8, DH])
        vcp = sb("vcp", [128, G, DH])
        reg_kt = sb("reg_kt", [128, 1024])
        obT = sb("obT", [128, KT, N])
        reg_pc = sb("reg_pc", [128, 1024])
        bs = sb("bs", [128, PAST + NQ])
        bsn = sb("bsn", [128, NB, 64])
        small = sb("small", [128, 96])
        page_sb = sb("page_sb", [1, 16], I32)

        obT_flat = obT[:, :, :].rearrange("p m n -> p (m n)")
        slots = [ring[:, s, :] for s in range(4)] + [late[:, s, :] for s in range(2)]
        xt = reg_x[:, 0:2 * XROWS * 128].rearrange("p (k r t) -> p k r t", k=2, r=XROWS)
        qT = reg_x[:, 0:2560].rearrange("p (m n) -> p m n", m=KT)
        qs = reg_x[:, 2560:3584].rearrange("p (b g n) -> p b g n", b=NB, g=G)
        tz = reg_x[:, 3584:7680].rearrange("p (h e) -> p h e", h=H)
        s_ring = [reg_x[:, 7680 + 640 * i:7680 + 640 * (i + 1)] for i in range(2)] + [reg_x[:, 8960:9472]]
        pcsm = reg_x[:, 8960:9216].rearrange("p (b c) -> p b c", b=NB)
        scm = reg_x[:, 9216:9456].rearrange("p (h c) -> p h c", h=H)
        gmT = [reg_x[:, a:a + 2560].rearrange("p (m n) -> p m n", m=KT) for a in (0, 3584)]
        v_junk = reg_x[:, 6144:9216].rearrange("p (t n) -> p t n", t=3)
        xo_half = reg_x[0:64, 5120:5632].rearrange("p (c n) -> p c n", c=2)
        mergedT = reg_x[:, 6144:8704].rearrange("p (m n) -> p m n", m=KT)
        xn2 = reg_x[:, 0:3072].rearrange("p (t n) -> p t n", t=3)
        xe = [reg_x[:, 5120 + 512 * i:5632 + 512 * i].rearrange("p (k n) -> p k n", k=KT) for i in range(2)]
        he = [reg_x[:, 6144 + 256 * i:6400 + 256 * i].rearrange("p (m n) -> p m n", m=4) for i in range(2)]
        sg = reg_x[64:128, 6656:7168]
        ye = [reg_x[:, 7168 + 512 * i:7680 + 512 * i] for i in range(2)]
        sel = [reg_x[:, 8960 + 192 * i:9152 + 192 * i].rearrange("p (t n) -> p t n", t=3) for i in range(2)]
        xn = reg_k[:, 0:3072].rearrange("p (t n) -> p t n", t=3)
        kvc = reg_k[:, 0:1024].rearrange("p (s g l d) -> p s g l d", s=2, g=G, l=2)
        kvp = reg_k[:, 1024:3072].rearrange("p (l s n) -> p l s n", l=2, s=2)
        kvs = reg_k[:, 3072:4608]
        pc = reg_k[:, 0:1024].rearrange("p (q h c) -> p q h c", q=2, h=H)
        ktb = [reg_k[:, 1024 + 1024 * i:2048 + 1024 * i].rearrange("p (g s l t) -> p g s l t", g=2, s=2, l=2) for i in range(2)]
        bmix = reg_k[:, 2560:3840].rearrange("p (g n) -> p g n", g=4)
        wsT = reg_k[:, 3840:4352].rearrange("p (g n) -> p g n", g=4)
        wssT = reg_k[:, 4352:4608].rearrange("p (g n) -> p g n", g=4)
        pp = reg_k[:, 0:3072].rearrange("p (t n) -> p t n", t=3)
        early = late[:, :, :].rearrange("p s n -> p (s n)")
        cst_in = [a.rearrange("p (a l d) -> p a l d", a=8, l=2) for a in
                  (early[:, 0:1024], early[:, 1024:2048], reg_pc[:, :], obT_flat[:, 0:1024], obT_flat[:, 1024:2048])]
        h1k = early[:, 2048:3128].rearrange("p (h r c) -> p h r c", h=2, r=36)
        h1v = early[:, 3200:6272].rearrange("p (h r c) -> p h r c", h=2, r=48)
        hot_sb = early[0:BUCKETS + 1, 7168:7168 + TABN]
        rel_sb = early[0:BUCKETS + 1, 7600:7600 + H]
        tab_sb = early[0:H, 7680:7680 + TABN]
        slc_in = [early[:, 1024 * i:1024 * i + 1024].rearrange("p (l n) -> p l n", l=2) for i in range(2)]
        win_in = [early[:, 2048 + 1024 * i:3072 + 1024 * i].rearrange("p (l n) -> p l n", l=2) for i in range(2)]
        v = [early[:, 4096:5120], early[:, 5120:6144], reg_k[:, 0:1024]]
        pcts = early[:, 7680:7936].rearrange("p (a n) -> p a n", a=2)
        ktn = early[:, 7936:8192].rearrange("p (g s t) -> p g s t", g=2, s=2)
        pts = [early[:, 6144 + 768 * i:6912 + 768 * i] for i in range(2)]
        uT = early[:, 0:2560].rearrange("p (m n) -> p m n", m=KT)
        ktp = reg_kt[:, :].rearrange("p (g s l t) -> p g s l t", g=2, s=2, l=2)
        gain_v = reg_kt[:, :]
        pct = reg_pc[:, :].rearrange("p (q g n) -> p q g n", q=2, g=G)
        ws_in = reg_pc[:, 0:512].rearrange("p (g n) -> p g n", g=4)
        p_in = reg_pc[:, 0:768].rearrange("p (t n) -> p t n", t=3)
        pT = obT[:, 0:2, :]
        gath = [[slots[3 + k][:, 1024 * t:1024 * t + 1024] for t in range(3)] for k in range(2)]
        gain_f = slots[5][:, 0:1024]
        ysb = slots[5][:, 1024:4096].rearrange("p (t n) -> p t n", t=3)
        pgate = reg_x[:, 3072:6144].rearrange("p (t n) -> p t n", t=3)
        mix_tmp = reg_x[:, 8960:8960 + N]
        route = reg_kt

        x_tiles = [x[:, t, :] for t in range(3)]
        ident = cst[:, K_ID:K_ID + 128]
        upper = cst[:, K_UP:K_UP + 128]
        iota = cst[:, K_IOTA:K_IOTA + N]

        tab = scratch("tab", (H, 128, TABN))
        gate_rows = scratch("gate_rows", (H, NS, 3))
        y_rows = scratch("y_rows", (NE * SLOTS, D))
        y_more = scratch("y_more", (NE * MORE, D))

        bank_full = [sem(f"bank_full{i}") for i in range(8)]
        bank_read = [sem(f"bank_read{i}") for i in range(8)]
        chunk_in = [sem(f"chunk_in{i}") for i in range(6)]
        x_in, cst_sem, rows_in, hot_in, rel_in = sem("x_in"), sem("cst_in"), sem("rows_in"), sem("hot_in"), sem("rel_in")
        rel_row, small_w = sem("rel_row"), sem("small_w")
        br_in, w2_in, pg_in = sem("br_in"), sem("w2_in"), sem("pg_in")
        hist_in = [sem(f"hist_in{i}") for i in range(5)]
        keys_in = [sem(f"keys_in{i}") for i in range(2)]
        values_in = [sem(f"values_in{i}") for i in range(2)]
        tab_out, bias_in, mask_in, gate_out, gate_in = sem("tab_out"), sem("bias_in"), sem("mask_in"), sem("gate_out"), sem("gate_in")
        kv_out, out_done = sem("kv_out"), sem("out_done")
        stat_init, sq_done, var_ready, rms_ready, rstd_ready = sem("stat_init"), sem("sq_done"), sem("var_ready"), sem("rms_ready"), sem("rstd_ready")
        xn_dve, xn_act, normed = sem("xn_dve"), sem("xn_act"), sem("normed")
        pe_row, h1_pad, b1_ready = sem("pe_row"), sem("h1_pad"), sem("b1_ready")
        qs_zero, csub, cexp, pc_ready = sem("qs_zero"), sem("csub"), sem("cexp"), sem("pc_ready")
        pp_in, x1_done = sem("pp_in"), sem("x1_done")
        normalised = sem("normalised")
        pv_done, v_out, v_gelu, gm_ready = sem("pv_done"), sem("v_out"), sem("v_gelu"), sem("gm_ready")
        neg_max, exp_done, p_ready, bsn_ready = sem("neg_max"), sem("exp_done"), sem("p_ready"), sem("bsn_ready")
        gain_v_in, ws_in_s, bmix_in, bmix_ready, v_ready = sem("gain_v_in"), sem("ws_in"), sem("bmix_in"), sem("bmix_ready"), sem("v_ready")
        p_in_s, xn2_pad = sem("p_in"), sem("xn2_pad")
        gexp_in, gexp, dexp_in, dexp, assigned, ranked = sem("gexp_in"), sem("gexp"), sem("dexp_in"), sem("dexp"), sem("assigned"), sem("ranked")
        sel_ready, gathered, xe_ready, up_done, silu_done, sg_ready, turned, he_ready, down_done, ye_ready, ye_out = (
            sem("sel_ready"), sem("gathered"), sem("xe_ready"), sem("up_done"), sem("silu_done"), sem("sg_ready"),
            sem("turned"), sem("he_ready"),
            sem("down_done"), sem("ye_ready"),
            [sem(f"ye_out{i}") for i in range(2)])
        ov = {n: sem("more_" + n) for n in ("chunk0", "chunk1", "chunk2", "sel", "gathered", "xe", "up", "silu", "sg", "turned", "he",
                                            "down", "ye", "stored", "out", "rows", "added")}
        rows_back = [sem(f"rows_back{i}") for i in range(6)]
        gain_f_in, x2_done, pg_sig, y_done = sem("gain_f_in"), sem("x2_done"), sem("pg_sig"), sem("y_done")
        act_chain, dve_chain, page_in = sem("act_chain"), sem("dve_chain"), sem("page_in")

        block = ctx.enter_context(nc.Block())

        def filled(eng, job):
            bank, full, _, _ = plan[job]
            eng.wait_ge(bank_full[bank], full)
            return ps[:, bank, :]

        def release(ins, job):
            ins.then_inc(bank_read[plan[job][0]], 1)

        def evacuated(eng, job):
            bank, _, _, read = plan[job]
            eng.wait_ge(bank_read[bank], read)

        def chunk_count(chunk):
            seen = [0] * 6
            for name, slot, _ in ring_entries:
                seen[slot] += 16
                if name == chunk:
                    return slot, seen[slot]
            raise KeyError(chunk)

        def chunk(eng, name):
            slot, count = chunk_count(name)
            eng.wait_ge(chunk_in[slot], count)
            return slots[slot]

        uses = [sum(slot == s for _, slot, _ in ring_entries) for s in range(6)]
        last_use = {slot: job for _, slot, job in ring_entries}
        last_use[5] = ("mx", 7)

        hist = cache_kv[0].rearrange("a (t l) s g d -> a t l (s g) d", l=2)

        @block.sync
        def _(sp):
            sp.dma_start(x[:, 0:2, :], x_prompt.rearrange("a (t p) n -> p (a t) n", p=128)).then_inc(x_in, 16)
            sp.dma_start(x[0:NS, 2, :], x_sample.rearrange("a b n -> (a b) n")).then_inc(x_in, 16)
            win = w_in.rearrange("a (k p) n -> p (a k) n", p=128)
            sources = {}
            for c in range(3):
                sources[("kv", c)] = win[:, :, CKV + 512 * c:CKV + 512 * c + 512]
            for c in range(2):
                sources[("q", c)] = win[:, :, CQ + 512 * c:CQ + 512 * c + 512]
                sources[("v", c)] = win[:, :, CV_ + 512 * c:CV_ + 512 * c + 512]
                sources[("u", c)] = win[:, :, CU + 512 * c:CU + 512 * c + 512]
                sources[("w1", c)] = w_phi1[0, c].rearrange("(j p) n -> p j n", p=128)
                sources[("xo", c)] = w_out[0].rearrange("(k p) n -> p k n", p=128)[:, :, 512 * c:512 * c + 512]
                for j in range(2):
                    sources[("br", j, c)] = w_branch[0, j].rearrange("(k p) n -> p k n", p=128)[:, :, 512 * c:512 * c + 512]
            for c in range(4):
                sources[("gm", c)] = win[:, :, CGM + 512 * c:CGM + 512 * c + 512]

            def load_history(b):
                for half in range(2):
                    page = sp.value_load(page_sb[0:1, 2 * b + half:2 * b + half + 1], min_val=0, max_val=n_pages - 1)
                    src = hist[bass.ds(page, 1)].rearrange("a t l s d -> (a t) l s d")
                    for l in range(2):
                        sp.dma_start(cst_in[b % 5][64 * half:64 * half + 64, :, l, :], src[:, l, 0:8, :]).then_inc(hist_in[b % 5], 16)

            sp.wait_ge(rows_in, 64)
            before = {}
            for name, slot, job in ring_entries:
                if name == ("kv", 1):
                    sp.dma_start(hot_sb, hot).then_inc(hot_in, 16)
                    sp.dma_start(rel_sb[0:BUCKETS, :], rel_bias).then_inc(rel_in, 16)
                    sp.dma_start(wgn[:, :, :], w_in[0].rearrange("(k p) n -> p k n", p=128)[:, :, CGN:CGN + 48]).then_inc(small_w, 16)
                if name == ("w1", 0):
                    sp.wait_ge(page_in, 16)
                    for b in range(5):
                        load_history(b)
                    sp.dma_start(w2[:, :, :, :], w_phi2[0].rearrange("k (h p) d -> p k h d", p=128)).then_inc(w2_in, 16)
                    sp.dma_start(wr[:, :, 0:4], w_router_group[0].rearrange("(k p) n -> p k n", p=128)).then_inc(br_in, 16)
                    sp.dma_start(wr[:, :, 4:36], w_router_expert[0].rearrange("(k p) n -> p k n", p=128)).then_inc(br_in, 16)
                    sp.dma_start(biasr[:, 0:4], at(b_router_group, 0, [[0, 128], [1, 4]])).then_inc(br_in, 16)
                    sp.dma_start(biasr[:, 4:36], at(b_router_expert, 0, [[0, 128], [1, 32]])).then_inc(br_in, 16)
                if name == ("v", 0):
                    for b in range(5, NB):
                        filled(sp, ("xt", b - 4, 1))
                        load_history(b)
                if slot in before:
                    filled(sp, before[slot])
                elif slot == 4:
                    filled(sp, ("br", 0, 7))
                before[slot] = job
                src = sources[name]
                k, n = src.shape[1], src.shape[2]
                sp.dma_start(slots[slot][:, 0:k * n].rearrange("p (k n) -> p k n", k=k), src).then_inc(chunk_in[slot], 16)

            exp_src = (w_exp_gate, w_exp_up, w_exp_down)

            def load_expert(e, par, first):
                for j in range(3):
                    slot = 3 * par + j
                    if first:
                        filled(sp, last_use[slot])
                    elif j == 0:
                        sp.wait_ge(up_done, e - 1)
                    elif j == 2:
                        sp.wait_ge(down_done, e - 1)
                    k = (8, 8, 4)[j]
                    src = exp_src[j][0, bass.ds(e, 1)].rearrange("a (k p) n -> p (a k) n", p=128)
                    sp.dma_start(slots[slot].rearrange("p (k n) -> p k n", k=k), src).then_inc(chunk_in[slot], 16)

            load_expert(0, 0, True)
            load_expert(1, 1, True)
            with sp.Fori(1, NE // 2) as i:
                for par in range(2):
                    load_expert(i * 2 + par, par, False)
            sp.wait_ge(ranked, 1)
            most = sp.value_load(route[:, :].bitcast(I32)[0:1, 1019:1020], min_val=0, max_val=N)
            with sp.If(most > SLOTS):
                sp.wait_ge(down_done, NE)
                with sp.Fori(0, NE) as e:
                    sp.wait_ge(ov["down"], e * EXTRA + 1)
                    for j in range(3):
                        k = (8, 8, 4)[j]
                        src = exp_src[j][0, bass.ds(e, 1)].rearrange("a (k p) n -> p (a k) n", p=128)
                        sp.dma_start(slots[j].rearrange("p (k n) -> p k n", k=k), src).then_inc(ov[f"chunk{j}"], 16)
                sp.wait_ge(ov["down"], NE * EXTRA + 1)
            sp.wait_ge(down_done, NE - 1)
            sp.dma_start(slots[2][:, 0:2048].rearrange("p (k n) -> p k n", k=2),
                         w_ple_proj[0].rearrange("(k p) n -> p k n", p=128)).then_inc(pp_in, 16)
            for c in range(2):
                src = w_ple_gate[0].rearrange("(k p) n -> p k n", p=128)[:, :, 512 * c:512 * c + 512]
                sp.dma_start(slots[c].rearrange("p (k n) -> p k n", k=8), src).then_inc(pg_in, 16)

        @block.tensor
        def _(pe):
            def begin(job):
                bank, _, read, _ = plan[job]
                if read:
                    pe.wait_ge(bank_read[bank], read)
                return ps[:, bank, :]

            def finish(ins, job):
                ins.then_inc(bank_full[plan[job][0]], 1)

            def transposed(names, src):
                for k in range(KT):
                    out = begin((names, k))
                    for t, (t0, rows) in enumerate(TILES):
                        last = pe.transpose(out[:, t0:t0 + rows], src[0:rows, t, 128 * k:128 * k + 128],
                                            ident[0:rows, 0:rows])
                    finish(last, (names, k))

            def by_channel(job, w, m, moving, n_k=KT):
                out = begin(job)
                for k in range(n_k):
                    last = pe.matmul(out[:, 0:N], w[:, k, 128 * m:128 * m + 128], moving[:, k, :],
                                     start=(k == 0), stop=(k == n_k - 1))
                finish(last, job)

            def by_token(job, stationary, w, t, n_k=KT, cols_=slice(0, 512)):
                t0, rows = TILES[t]
                out = begin(job)
                for k in range(n_k):
                    if rows == 64 and n_k == KT:
                        last = two_halves(out, stationary[:, k, t0:t0 + rows], w[:, k, cols_], k)
                    else:
                        last = pe.matmul(out[0:rows, 0:512], stationary[:, k, t0:t0 + rows], w[:, k, cols_],
                                         start=(k == 0), stop=(k == n_k - 1))
                finish(last, job)

            def two_halves(out, lhs, rhs, k):
                for half in range(2):
                    last = pe.matmul(out[64 * half:64 * half + 64, 0:256], lhs, rhs[:, 256 * half:256 * half + 256],
                                     start=(k == 0), stop=(k == KT - 1))
                return last

            def chunk_k(name, k=8):
                return chunk(pe, name)[:, 0:4096].rearrange("p (k n) -> p k n", k=k)

            pe.wait_ge(cst_sem, 16)
            pe.wait_ge(rows_in, 64)
            out = begin("cols")
            finish(pe.transpose(out[:, 0:56], rows56[:, :], ident[0:56, 0:56]), "cols")
            pe.wait_ge(xn_dve, 2)
            pe.wait_ge(xn_act, 1)
            transposed("hT", xn)
            for k in range(KT):
                evacuated(pe, ("hT", k))
            for c in range(3):
                w = chunk_k(("kv", c))
                for s in range(3):
                    out = begin(("kv", c, s))
                    rows = (128, 128, 64)[s]
                    for k in range(KT):
                        if s == 2:
                            last = two_halves(out, hT[:, k, NP:N], w[:, k, :], k)
                        else:
                            last = pe.matmul(out[0:rows, :], hT[:, k, s:NP:2], w[:, k, :], start=(k == 0), stop=(k == KT - 1))
                    finish(last, ("kv", c, s))
                if c == 0:
                    pe.wait_ge(hot_in, 16)
                    pe.wait_ge(rel_in, 16)
                    pe.wait_ge(rel_row, 1)
                    out = begin("tab")
                    finish(pe.matmul(out[0:H, 0:TABN], rel_sb, hot_sb, start=True, stop=True), "tab")
            pe.wait_ge(small_w, 16)
            out = begin("gates")
            for t, (t0, rows) in enumerate(TILES):
                for k in range(KT):
                    last = pe.matmul(out[0:rows, 48 * t:48 * t + 48], hT[:, k, t0:t0 + rows], wgn[:, k, :],
                                     start=(k == 0), stop=(k == KT - 1))
            finish(last, "gates")
            for c in (1, 2):
                for s in range(3):
                    evacuated(pe, ("kv", c, s))
            for gp in range(2):
                out = begin(("ktp", gp))
                for s in range(2):
                    for l in range(2):
                        last = pe.transpose(out[:, (2 * s + l) * 128:(2 * s + l) * 128 + 128],
                                            kvp[:, l, s, 128 * gp:128 * gp + 128], ident)
                finish(last, ("ktp", gp))
            out = begin("ktn")
            for gp in range(2):
                for s in range(2):
                    last = pe.transpose(out[:, (2 * gp + s) * 64:(2 * gp + s) * 64 + 64],
                                        kvs[0:64, 512 + 512 * s + 128 * gp:512 + 512 * s + 128 * gp + 128],
                                        ident[0:64, 0:64])
            finish(last, "ktn")
            for s in range(NSEQ):
                if s == 0:
                    evacuated(pe, ("kv", 0, 0))
                    evacuated(pe, ("kv", 0, 1))
                else:
                    pe.wait_ge(hist_in[(s - 1) % 5], 64 * ((s - 1) // 5 + 1))
                for kv in range(2):
                    out = begin(("xt", s, kv))
                    for g in range(G):
                        src = kvc[:, kv, g, :, :].rearrange("p l d -> p (l d)") if s == 0 else \
                            cst_in[(s - 1) % 5][:, 4 * kv + g, :, :].rearrange("p l d -> p (l d)")
                        last = pe.transpose(out[:, 128 * g:128 * g + 128], src, ident)
                    finish(last, ("xt", s, kv))
            pe.wait_ge(pe_row, 2)
            for s in range(NSEQ):
                for kv in range(2):
                    evacuated(pe, ("xt", s, kv))
            for kv in range(2):
                w = chunk_k(("w1", kv), 16)
                for hid in range(2):
                    for half in (1, 0):
                        r0, nr = (18, 19) if half else (0, 18)
                        out = begin(("h1", kv, hid, half))
                        for j in range(16):
                            last = pe.matmul(out[:, 0:nr * NC], w[:, j, 128 * hid:128 * hid + 128],
                                             xt[:, kv, r0:r0 + nr, j:j + 8 * NC - 7:8],
                                             start=(j == 0), stop=(j == 15))
                        finish(last, ("h1", kv, hid, half))
            pe.wait_ge(w2_in, 16)
            for hid in range(2):
                for half in range(2):
                    evacuated(pe, ("h1", 0, hid, half))
                    evacuated(pe, ("h1", 1, hid, half))
            for half in range(2):
                out = begin(("kc", half))
                for hid in range(2):
                    last = pe.matmul(out[0:DH, 0:18 * NC], w2[:, 0, hid, :],
                                     h1k[:, hid, 18 * half:18 * half + 18, :].rearrange("p r c -> p (r c)"),
                                     start=(hid == 0), stop=(hid == 1))
                finish(last, ("kc", half))
            for job, first, n in (("vcs", 0, 8), ("vcp", 8, 4)):
                out = begin(job)
                for blk in range(n):
                    r = 4 * (first + blk)
                    for hid in range(2):
                        last = pe.matmul(out[:, DH * blk:DH * blk + DH],
                                         h1v[:, hid, r:r + 4, :].rearrange("p r c -> p (r c)"), w2[:, 1, hid, :],
                                         start=(hid == 0), stop=(hid == 1))
                finish(last, job)
            for c in range(2):
                w = chunk_k(("q", c))
                for m in range(4):
                    by_channel(("q", 4 * c + m), w, m, hT)
            def v_part(n):
                c, t, k = n // 24, n // 8 % 3, n % 8
                t0, rows = TILES[t]
                if n % 24 == 0:
                    chunk(pe, ("v", c))
                if k == 0:
                    begin(("v", c, t))
                out, w = ps[:, plan[("v", c, t)][0], :], slots[chunk_count(("v", c))[0]][:, 512 * k:512 * k + 512]
                if t == 2:
                    ins = two_halves(out, hT[:, k, NP:N], w, k)
                else:
                    ins = pe.matmul(out, hT[:, k, t0:t0 + rows], w, start=(k == 0), stop=(k == KT - 1))
                if k == 7:
                    finish(ins, ("v", c, t))

            for m in range(KT):
                evacuated(pe, ("q", m))
            for half in range(2):
                evacuated(pe, ("kc", half))
            for qt in range(2):
                n = 7 if qt == 0 else NC
                for par in range(2):
                    out = begin(("sc", qt, par))
                    for j in range(8):
                        last = pe.matmul(out[:, 16 * j:16 * j + n], qT[64 * par:64 * par + 64, j, 128 * qt:128 * qt + 128],
                                         kcT[64 * par:64 * par + 64, j // 4, 0, 0:n], start=True, stop=True)
                    finish(last, ("sc", qt, par))
            out = begin("scs")
            for b in range(NB):
                for g in range(G):
                    last = pe.matmul(out[32 * g:32 * g + 32, 16 * b:16 * b + NC], qs[:, b, g, :],
                                     kcT[:, g // 2, 1 + b, :], start=True, stop=True)
            finish(last, "scs")
            for n in range(8):
                v_part(n)
            for qt in range(2):
                pe.wait_ge(pc_ready, qt + 1)
                out = begin(("pct", qt))
                for g in range(G):
                    last = pe.transpose(out[:, 128 * g:128 * g + 128],
                                        pc[:, qt, 4 * g:4 * g + 4, :].rearrange("p h c -> p (h c)"), ident)
                finish(last, ("pct", qt))
                for n in range(4):
                    v_part(8 + 4 * qt + n)
            pe.wait_ge(pc_ready, 3)
            out = begin("pcts")
            for j in range(2):
                last = pe.transpose(out[:, 128 * j:128 * j + 128],
                                    pcsm[:, 4 * j:4 * j + 4, :].rearrange("p b c -> p (b c)"), ident)
            finish(last, "pcts")

            def step(i):
                hp, qt, par = i // 4, (i // 2) % 2, i % 2
                h = 2 * hp + par
                return h, h // HPG, h % HPG, qt, 64 * (qt + 1)

            def gm_parts(first, count):
                for n in range(first, first + count):
                    c, m, k = n // 32, n // 8, n % 8
                    if n % 32 == 0:
                        chunk(pe, ("gm", c))
                    if k == 0:
                        begin(("gm", m))
                    c0 = 512 * k + 128 * (m % 4)
                    ins = pe.matmul(ps[:, plan[("gm", m)][0], 0:N], slots[chunk_count(("gm", c))[0]][:, c0:c0 + 128],
                                    hT[:, k, :], start=(k == 0), stop=(k == 7))
                    if k == 7:
                        finish(ins, ("gm", m))

            def u_parts(first, count):
                for n in range(first, first + count):
                    m, k = n // 8, n % 8
                    if n == 0:
                        chunk(pe, ("u", 0))
                    if k == 0:
                        begin(("u", m))
                    c0 = 512 * k + 128 * m
                    ins = pe.matmul(ps[:, plan[("u", m)][0], 0:N], slots[chunk_count(("u", 0))[0]][:, c0:c0 + 128],
                                    hT[:, k, :], start=(k == 0), stop=(k == 7))
                    if k == 7:
                        finish(ins, ("u", m))

            evacuated(pe, ("ktp", 0))
            evacuated(pe, ("ktp", 1))
            evacuated(pe, "vcp")
            evacuated(pe, ("pct", 0))
            evacuated(pe, ("pct", 1))
            for i in range(35):
                if i < 32:
                    h, g, hh, qt, w_ = step(i)
                    base = 64 * (g % 2)
                    out = begin(("s", i))
                    rhs = ktp[base:base + 64, g // 2, :, :, 0:w_].rearrange("p s l t -> p (s l) t")
                    finish(pe.matmul(out[:, 0:4 * w_], qT[base:base + 64, 4 * (g // 2) + hh, 128 * qt:128 * qt + 128],
                                     rhs, start=True, stop=True), ("s", i))
                if 2 <= i <= 33:
                    h, g, hh, qt, w_ = step(i - 2)
                    pe.wait_ge(p_ready, i - 1)
                    out = begin(("pt", i - 2))
                    for j in range(4):
                        last = pe.transpose(out[0:w_, 128 * j:128 * j + 128],
                                            s_ring[(i - 2) % 3][:, w_ * j:w_ * j + w_], ident)
                    finish(last, ("pt", i - 2))
                if 2 <= i < 18:
                    v_part(2 * i + 12)
                if i >= 3:
                    h, g, hh, qt, w_ = step(i - 3)
                    par = (i - 3) % 2
                    evacuated(pe, ("pt", i - 3))
                    if par == 0:
                        out_o = begin(("o", (i - 3) // 2))
                    dst = out_o[64 * par:64 * par + 64, 0:128]
                    for j in range(4):
                        s, l = j // 2, j % 2
                        pe.matmul(dst, kvp[0:w_, l, s, 256 + DH * g:256 + DH * g + DH],
                                  pts[(i - 3) % 2][0:w_, 128 * j:128 * j + 128], start=(j == 0), stop=False)
                    last = pe.matmul(dst, vcp[32 * hh:32 * hh + 32, g, :], pct[32 * hh:32 * hh + 32, qt, g, :],
                                     start=False, stop=True)
                    if par == 1:
                        finish(last, ("o", (i - 3) // 2))
                    else:
                        last.then_inc(pv_done, 1)
                if 2 <= i < 18:
                    v_part(2 * i + 13)

            evacuated(pe, "ktn")
            evacuated(pe, "vcs")
            evacuated(pe, "pcts")
            for b in range(NB + 1):
                if b < NB:
                    pe.wait_ge(keys_in[b % 2], 48 * (b // 2 + 1))
                    for gp in range(2):
                        out = begin(("ktb", b, gp))
                        for s, stage in enumerate((slc_in, win_in)):
                            for l in range(2):
                                last = pe.transpose(out[:, (2 * s + l) * 128:(2 * s + l) * 128 + 128],
                                                    stage[b % 2][:, l, 128 * gp:128 * gp + 128], ident)
                        finish(last, ("ktb", b, gp))
                    gm_parts(16 * b, 4)
                if b == NB:
                    u_parts(0, 8)
                if b >= 1:
                    pe.wait_ge(p_ready, 32 + b)
                    src = s_ring[(b - 1) % 2]
                    for s in range(2):
                        out = begin(("pts", b - 1, s))
                        for l in range(2):
                            pe.transpose(out[:, 128 * l:128 * l + 128], src[:, 320 * s + 128 * l:320 * s + 128 * l + 128], ident)
                        finish(pe.transpose(out[0:64, 256:384], src[:, 320 * s + 256:320 * s + 320], ident), ("pts", b - 1, s))
                if b == NB:
                    u_parts(8, 8)
                if b < NB:
                    gm_parts(16 * b + 4, 4)
                    evacuated(pe, ("ktb", b, 0))
                    evacuated(pe, ("ktb", b, 1))
                    out = begin(("ss", b))
                    for g in range(G):
                        last = pe.matmul(out[32 * g:32 * g + 32, 0:512], qs[:, b, g, :],
                                         ktb[b % 2][:, g // 2, :, :, :].rearrange("p s l t -> p (s l t)"),
                                         start=True, stop=True)
                    finish(last, ("ss", b))
                    out = begin(("sn", b))
                    for g in range(G):
                        last = pe.matmul(out[32 * g:32 * g + 32, 0:128], qs[:, b, g, :],
                                         ktn[:, g // 2, :, :].rearrange("p s t -> p (s t)"), start=True, stop=True)
                    finish(last, ("sn", b))
                    gm_parts(16 * b + 8, 8)
                if b >= 1:
                    c = b - 1
                    evacuated(pe, ("pts", c, 0))
                    evacuated(pe, ("pts", c, 1))
                    pe.wait_ge(values_in[c % 2], 48 * (c // 2 + 1))
                    out = begin(("os", c))
                    for g in range(G):
                        dst = out[0:64, 32 * g:32 * g + 32]
                        for s, stage in enumerate((slc_in, win_in)):
                            for l in range(2):
                                pe.matmul(dst, stage[c % 2][:, l, 256 + DH * g:256 + DH * g + DH],
                                          pts[c % 2][:, 384 * s + 128 * l + 32 * g:384 * s + 128 * l + 32 * g + 32],
                                          start=(s == 0 and l == 0), stop=False)
                        for s in range(2):
                            pe.matmul(dst, kvs[0:64, 768 + 512 * s + DH * g:768 + 512 * s + DH * g + DH],
                                      pts[c % 2][0:64, 384 * s + 256 + 32 * g:384 * s + 256 + 32 * g + 32],
                                      start=False, stop=False)
                        r = 32 * (c % 4)
                        last = pe.matmul(dst, vcs[r:r + 32, 2 * g + c // 4, :], pcts[r:r + 32, c // 4, 32 * g:32 * g + 32],
                                         start=False, stop=True)
                    finish(last, ("os", c))

            pe.wait_ge(ws_in_s, 16)
            out = begin("ws")
            for g in range(4):
                last = pe.transpose(out[:, 128 * g:128 * g + 128], ws_in[:, g, :], ident)
            finish(last, "ws")
            for c in range(2):
                w = chunk_k(("u", c))
                for m in range(2 if c == 0 else 0, 4):
                    by_channel(("u", 4 * c + m), w, m, hT)
                if c == 0:
                    evacuated(pe, "ws")
                    out = begin("wss")
                    finish(pe.matmul(out[0:64, 0:256], cst[0:NQ, K_REP:K_REP + 64],
                                     wsT[0:NQ, :, 0:NQ].unsqueeze(2).broadcast_to([NQ, 4, NB, NQ]), start=True, stop=True), "wss")
            evacuated(pe, "wss")
            pe.wait_ge(v_ready, 3)
            for m in range(KT):
                out = begin(("mx", m))
                g = m // 2
                for t, (t0, rows) in enumerate(TILES):
                    rhs = wsT[:, g, :] if t < 2 else wssT[0:64, g, :]
                    last = pe.matmul(out[:, t0:t0 + rows], v[t][0:rows, 128 * m:128 * m + 128], rhs, start=True, stop=True)
                finish(last, ("mx", m))
            for m in range(KT):
                evacuated(pe, ("mx", m))
            for b in range(NB):
                evacuated(pe, ("os", b))
            for j in range(2):
                for c in range(2):
                    w = chunk_k(("br", j, c))
                    for m in range(4):
                        by_channel(("br", j, 4 * c + m), w, m, uT if j == 0 else obT)
            pe.wait_ge(normed, KT)
            for t in range(3):
                for c in range(2):
                    by_token(("xo", c, t), mergedT, chunk_k(("xo", c)), t)
            pe.wait_ge(xn_dve, 4)
            pe.wait_ge(xn_act, 2)
            transposed("hT2", xn2)
            for k in range(KT):
                evacuated(pe, ("hT2", k))
            pe.wait_ge(br_in, 64)
            out = begin("router")
            for t, (t0, rows) in enumerate(TILES):
                for k in range(KT):
                    last = pe.matmul(out[0:rows, 36 * t:36 * t + 36], hT[:, k, t0:t0 + rows], wr[:, k, :],
                                     start=(k == 0), stop=(k == KT - 1))
            finish(last, "router")
            pe.wait_ge(assigned, 1)
            out = begin("rank")
            ones = cst[:, K_UP + 127:K_UP + 128]
            a_all = route[:, 576:672].rearrange("p (t e) -> p t e", t=3)
            for t in range(4):
                for j in range(min(t, 2) + 1):
                    full_sum = j < t
                    lhs = ones.broadcast_to([128, 128]) if full_sum else upper
                    last = pe.matmul(out[:, 32 * t:32 * t + 32], lhs, a_all[:, j, :], start=(j == 0), stop=(j == min(t, 2)))
            finish(last, "rank")

            def gather(bufs, out, s_ready, count, s_done):
                pe.wait_ge(s_ready, count)
                for k in range(KT):
                    for t in range(3):
                        for half in range(2):
                            c0 = 128 * k + 64 * half
                            last = pe.matmul(out[64 * half:64 * half + 64, SLOTS * k:SLOTS * k + SLOTS], xn2[:, t, c0:c0 + 64],
                                             bufs[:, t, :], start=(t == 0), stop=(t == 2))
                last.then_inc(s_done, 1)

            def gate_up(w_gate, w_up, xb, out):
                ws_ = [w.rearrange("p (k n) -> p k n", k=8) for w in (w_gate, w_up)]
                for k in range(KT):
                    for part in range(2):
                        last = pe.matmul(out[64 * part:64 * part + 64, :], xb[:, k, :], ws_[part][:, k, :],
                                         start=(k == 0), stop=(k == KT - 1))
                return last

            def turn(out):
                for m in range(4):
                    last = pe.matmul(out[:, SLOTS * m:SLOTS * m + SLOTS], sg[:, 128 * m:128 * m + 128],
                                     ident[64:128, 64:128], start=True, stop=True)
                return last

            def down(w_down, hb, out):
                w = w_down.rearrange("p (k n) -> p k n", k=4)
                for m in range(4):
                    for c in range(2):
                        last = pe.matmul(out[64 * c:64 * c + 64, :], hb[:, m, :], w[:, m, 512 * c:512 * c + 512],
                                         start=(m == 0), stop=(m == 3))
                return last

            for bank in range(8):
                pe.wait_ge(bank_read[bank], plan["expert loop"][bank])
            pe.wait_ge(xn2_pad, 1)
            gather(sel[0], ps[:, 0, :], sel_ready, 1, gathered)

            def expert(i, par, last_one=False):
                e = i * 2 + par
                pe.wait_ge(xe_ready, e + 1)
                for slot in (3 * par, 3 * par + 1):
                    pe.wait_ge(chunk_in[slot], (i + uses[slot] + 1) * 16)
                gate_up(slots[3 * par], slots[3 * par + 1], xe[par], ps[:, 2 + par, :]).then_inc(up_done, 1)
                if not last_one:
                    gather(sel[1 - par], ps[:, 1 - par, :], sel_ready, e + 2, gathered)
                pe.wait_ge(sg_ready, e + 1)
                turn(ps[:, 6, :]).then_inc(turned, 1)
                pe.wait_ge(he_ready, e + 1)
                pe.wait_ge(ye_ready, e + 1)
                pe.wait_ge(chunk_in[3 * par + 2], (i + uses[3 * par + 2] + 1) * 16)
                down(slots[3 * par + 2], he[par], ps[:, 4 + par, :]).then_inc(down_done, 1)

            with pe.Fori(0, NE // 2 - 1) as i:
                expert(i, 0)
                expert(i, 1)
            expert(NE // 2 - 1, 0)
            expert(NE // 2 - 1, 1, True)
            pe.wait_ge(ranked, 1)
            most = pe.value_load(route[:, :].bitcast(I32)[0:1, 1019:1020], min_val=0, max_val=N)
            with pe.If(most > SLOTS):
                pe.sem_inc(ov["down"], 1)
                pe.wait_ge(ye_ready, NE + 2)
                with pe.Fori(0, NE) as e:
                    for blk in range(EXTRA):
                        n = e * EXTRA + blk + 1
                        gather(sel[0], ps[:, 0, :], ov["sel"], n, ov["gathered"])
                        if blk == 0:
                            pe.wait_ge(ov["chunk0"], (e + 1) * 16)
                            pe.wait_ge(ov["chunk1"], (e + 1) * 16)
                            pe.wait_ge(ov["chunk2"], (e + 1) * 16)
                        pe.wait_ge(ov["xe"], n)
                        gate_up(slots[0], slots[1], xe[0], ps[:, 2, :]).then_inc(ov["up"], 1)
                        pe.wait_ge(ov["sg"], n)
                        turn(ps[:, 6, :]).then_inc(ov["turned"], 1)
                        pe.wait_ge(ov["he"], n)
                        pe.wait_ge(ov["ye"], n)
                        down(slots[2], he[0], ps[:, 4, :]).then_inc(ov["down"], 1)
                pe.wait_ge(ov["ye"], NE * EXTRA + 1)
            pe.wait_ge(ye_ready, NE + 2)
            pe.wait_ge(p_in_s, 32)
            for k in range(2):
                out = begin(("ppT", k))
                for t, (t0, rows) in enumerate(TILES):
                    last = pe.transpose(out[:, t0:t0 + rows], p_in[0:rows, t, 128 * k:128 * k + 128], ident[0:rows, 0:rows])
                finish(last, ("ppT", k))
            evacuated(pe, ("ppT", 0))
            evacuated(pe, ("ppT", 1))
            pe.wait_ge(pp_in, 16)
            w = slots[2][:, 0:2048].rearrange("p (k n) -> p k n", k=2)
            for c in range(2):
                for t in range(3):
                    by_token(("pp", c, t), pT, w, t, 2, slice(512 * c, 512 * c + 512))
            pe.wait_ge(xn_dve, 6)
            pe.wait_ge(xn_act, 3)
            transposed("hT3", xn2)
            for k in range(KT):
                evacuated(pe, ("hT3", k))
            pe.wait_ge(pg_in, 32)
            for t in range(3):
                for c in range(2):
                    by_token(("pg", c, t), hT, slots[c].rearrange("p (k n) -> p k n", k=8), t)

        @block.scalar
        def _(act):
            chain = [0]

            def link(ins):
                chain[0] += 1
                ins.then_inc(act_chain, 1)
                act.wait_ge(act_chain, chain[0])

            act.dma_start(cst[:, :], consts).then_inc(cst_sem, 16)
            for n, src in enumerate((norm_mix, norm_ffn, norm_ple)):
                act.dma_start(rows56[8 * n:8 * n + 8, :], src.rearrange("a (k p) -> (a k) p", p=128)).then_inc(rows_in, 16)
            act.dma_start(rows56[24:56, :], pe_cmp[0].rearrange("k (j l) d -> (k j) (l d)", l=2)).then_inc(rows_in, 16)

            def squares(n, src, junk, tile_ready=None):
                act.wait_ge(stat_init, 1)
                for t, (_, rows) in enumerate(TILES):
                    if tile_ready:
                        tile_ready(t)
                    act.activation(junk[0:rows, t, :], src[t][0:rows, :], ACT.Square,
                                   accum_out=stat[0:rows, n, 0, t:t + 1]).then_inc(sq_done, 1)
                act.wait_ge(var_ready, n + 1)
                act.activation(stat[:, n, 2, :], stat[:, n, 1, :], ACT.Sqrt).then_inc(rms_ready, 1)

            def scaled(n, src, dst):
                act.wait_ge(rstd_ready, n + 1)
                act.activation(dst[:, 1, :], src[:, 1, :], ACT.Copy, scale=stat[:, n, 3, 1:2]).then_inc(xn_act, 1)

            act.wait_ge(x_in, 32)
            squares(0, x_tiles, xn)
            scaled(0, x, xn)
            evacuated(act, "cols")
            for k in range(1, KT, 2):
                src = filled(act, ("hT", k))
                release(act.activation(hT[:, k, :], src[:, 0:N], ACT.Copy, scale=cols[:, k:k + 1]), ("hT", k))
            src = filled(act, ("kv", 0, 1))
            release(act.activation(kvc[:, :, :, 1, :], src.rearrange("p (s g d) -> p s g d", s=2, g=G), ACT.Copy), ("kv", 0, 1))
            for c in (1, 2):
                src = filled(act, ("kv", c, 1))
                release(act.activation(kvp[:, 1, c - 1, :], src, ACT.Copy), ("kv", c, 1))
            src = filled(act, "gates")
            release(act.activation(gates[:, 0:2, :], src[:, 0:96].rearrange("p (t n) -> p t n", t=2), ACT.Sigmoid), "gates")
            release(act.activation(gates[0:64, 2, :], src[0:64, 96:144], ACT.Sigmoid), "gates")
            src = filled(act, ("ktp", 1))
            release(act.activation(ktp[:, 1].rearrange("p s l t -> p (s l t)"), src, ACT.Copy), ("ktp", 1))
            for s in range(NSEQ):
                src = filled(act, ("xt", s, 1))
                release(act.activation(xt[:, 1, s:s + 3 * NSEQ + 1:NSEQ, :], src.rearrange("p (g t) -> p g t", g=G), ACT.Copy), ("xt", s, 1))
            act.wait_ge(h1_pad, 1)
            for kv in range(2):
                for hid in range(2):
                    for half in (1, 0):
                        job = ("h1", kv, hid, half)
                        src = filled(act, job)[:, 0:18 * NC]
                        act.wait_ge(b1_ready, 2 * kv + hid + 1)
                        bias = b1[:, 2 * kv + hid:2 * kv + hid + 1]
                        if kv == 0:
                            release(act.activation(h1k[:, hid, 18 * half:18 * half + 18, :],
                                                   src.rearrange("p (r c) -> p r c", c=NC), ACT.Gelu_apprx_tanh, bias=bias), job)
                            continue
                        rows = src.rearrange("p (g s c) -> p g s c", g=2, s=NSEQ)
                        out = h1v[:, hid, 16 * half:16 * half + 16, 0:NC].rearrange("p (g s) c -> p g s c", g=2)
                        release(act.activation(out, rows[:, :, 1:NSEQ, :], ACT.Gelu_apprx_tanh, bias=bias), job)
                        out = h1v[:, hid, 32 + 8 * half:40 + 8 * half, 0:NC].rearrange("p (g r) c -> p g r c", g=2)
                        release(act.activation(out, rows[:, :, 0:1, :].broadcast_to([128, 2, 4, NC]),
                                               ACT.Gelu_apprx_tanh, bias=bias), job)
            act.wait_ge(qs_zero, 1)
            for m in range(KT):
                src = filled(act, ("q", m))
                g, hh = m // 2, 2 * (m % 2) + 1
                base = 64 * (g % 2)
                act.activation(qT[base:base + 64, 4 * (g // 2) + hh, :], src[64:128, 0:N], ACT.Copy, scale=0.125)
                release(act.activation(qs[base:base + 64, :, g, hh * NQ:hh * NQ + NQ],
                                       src[64:128, NP:N].rearrange("p (b t) -> p b t", b=NB), ACT.Copy, scale=0.125), ("q", m))
            def copy_v(n):
                c, t = n // 3, n % 3
                rows = TILES[t][1]
                src = filled(act, ("v", c, t))
                if t == 2:
                    for half in range(2):
                        c0 = 512 * c + 256 * half
                        release(act.activation(v[t][0:64, c0:c0 + 256], src[64 * half:64 * half + 64, 0:256], ACT.Copy), ("v", c, t))
                else:
                    release(act.activation(v[t][0:rows, 512 * c:512 * c + 512], src[0:rows, :], ACT.Copy), ("v", c, t))

            for n in range(3):
                act.wait_ge(csub, n + 1)
                if n < 2:
                    c = 7 if n == 0 else NC
                    act.activation(scm[:, :, 0:c], scm[:, :, 0:c], ACT.Exp).then_inc(cexp, 1)
                else:
                    act.activation(scm[:, 0:NB, :], scm[:, 0:NB, :], ACT.Exp).then_inc(cexp, 1)
            copy_v(0)
            copy_v(1)
            def copy_gm(m):
                src = filled(act, ("gm", m))
                release(act.activation(gmT[m // KT][:, m % KT, :], src[:, 0:N], ACT.Copy), ("gm", m))

            for i in range(34):
                if i < 32:
                    w_ = 64 * ((i // 2) % 2 + 1)
                    act.wait_ge(neg_max, i + 1)
                    for s in range(2):
                        p_ = s_ring[i % 3][:, 2 * w_ * s:2 * w_ * s + 2 * w_]
                        last = act.activation(p_, p_, ACT.Exp, bias=small[:, 8 * (i % 3) + s:8 * (i % 3) + s + 1],
                                              accum_out=small[:, 8 * (i % 3) + 2 + s:8 * (i % 3) + 3 + s])
                    last.then_inc(exp_done, 1)
                if i >= 2:
                    w_ = 64 * (((i - 2) // 2) % 2 + 1)
                    src = filled(act, ("pt", i - 2))
                    if i >= 4:
                        if i % 2:
                            filled(act, ("o", (i - 4) // 2))
                        else:
                            act.wait_ge(pv_done, (i - 4) // 2 + 1)
                    release(act.activation(pts[(i - 2) % 2][0:w_, 0:512], src[0:w_, :], ACT.Copy), ("pt", i - 2))
                if i >= 6 and i % 4 == 2 and i < 22:
                    copy_v((i + 2) // 4)
            evacuated(act, ("s", 31))
            for b in range(NB + 1):
                if b < NB:
                    src = filled(act, ("ktb", b, 1))
                    if b >= 2:
                        filled(act, ("ss", b - 2))
                    release(act.activation(ktb[b % 2][:, 1].rearrange("p s l t -> p (s l t)"), src, ACT.Copy), ("ktb", b, 1))
                if b >= 1:
                    src = filled(act, ("pts", b - 1, 0))
                    if b >= 3:
                        filled(act, ("os", b - 3))
                    else:
                        filled(act, ("o", 15))
                    release(act.activation(pts[(b - 1) % 2][:, 0:256], src[:, 0:256], ACT.Copy), ("pts", b - 1, 0))
                    release(act.activation(pts[(b - 1) % 2][0:64, 256:384], src[0:64, 256:384], ACT.Copy), ("pts", b - 1, 0))
                if b >= 1:
                    copy_gm(2 * b - 1)
                if b < NB:
                    copy_gm(2 * b)
                    act.wait_ge(neg_max, 33 + b)
                    for s in range(2):
                        p_ = s_ring[b % 2][:, 320 * s:320 * s + 320]
                        last = act.activation(p_, p_, ACT.Exp, bias=small[:, 8 * (b % 2) + s:8 * (b % 2) + s + 1],
                                              accum_out=small[:, 8 * (b % 2) + 2 + s:8 * (b % 2) + 3 + s])
                    last.then_inc(exp_done, 1)
            for c in range(2):
                for t in range(3):
                    evacuated(act, ("v", c, t))
            for t, (_, rows) in enumerate(TILES):
                act.activation(v[t][0:rows, :], v[t][0:rows, :], ACT.Gelu_apprx_tanh).then_inc(v_gelu, 1)
            act.wait_ge(v_gelu, 3)
            filled(act, ("os", NB - 1))
            squares(1, v, v_junk)
            for m in range(KT):
                src = filled(act, ("u", m))
                release(act.activation(uT[:, m, :], src[:, 0:N], ACT.Gelu_apprx_tanh), ("u", m))
            for m in range(2 * KT):
                evacuated(act, ("gm", m))
            for j in range(2):
                act.activation(gmT[j], gmT[j], ACT.Sigmoid).then_inc(gm_ready, 1)
            def projected(t):
                if t == 2:
                    for c in range(2):
                        src = filled(act, ("xo", c, 2))
                        release(act.activation(xo_half[:, c, :], src[64:128, 0:256], ACT.Copy), ("xo", c, 2))
                act.wait_ge(x1_done, 2 * t + 2)

            squares(2, x_tiles, xn2, projected)
            scaled(2, x, xn2)
            for k in range(1, KT, 2):
                src = filled(act, ("hT2", k))
                release(act.activation(hT[:, k, :], src[:, 0:N], ACT.Copy, scale=cols[:, 8 + k:9 + k]), ("hT2", k))
            act.wait_ge(gexp_in, 1)
            lg = route[:, 864:876].rearrange("p (t g) -> p t g", t=3)
            act.activation(lg, lg, ACT.Exp).then_inc(gexp, 1)
            act.wait_ge(dexp_in, 1)
            dl = route[:, 880:883]
            act.activation(dl, dl, ACT.Exp).then_inc(dexp, 1)
            def expert(i, par, first=False):
                e = i * 2 + par
                act.wait_ge(up_done, e + 1)
                act.activation(sg, ps[0:64, 2 + par, :], ACT.Silu).then_inc(silu_done, 1)
                act.wait_ge(down_done, e + 1)
                if not first:
                    act.wait_ge(ye_out[par], i * 16)
                act.activation(ye[par], ps[:, 4 + par, :], ACT.Copy).then_inc(ye_ready, 1)

            act.sem_inc(ye_ready, 2)
            expert(0, 0, True)
            expert(0, 1, True)
            with act.Fori(1, NE // 2) as i:
                expert(i, 0)
                expert(i, 1)
            act.wait_ge(ranked, 1)
            most = act.value_load(route[:, :].bitcast(I32)[0:1, 1019:1020], min_val=0, max_val=N)
            with act.If(most > SLOTS):
                for par in range(2):
                    act.wait_ge(ye_out[par], NE // 2 * 16)
                act.sem_inc(ov["ye"], 1)
                with act.Fori(0, NE) as e:
                    for blk in range(EXTRA):
                        n = e * EXTRA + blk + 1
                        act.wait_ge(ov["up"], n)
                        act.activation(sg, ps[0:64, 2, :], ACT.Silu).then_inc(ov["silu"], 1)
                        act.wait_ge(ov["down"], n + 1)
                        act.wait_ge(ov["out"], n)
                        act.activation(ye[0], ps[:, 4, :], ACT.Copy).then_inc(ov["ye"], 1)
                act.wait_ge(ov["ye"], NE * EXTRA + 1)
            act.wait_ge(v_out, 16)
            for c in range(2):
                for t in range(3):
                    src = filled(act, ("pp", c, t))
                    rows = TILES[t][1]
                    release(act.activation(pp[0:rows, t, 512 * c:512 * c + 512], src[0:rows, :], ACT.Copy), ("pp", c, t))
            squares(3, x_tiles, xn2, lambda t: act.wait_ge(x2_done, t + 1))
            scaled(3, x, xn2)
            for k in range(1, KT, 2):
                src = filled(act, ("hT3", k))
                release(act.activation(hT[:, k, :], src[:, 0:N], ACT.Copy, scale=cols[:, 16 + k:17 + k]), ("hT3", k))
            for t in range(3):
                rows = TILES[t][1]
                for c in range(2):
                    src = filled(act, ("pg", c, t))
                    if t == 2:
                        for half in range(2):
                            c0 = 512 * c + 256 * half
                            ins = act.activation(pgate[0:64, t, c0:c0 + 256], src[64 * half:64 * half + 64, 0:256], ACT.Sigmoid)
                    else:
                        ins = act.activation(pgate[0:rows, t, 512 * c:512 * c + 512], src[0:rows, :], ACT.Sigmoid)
                    ins.then_inc(pg_sig, 1)
                act.wait_ge(y_done, 2 * t + 2)
                act.activation(ysb[0:rows, t, :], x[0:rows, t, :], ACT.Square,
                               accum_out=stat[0:rows, 4, 0, t:t + 1]).then_inc(sq_done, 1)
                act.wait_ge(var_ready, 5 + t)
                act.activation(stat[:, 4, 2, t:t + 1], stat[:, 4, 1, t:t + 1], ACT.Sqrt).then_inc(rms_ready, 1)

        @block.vector
        def _(dve):
            chain = [0]

            def link(ins):
                chain[0] += 1
                ins.then_inc(dve_chain, 1)
                dve.wait_ge(dve_chain, chain[0])

            def rstd(n):
                dve.wait_ge(sq_done, 3 * (n + 1))
                dve.tensor_scalar(stat[:, n, 1, :], stat[:, n, 0, :], 1.0 / D, EPS, ALU.mult, ALU.add).then_inc(var_ready, 1)
                dve.wait_ge(rms_ready, n + 1)
                dve.reciprocal(stat[:, n, 3, :], stat[:, n, 2, :]).then_inc(rstd_ready, 1)
                dve.wait_ge(rstd_ready, n + 1)

            def scaled(n, src, dst):
                for t in (0, 2):
                    rows = TILES[t][1]
                    dve.tensor_scalar(dst[0:rows, t, :], src[0:rows, t, :], stat[0:rows, n, 3, t:t + 1], None,
                                      ALU.mult).then_inc(xn_dve, 1)

            dve.memset(stat[:, :, 0, :], 1.0).then_inc(stat_init, 1)
            dve.memset(rel_sb[BUCKETS:BUCKETS + 1, :], NEG).then_inc(rel_row, 1)
            src = filled(dve, "cols")
            release(dve.tensor_copy(cols[:, :], src[:, 0:56]), "cols")
            rstd(0)
            scaled(0, x, xn)
            evacuated(dve, "cols")
            for k in range(0, KT, 2):
                src = filled(dve, ("hT", k))
                release(dve.tensor_scalar(hT[:, k, :], src[:, 0:N], cols[:, k:k + 1], None, ALU.mult), ("hT", k))
            link(dve.memset(xt[:, :, XROWS - 1, :], 0.0))
            for kv in range(2):
                dve.tensor_copy(xt[:, kv, XROWS - 1, 0:16], cols[:, 24 + 16 * kv:40 + 16 * kv]).then_inc(pe_row, 1)
            dve.memset(h1v[:, :, :, :].rearrange("p h r c -> p (h r c)"), 0.0).then_inc(h1_pad, 1)
            for c in range(3):
                src = filled(dve, ("kv", c, 0))
                if c == 0:
                    release(dve.tensor_copy(kvc[:, :, :, 0, :], src.rearrange("p (s g d) -> p s g d", s=2, g=G)), ("kv", 0, 0))
                else:
                    release(dve.tensor_copy(kvp[:, 0, c - 1, :], src), ("kv", c, 0))
                src = filled(dve, ("kv", c, 2))
                for half in range(2):
                    c0 = 512 * c + 256 * half
                    release(dve.tensor_copy(kvs[0:64, c0:c0 + 256], src[64 * half:64 * half + 64, 0:256]), ("kv", c, 2))
                if c == 0:
                    src = filled(dve, "tab")
                    release(dve.tensor_copy(tab_sb, src[0:H, 0:TABN]), "tab")
            src = filled(dve, ("ktp", 0))
            release(dve.tensor_copy(ktp[:, 0].rearrange("p s l t -> p (s l t)"), src), ("ktp", 0))
            src = filled(dve, "ktn")
            dve.wait_ge(tab_out, 16)
            release(dve.tensor_copy(ktn[:, :, :, :].rearrange("p g s t -> p (g s t)"), src[:, 0:256]), "ktn")
            for s in range(NSEQ):
                src = filled(dve, ("xt", s, 0))
                release(dve.tensor_copy(xt[:, 0, s:s + 3 * NSEQ + 1:NSEQ, :], src.rearrange("p (g t) -> p g t", g=G)), ("xt", s, 0))
            for kv in range(2):
                for hid in range(2):
                    job = ("h1", kv, hid, 1)
                    src = filled(dve, job)
                    dve.tensor_copy(b1[:, 2 * kv + hid:2 * kv + hid + 1], src[:, 18 * NC:18 * NC + 1]).then_inc(b1_ready, 1)
                    dve.wait_ge(b1_ready, 2 * kv + hid + 1)
                    dve.sem_inc(bank_read[plan[job][0]], 1)
            for half in range(2):
                src = filled(dve, ("kc", half))[0:64, 0:18 * NC].rearrange("p (g s c) -> p g s c", g=2, s=NSEQ)
                for par in range(2):
                    release(dve.tensor_copy(kcT[64 * par:64 * par + 64, half, :, :], src[:, par, :, :]), ("kc", half))
            src = filled(dve, "vcs")
            release(dve.tensor_copy(vcs[:, :, :].rearrange("p a d -> p (a d)"), src), "vcs")
            src = filled(dve, "vcp")
            release(dve.tensor_copy(vcp[:, :, :].rearrange("p a d -> p (a d)"), src[:, 0:256]), "vcp")
            dve.memset(qs.rearrange("p b g n -> p (b g n)"), 0.0).then_inc(qs_zero, 1)
            dve.wait_ge(qs_zero, 1)
            for m in range(KT):
                src = filled(dve, ("q", m))
                g, hh = m // 2, 2 * (m % 2)
                base = 64 * (g % 2)
                dve.tensor_scalar(qT[base:base + 64, 4 * (g // 2) + hh, :], src[0:64, 0:N], 0.125, None, ALU.mult)
                release(dve.tensor_scalar(qs[base:base + 64, :, g, hh * NQ:hh * NQ + NQ],
                                          src[0:64, NP:N].rearrange("p (b t) -> p b t", b=NB), 0.125, None, ALU.mult), ("q", m))
            dve.wait_ge(kv_out, 16 * 6)
            link(dve.memset(pc.rearrange("p q h c -> p (q h c)"), 0.0))
            dve.memset(pcsm.rearrange("p b c -> p (b c)"), 0.0)
            dve.wait_ge(bias_in, 32)
            for qt in range(2):
                n = 7 if qt == 0 else NC
                e0 = 31 + 128 - 128 * qt
                for par in range(2):
                    job = ("sc", qt, par)
                    src = filled(dve, job)[:, 0:128].rearrange("p (g h c) -> p g h c", g=2, h=4)[:, :, :, 0:n]
                    out = scm.rearrange("p (g r h) c -> p g r h c", g=2, r=2)[:, :, par, :, 0:n]
                    bias = tz.rearrange("p (g r h) e -> p g r h e", g=2, r=2)[:, :, par, :, e0:e0 + 16 * n - 15:16]
                    ins = dve.tensor_tensor(out, src, bias, ALU.add)
                    release(ins, job)
                    evacuated(dve, job)
                sc_ = scm[:, :, 0:n]
                link(dve.tensor_reduce(small[:, 16:32], sc_, AX.X, ALU.max))
                dve.tensor_tensor(sc_, sc_, small[:, 16:32].unsqueeze(2).broadcast_to([128, H, n]), ALU.subtract).then_inc(csub, 1)
                dve.wait_ge(cexp, qt + 1)
                link(dve.tensor_reduce(small[:, 32:48], sc_, AX.X, ALU.add))
                link(dve.reciprocal(small[:, 48:64], small[:, 32:48]))
                link(dve.tensor_tensor(small[:, 48:64], small[:, 48:64], gates[:, qt, 0:16], ALU.mult))
                if qt == 0:
                    link(dve.tensor_scalar(small[:, 48:64], small[:, 48:64], cst[:, K_VALID:K_VALID + 1], None, ALU.mult))
                dve.tensor_tensor(pc[:, qt, :, 0:n], sc_, small[:, 48:64].unsqueeze(2).broadcast_to([128, H, n]),
                                  ALU.mult).then_inc(pc_ready, 1)
                dve.wait_ge(pc_ready, qt + 1)
            src = filled(dve, "scs")[:, 0:128].rearrange("p (b c) -> p b c", b=NB)[:, :, 0:NC]
            bias = bs[:, 31:31 + 16 * NC - 15:16].unsqueeze(1).broadcast_to([128, NB, NC])
            sc_ = scm[:, 0:NB, :]
            release(dve.tensor_tensor(sc_, src, bias, ALU.add), "scs")
            evacuated(dve, "scs")
            link(dve.tensor_reduce(small[:, 16:24], sc_, AX.X, ALU.max))
            dve.tensor_tensor(sc_, sc_, small[:, 16:24].unsqueeze(2).broadcast_to([128, NB, NC]), ALU.subtract).then_inc(csub, 1)
            dve.wait_ge(cexp, 3)
            link(dve.tensor_reduce(small[:, 32:40], sc_, AX.X, ALU.add))
            link(dve.reciprocal(small[:, 48:56], small[:, 32:40]))
            dve.wait_ge(gate_in, 16 * NB)
            link(dve.tensor_tensor(small[:, 48:56], small[:, 48:56], gsamp[:, :, 0], ALU.mult))
            dve.tensor_tensor(pcsm[:, :, 0:NC], sc_, small[:, 48:56].unsqueeze(2).broadcast_to([128, NB, NC]),
                              ALU.mult).then_inc(pc_ready, 1)
            dve.wait_ge(pc_ready, 3)
            dve.wait_ge(mask_in, 16)
            bn = bsn[:, :, :].rearrange("p b (c t) -> p (b c) t", t=NQ)
            dve.tensor_tensor(bn, bn, bs[:, PAST:PAST + NQ].unsqueeze(1).broadcast_to([128, NB * NB, NQ]), ALU.add).then_inc(bsn_ready, 1)
            dve.wait_ge(bsn_ready, 1)
            for qt in range(2):
                src = filled(dve, ("pct", qt))
                release(dve.tensor_copy(pct[:, qt].rearrange("p g n -> p (g n)"), src), ("pct", qt))
            src = filled(dve, "pcts")
            release(dve.tensor_copy(pcts[:, :, :].rearrange("p a n -> p (a n)"), src[:, 0:256]), "pcts")

            def maxima(buf, n, view):
                o = 8 * buf
                link(dve.tensor_reduce(small[:, o + 4:o + 6], view, AX.X, ALU.max))
                dve.tensor_scalar(small[:, o:o + 2], small[:, o + 4:o + 6], -1.0, None, ALU.mult).then_inc(neg_max, 1)

            def weighted(n, buf, view, gate, width):
                o = 8 * buf
                dve.wait_ge(exp_done, n + 1)
                link(dve.reciprocal(small[:, o + 6:o + 8], small[:, o + 2:o + 4]))
                link(dve.tensor_tensor(small[:, o + 6:o + 8], small[:, o + 6:o + 8], gate, ALU.mult))
                dve.tensor_tensor(view, view, small[:, o + 6:o + 8].unsqueeze(2).broadcast_to([128, 2, width]),
                                  ALU.mult).then_inc(p_ready, 1)

            for i in range(36):
                if i < 32:
                    h, qt = 2 * (i // 4) + i % 2, (i // 2) % 2
                    w_ = 64 * (qt + 1)
                    src = filled(dve, ("s", i))
                    if i >= 3:
                        filled(dve, ("pt", i - 3))
                    e0 = 128 - 128 * qt
                    bias = tz[:, h, e0:e0 + 2 * w_].rearrange("p (t l) -> p l t", l=2).unsqueeze(1).broadcast_to([128, 2, 2, w_])
                    out = s_ring[i % 3][:, 0:4 * w_]
                    release(dve.tensor_tensor(out.rearrange("p (s l t) -> p s l t", s=2, l=2),
                                              src[:, 0:4 * w_].rearrange("p (s l t) -> p s l t", s=2, l=2), bias, ALU.add), ("s", i))
                    evacuated(dve, ("s", i))
                    maxima(i % 3, i, out.rearrange("p (s n) -> p s n", s=2))
                if 1 <= i <= 32:
                    j = i - 1
                    h, qt = 2 * (j // 4) + j % 2, (j // 2) % 2
                    w_ = 64 * (qt + 1)
                    weighted(j, j % 3, s_ring[j % 3][:, 0:4 * w_].rearrange("p (s n) -> p s n", s=2),
                             gates[:, qt, 16 + h:48:16], 2 * w_)
                if i >= 5 and i % 2 == 1:
                    j = (i - 5) // 2
                    src = filled(dve, ("o", j))
                    release(dve.tensor_copy(obT[:, j // 2, 128 * (j % 2):128 * (j % 2) + 128], src[:, 0:128]), ("o", j))
            for b in range(NB + 1):
                if b < NB:
                    src = filled(dve, ("ktb", b, 0))
                    if b >= 2:
                        filled(dve, ("ss", b - 2))
                    release(dve.tensor_copy(ktb[b % 2][:, 0].rearrange("p s l t -> p (s l t)"), src), ("ktb", b, 0))
                if b >= 1:
                    c = b - 1
                    weighted(32 + c, c % 2, s_ring[c % 2].rearrange("p (s n) -> p s n", s=2), gsamp[:, c, 1:3], 320)
                    src = filled(dve, ("pts", c, 1))
                    filled(dve, ("os", b - 3) if b >= 3 else ("o", 15))
                    release(dve.tensor_copy(pts[c % 2][:, 384:640], src[:, 0:256]), ("pts", c, 1))
                    release(dve.tensor_copy(pts[c % 2][0:64, 640:768], src[0:64, 256:384]), ("pts", c, 1))
                if b < NB:
                    src = filled(dve, ("ss", b))
                    buf = s_ring[b % 2].rearrange("p (s n) -> p s n", s=2)
                    bias = bs[:, 0:PAST].rearrange("p (t l) -> p l t", l=2).unsqueeze(1).broadcast_to([128, 2, 2, 128])
                    release(dve.tensor_tensor(buf[:, :, 0:256].rearrange("p s (l t) -> p s l t", l=2),
                                              src.rearrange("p (s l t) -> p s l t", s=2, l=2), bias, ALU.add), ("ss", b))
                    src = filled(dve, ("sn", b))
                    release(dve.tensor_tensor(buf[:, :, 256:320], src[:, 0:128].rearrange("p (s t) -> p s t", s=2),
                                              bsn[:, b, :].unsqueeze(1).broadcast_to([128, 2, 64]), ALU.add), ("sn", b))
                    evacuated(dve, ("ss", b))
                    evacuated(dve, ("sn", b))
                    maxima(b % 2, 32 + b, buf)
                if b >= 1:
                    c = b - 1
                    src = filled(dve, ("os", c))[0:64, 0:128].rearrange("p (m r t) -> p m r t", m=KT, r=2)
                    for par in range(2):
                        release(dve.tensor_copy(obT[64 * par:64 * par + 64, :, NP + NQ * c:NP + NQ * c + NQ], src[:, :, par, :]), ("os", c))
            src = filled(dve, "ws")
            release(dve.tensor_tensor(wsT, src.rearrange("p (g n) -> p g n", g=4),
                                      upper.unsqueeze(1).broadcast_to([128, 4, 128]), ALU.mult), "ws")
            src = filled(dve, "wss")
            release(dve.tensor_tensor(wssT[0:64], src[0:64, 0:256].rearrange("p (g n) -> p g n", g=4),
                                      cst[0:64, K_BLK:K_BLK + 64].unsqueeze(1).broadcast_to([64, 4, 64]), ALU.mult), "wss")
            dve.wait_ge(bmix_in, 16)
            dve.tensor_copy(bmix[:, :, 128:256], bmix[:, :, 0:128]).then_inc(bmix_ready, 1)
            dve.tensor_copy(bmix[:, :, 256:320].rearrange("p g (b t) -> p g b t", b=NB),
                            bmix[:, :, 0:NQ].unsqueeze(2).broadcast_to([128, 4, NB, NQ])).then_inc(bmix_ready, 1)
            rstd(1)
            dve.wait_ge(gain_v_in, 16)
            for t, (_, rows) in enumerate(TILES):
                dve.scalar_tensor_tensor(out=v[t][0:rows, :], in0=v[t][0:rows, :], scalar=stat[0:rows, 1, 3, t:t + 1],
                                         in1=gain_v[0:rows, :], op0=ALU.mult, op1=ALU.mult).then_inc(v_ready, 1)
            dve.wait_ge(bmix_ready, 2)
            for m in range(KT):
                src = filled(dve, ("mx", m))
                job = ("mx", m)
                ins = dve.tensor_tensor(mix_tmp, src[:, 0:N], bmix[:, m // 2, :], ALU.add)
                release(ins, job)
                bank, _, read, _ = plan[job]
                dve.wait_ge(bank_read[bank], read + 1)
                evacuated(dve, ("u", m))
                release(dve.tensor_tensor(uT[:, m, :], uT[:, m, :], mix_tmp, ALU.mult), job)
                evacuated(dve, job)
            for m in range(KT):
                src = filled(dve, ("br", 0, m))
                dve.wait_ge(gm_ready, 1)
                release(dve.tensor_tensor(mergedT[:, m, :], src[:, 0:N], gmT[0][:, m, :], ALU.mult), ("br", 0, m))
            for m in range(KT):
                src = filled(dve, ("br", 1, m))
                dve.wait_ge(gm_ready, 2)
                evacuated(dve, ("br", 0, m))
                release(dve.tensor_tensor(gmT[1][:, m, :], src[:, 0:N], gmT[1][:, m, :], ALU.mult), ("br", 1, m))
                evacuated(dve, ("br", 1, m))
                dve.tensor_tensor(mergedT[:, m, :], mergedT[:, m, :], gmT[1][:, m, :], ALU.add).then_inc(normed, 1)
            dve.memset(xn2[64:128, 2, :], 0.0).then_inc(xn2_pad, 1)
            for t in range(2):
                for c in range(2):
                    src = filled(dve, ("xo", c, t))
                    xs = x[:, t, 512 * c:512 * c + 512]
                    release(dve.tensor_tensor(xs, xs, src, ALU.add), ("xo", c, t))
                    evacuated(dve, ("xo", c, t))
                    dve.sem_inc(x1_done, 1)
            for c in range(2):
                src = filled(dve, ("xo", c, 2))
                xs = x[0:64, 2, 512 * c:512 * c + 256]
                release(dve.tensor_tensor(xs, xs, src[0:64, 0:256], ALU.add), ("xo", c, 2))
                evacuated(dve, ("xo", c, 2))
                xs = x[0:64, 2, 512 * c + 256:512 * c + 512]
                dve.tensor_tensor(xs, xs, xo_half[:, c, :], ALU.add).then_inc(x1_done, 1)
            rstd(2)
            scaled(2, x, xn2)
            for k in range(0, KT, 2):
                src = filled(dve, ("hT2", k))
                release(dve.tensor_scalar(hT[:, k, :], src[:, 0:N], cols[:, 8 + k:9 + k], None, ALU.mult), ("hT2", k))
            def r3(a, n):
                return route[:, a:a + 3 * n].rearrange("p (t n) -> p t n", t=3)
            logits, g8, gtop, gidx = r3(0, 36), r3(108, 8), r3(132, 8), route[:, :].bitcast(U32)[:, 156:180].rearrange("p (t n) -> p t n", t=3)
            ohg, prod, se8, stop_, sidx = r3(180, 4), r3(192, 32), r3(288, 8), r3(312, 8), route[:, :].bitcast(U32)[:, 336:360].rearrange("p (t n) -> p t n", t=3)
            a1, a2, aa = r3(360, 32), r3(456, 32), r3(576, 32)
            ranks, tmp = r3(672, 32), r3(768, 32)
            lg4, dl = r3(864, 4), route[:, 880:883]
            gf, e1, e2, i1, pg, w1_, w2_, den = (route[:, 884 + 3 * j:887 + 3 * j] for j in range(8))
            dest = route[:, 908:914]
            desti = route[:, :].bitcast(U32)[:, 914:920]
            rank_a = route[:, 920:1016].rearrange("p (e t) -> p e t", e=NE)
            rank12, w_more, dest_more = route[:, 108:114], route[:, 114:120], route[:, 120:126]
            mostf = route[:, 1018:1019]
            iota_e = cst[:, K_E:K_E + NE]

            def bc(ap, n):
                return ap.unsqueeze(2).broadcast_to([128, 3, n])

            link(dve.memset(logits, 0.0))
            link(dve.memset(g8, -3e38))
            src = filled(dve, "router")
            dve.wait_ge(br_in, 64)
            release(dve.tensor_tensor(logits[:, 0:2, :], src[:, 0:72].rearrange("p (t n) -> p t n", t=2),
                                      biasr[:, :].unsqueeze(1).broadcast_to([128, 2, 36]), ALU.add), "router")
            release(dve.tensor_tensor(logits[0:64, 2, :], src[0:64, 72:108], biasr[0:64, :], ALU.add), "router")
            evacuated(dve, "router")
            link(dve.tensor_copy(g8[:, :, 0:4], logits[:, :, 0:4]))
            for t in range(3):
                link(dve.max(out=gtop[:, t, :], in_=g8[:, t, :]))
                link(dve.max_index(out=gidx[:, t, :], in_max=gtop[:, t, :], in_values=g8[:, t, :]))
            dve.tensor_tensor(lg4, g8[:, :, 0:4], bc(gtop[:, :, 0], 4), ALU.subtract).then_inc(gexp_in, 1)
            link(dve.tensor_copy(gf, gidx[:, :, 0]))
            link(dve.tensor_tensor(ohg, iota_e[:, 0:4].unsqueeze(1).broadcast_to([128, 3, 4]), bc(gf, 4), ALU.is_equal))
            for t in range(3):
                ins = dve.tensor_tensor(prod[:, t, :].rearrange("p (g j) -> p g j", g=4),
                                        logits[:, t, 4:36].rearrange("p (g j) -> p g j", g=4),
                                        ohg[:, t, :].unsqueeze(2).broadcast_to([128, 4, 8]), ALU.mult)
            link(ins)
            link(dve.tensor_reduce(se8, prod.rearrange("p t (g j) -> p t j g", g=4), AX.X, ALU.add))
            for t in range(3):
                link(dve.max(out=stop_[:, t, :], in_=se8[:, t, :]))
                link(dve.max_index(out=sidx[:, t, :], in_max=stop_[:, t, :], in_values=se8[:, t, :]))
            dve.tensor_tensor(dl, stop_[:, :, 1], stop_[:, :, 0], ALU.subtract).then_inc(dexp_in, 1)
            for k, (e_, a_) in enumerate(((e1, a1), (e2, a2))):
                link(dve.tensor_copy(i1, sidx[:, :, k]))
                link(dve.scalar_tensor_tensor(out=e_, in0=gf, scalar=float(EPG), in1=i1, op0=ALU.mult, op1=ALU.add))
                link(dve.tensor_tensor(a_, iota_e.unsqueeze(1).broadcast_to([128, 3, NE]), bc(e_, NE), ALU.is_equal))
                link(dve.memset(a_[64:128, 2, :], 0.0))
            dve.tensor_tensor(aa, a1, a2, ALU.add).then_inc(assigned, 1)
            dve.wait_ge(gexp, 1)
            link(dve.tensor_reduce(den, lg4, AX.X, ALU.add))
            link(dve.reciprocal(pg, den))
            dve.wait_ge(dexp, 1)
            link(dve.tensor_scalar(den, dl, 1.0, None, ALU.add))
            link(dve.reciprocal(den, den))
            link(dve.tensor_tensor(w1_, pg, den, ALU.mult))
            link(dve.tensor_tensor(w2_, w1_, dl, ALU.mult))
            src = filled(dve, "rank")
            dve.tensor_reduce(mostf, src[:, 96:128], AX.X, ALU.max)
            release(dve.tensor_copy(ranks, src[:, 0:96].rearrange("p (t e) -> p t e", t=3)), "rank")
            evacuated(dve, "rank")
            link(dve.tensor_tensor(tmp, aa, ranks, ALU.mult))
            link(dve.tensor_scalar(rank_a.rearrange("p e t -> p t e"), tmp, -1.0, None, ALU.add))
            dve.tensor_copy(route[:, :].bitcast(I32)[:, 1019:1020], mostf).then_inc(ranked, 1)
            for k, (e_, a_) in enumerate(((e1, a1), (e2, a2))):
                link(dve.tensor_tensor(tmp, a_, ranks, ALU.mult))
                link(dve.tensor_reduce(i1, tmp, AX.X, ALU.add))
                rk, wm, wk = rank12[:, 3 * k:3 * k + 3], w_more[:, 3 * k:3 * k + 3], (w1_, w2_)[k]
                link(dve.tensor_scalar(rk, i1, -1.0, None, ALU.add))
                link(dve.tensor_scalar(i1, rk, float(SLOTS - 1), None, ALU.min))
                dve.scalar_tensor_tensor(out=dest[:, 3 * k:3 * k + 3], in0=e_, scalar=float(SLOTS), in1=i1, op0=ALU.mult, op1=ALU.add)
                link(dve.tensor_scalar(wm, rk, float(SLOTS), None, ALU.is_ge))
                link(dve.tensor_tensor(wm, wm, wk, ALU.mult))
                link(dve.tensor_tensor(wk, wk, wm, ALU.subtract))
                link(dve.tensor_scalar(i1, rk, -float(SLOTS), 0.0, ALU.add, ALU.max))
                link(dve.scalar_tensor_tensor(out=dest_more[:, 3 * k:3 * k + 3], in0=e_, scalar=float(MORE), in1=i1, op0=ALU.mult, op1=ALU.add))
            link(dve.tensor_copy(route[:, :].bitcast(U32)[:, 126:132], dest_more))
            dve.tensor_copy(desti, dest).then_inc(ranked, 1)
            dve.wait_ge(ranked, 2)

            def select(e, buf, first):
                return dve.tensor_tensor(buf, iota[:, first:first + SLOTS].unsqueeze(1).broadcast_to([128, 3, SLOTS]),
                                         rank_a[:, bass.ds(e, 1), :].rearrange("p a t -> p (a t)").unsqueeze(2).broadcast_to([128, 3, SLOTS]),
                                         ALU.is_equal)

            gain = cols[:, 8:16].unsqueeze(2).broadcast_to([128, KT, SLOTS])

            select(0, sel[0], 0).then_inc(sel_ready, 1)

            def expert_steps(i, par, last_one=False):
                e = i * 2 + par
                if not last_one:
                    dve.wait_ge(gathered, e + 1)
                    select(e + 1, sel[1 - par], 0).then_inc(sel_ready, 1)
                dve.wait_ge(gathered, e + 1)
                dve.tensor_tensor(xe[par], ps[:, par, :].rearrange("p (k n) -> p k n", k=KT), gain, ALU.mult).then_inc(xe_ready, 1)
                dve.wait_ge(silu_done, e + 1)
                dve.wait_ge(up_done, e + 1)
                dve.tensor_tensor(sg, sg, ps[64:128, 2 + par, :], ALU.mult).then_inc(sg_ready, 1)
                dve.wait_ge(turned, e + 1)
                dve.tensor_copy(he[par].rearrange("p m n -> p (m n)"), ps[:, 6, 0:256]).then_inc(he_ready, 1)

            with dve.Fori(0, NE // 2 - 1) as i:
                expert_steps(i, 0)
                expert_steps(i, 1)
            expert_steps(NE // 2 - 1, 0)
            expert_steps(NE // 2 - 1, 1, True)
            most = dve.value_load(route[:, :].bitcast(I32)[0:1, 1019:1020], min_val=0, max_val=N)
            with dve.If(most > SLOTS):
                dve.wait_ge(ye_ready, NE + 2)
                with dve.Fori(0, NE) as e:
                    for blk in range(EXTRA):
                        n = e * EXTRA + blk + 1
                        select(e, sel[0], SLOTS * (blk + 1)).then_inc(ov["sel"], 1)
                        dve.wait_ge(ov["gathered"], n)
                        dve.tensor_tensor(xe[0], ps[:, 0, :].rearrange("p (k n) -> p k n", k=KT), gain, ALU.mult).then_inc(ov["xe"], 1)
                        dve.wait_ge(ov["silu"], n)
                        dve.tensor_tensor(sg, sg, ps[64:128, 2, :], ALU.mult).then_inc(ov["sg"], 1)
                        dve.wait_ge(ov["turned"], n)
                        dve.tensor_copy(he[0].rearrange("p m n -> p (m n)"), ps[:, 6, 0:256]).then_inc(ov["he"], 1)
                        dve.wait_ge(ov["down"], n + 1)
                dve.wait_ge(ov["rows"], 96)
                for t, (_, rows) in enumerate(TILES):
                    for k in range(2):
                        dve.scalar_tensor_tensor(out=x[0:rows, t, :], in0=gath[k][t][0:rows, :],
                                                 scalar=w_more[0:rows, 3 * k + t:3 * k + t + 1],
                                                 in1=x[0:rows, t, :], op0=ALU.mult, op1=ALU.add).then_inc(ov["added"], 1)
                        dve.wait_ge(ov["added"], 2 * t + k + 1)
            for k in range(2):
                src = filled(dve, ("ppT", k))
                release(dve.tensor_copy(pT[:, k, :], src[:, 0:N]), ("ppT", k))
            for t, (_, rows) in enumerate(TILES):
                for k, w_ in enumerate((w1_, w2_)):
                    dve.wait_ge(rows_back[2 * t + k], 16)
                    ins = dve.scalar_tensor_tensor(out=x[0:rows, t, :], in0=gath[k][t][0:rows, :], scalar=w_[0:rows, t:t + 1],
                                                   in1=x[0:rows, t, :], op0=ALU.mult, op1=ALU.add)
                    if k == 0:
                        link(ins)
                ins.then_inc(x2_done, 1)
            rstd(3)
            scaled(3, x, xn2)
            for k in range(0, KT, 2):
                src = filled(dve, ("hT3", k))
                release(dve.tensor_scalar(hT[:, k, :], src[:, 0:N], cols[:, 16 + k:17 + k], None, ALU.mult), ("hT3", k))
            dve.wait_ge(gain_f_in, 16)
            for t, (_, rows) in enumerate(TILES):
                for c in range(2):
                    part = pgate[0:rows, t, 512 * c:512 * c + 512]
                    xs = x[0:rows, t, 512 * c:512 * c + 512]
                    dve.wait_ge(pg_sig, 2 * t + c + 1)
                    evacuated(dve, ("pp", c, t))
                    link(dve.tensor_tensor(part, part, pp[0:rows, t, 512 * c:512 * c + 512], ALU.mult))
                    dve.tensor_tensor(xs, xs, part, ALU.add).then_inc(y_done, 1)
                dve.wait_ge(sq_done, 13 + t)
                dve.tensor_scalar(stat[:, 4, 1, t:t + 1], stat[:, 4, 0, t:t + 1], 1.0 / D, EPS, ALU.mult, ALU.add).then_inc(var_ready, 1)
                dve.wait_ge(rms_ready, 5 + t)
                link(dve.reciprocal(stat[:, 4, 3, t:t + 1], stat[:, 4, 2, t:t + 1]))
                dve.scalar_tensor_tensor(out=ysb[0:rows, t, :], in0=x[0:rows, t, :], scalar=stat[0:rows, 4, 3, t:t + 1],
                                         in1=gain_f[0:rows, :], op0=ALU.mult, op1=ALU.mult).then_inc(normalised, 1)

        @block.gpsimd
        def _(pool):
            pool.dma_start(page_sb[:, :], page_table.rearrange("b p -> (b p)").unsqueeze(0)).then_inc(page_in, 16)
            pool.dma_start(bsn[:, :, :], at(other, 0, [[0, 128], [64, NB], [1, 64]])).then_inc(mask_in, 16)
            evacuated(pool, "tab")
            pool.dma_start(tab, tab_sb.unsqueeze(1).broadcast_to([H, 128, TABN])).then_inc(tab_out, 16)

            def page_rows(b, half):
                page = pool.value_load(page_sb[0:1, 2 * b + half:2 * b + half + 1], min_val=0, max_val=n_pages - 1)
                return hist[bass.ds(page, 1)].rearrange("a t l s d -> (a t) l s d")

            pool.wait_ge(tab_out, 16)
            pool.dma_start(bs[:, :], at(tab, NQ - 1, [[128 * TABN, H], [TABN - 1, NQ], [1, PAST + NQ]])).then_inc(bias_in, 16)
            for c in range(3):
                for s in range(3):
                    evacuated(pool, ("kv", c, s))
            rows = kv_rows_prompt.rearrange("a b (t l) s g d -> (a b t) l (s g d)", l=2)
            for l in range(2):
                pool.dma_start(rows[:, l, 0:512].rearrange("t (a d) -> t a d", d=DH),
                               kvc[:, :, :, l, :].rearrange("p s g d -> p (s g) d")).then_inc(kv_out, 16)
            pool.dma_start(rows[:, :, 512:1024], kvp[:, :, 0, :]).then_inc(kv_out, 16)
            pool.dma_start(win_prompt.rearrange("a b (t l) s g d -> (a b t) l (s g d)", l=2), kvp[:, :, 1, :]).then_inc(kv_out, 16)
            pool.dma_start(kv_rows_sample.rearrange("a b t s g d -> (a b t) (s g d)"), kvs[0:64, 0:1024]).then_inc(kv_out, 16)
            wnew = win_sample.rearrange("a b t s g d -> (a b) t (s g d)")
            pool.dma_start(wnew[:, PAST - NQ:PAST, :], kvs[0:64, 1024:1536]).then_inc(kv_out, 16)
            evacuated(pool, "gates")
            for br in range(3):
                pool.dma_start(at(gate_rows, br, [[3, NS], [3 * NS, H]]), gates[0:64, 2, H * br:H * br + H],
                               allow_slow_non_contiguous=True).then_inc(gate_out, 16)
            filled(pool, ("h1", 1, 1, 0))
            pool.dma_start(tz, at(tab, MAXD - 128, [[TABN - 1, 128], [128 * TABN, H], [1, 256]])).then_inc(bias_in, 16)
            pool.wait_ge(gate_out, 48)
            for b in range(NB):
                pool.dma_start(gsamp[:, b, :], at(gate_rows, 3 * NQ * b, [[3 * NS, H], [3, NQ], [1, 3]])).then_inc(gate_in, 16)
            filled(pool, "vcp")
            for b in range(NB):
                if b == 2:
                    filled(pool, ("o", 15))
                    pool.dma_start(gain_v, at(v_norm, 0, [[0, 128], [1, D]])).then_inc(gain_v_in, 16)
                    pool.dma_start(ws_in, w_spatial[0].rearrange("g r s -> r g s")).then_inc(ws_in_s, 16)
                for part, sems in ((0, keys_in), (1, values_in)):
                    if b >= 2:
                        filled(pool, ("ktb", b - 2, 1) if part == 0 else ("os", b - 2))
                    cols_ = slice(256 * part, 256 * part + 256)
                    for half in range(2):
                        pool.dma_start(slc_in[b % 2][64 * half:64 * half + 64, :, cols_].rearrange("p l (a d) -> p l a d", d=DH),
                                       page_rows(b, half)[:, :, 8 + 4 * part:12 + 4 * part, :]).then_inc(sems[b % 2], 16)
                    pool.dma_start(win_in[b % 2][:, :, cols_],
                                   state_win_kv[0, b].rearrange("(t l) s g d -> t l (s g d)", l=2)[:, :, cols_]).then_inc(sems[b % 2], 16)
            wold = state_win_kv.rearrange("a b t s g d -> (a b) t (s g d)")
            pool.dma_start(wnew[:, 0:PAST - NQ, :], wold[:, NQ:PAST, :]).then_inc(out_done, 16)
            filled(pool, ("os", NB - 1))
            pool.dma_start(bmix[:, :, 0:128], at(b_spatial, 0, [[0, 128], [128, 4], [1, 128]])).then_inc(bmix_in, 16)
            filled(pool, "ws")
            pool.dma_start(p_in[:, 0:2, :], p_prompt.rearrange("a b (t p) n -> p (a b t) n", p=128)).then_inc(p_in_s, 16)
            pool.dma_start(p_in[0:64, 2, :], p_sample.rearrange("a b t n -> (a b t) n")).then_inc(p_in_s, 16)
            pool.wait_ge(v_ready, 3)
            pool.dma_start(chunk_v_sample.rearrange("a b t n -> (a b t) n"), v[2][0:64, :]).then_inc(v_out, 16)

            first_rows = y_rows.rearrange("(e r) n -> e r n", e=NE)
            more_rows = y_more.rearrange("(e r) n -> e r n", e=NE)

            def halves(rows_dram):
                return rows_dram.rearrange("r (c n) -> c r n", c=2)

            def gather_rows(rows_dram, first_col, sems):
                idx = route[:, :].bitcast(U32)[:, first_col:first_col + 6]
                for t, (_, rows) in enumerate(TILES):
                    for k in range(2):
                        pool.indirect_dma_start(gath[k][t][0:rows, :], None, rows_dram,
                                                bass.IndirectOffsetOnAxis(ap=idx[0:rows, 3 * k + t:3 * k + t + 1], axis=0)
                                                ).then_inc(sems[2 * t + k], 16)

            with pool.Fori(0, NE // 2) as i:
                for par in range(2):
                    pool.wait_ge(ye_ready, i * 2 + par + 3)
                    dst = first_rows[bass.ds(i * 2 + par, 1)].rearrange("a r n -> (a r) n")
                    pool.dma_start(halves(dst), ye[par]).then_inc(ye_out[par], 16)
            for par in range(2):
                pool.wait_ge(ye_out[par], NE // 2 * 16)
            pool.wait_ge(ranked, 2)
            most = pool.value_load(route[:, :].bitcast(I32)[0:1, 1019:1020], min_val=0, max_val=N)
            with pool.If(most > SLOTS):
                pool.sem_inc(ov["out"], 1)
                with pool.Fori(0, NE) as e:
                    for blk in range(EXTRA):
                        n = e * EXTRA + blk + 1
                        pool.wait_ge(ov["ye"], n + 1)
                        dst = more_rows[bass.ds(e, 1), SLOTS * blk:SLOTS * (blk + 1)].rearrange("a r n -> (a r) n")
                        pool.dma_start(halves(dst), ye[0]).then_inc(ov["stored"], 16)
                        pool.wait_ge(ov["stored"], n * 16)
                        pool.sem_inc(ov["out"], 1)
                gather_rows(y_more, 126, [ov["rows"]] * 6)
                pool.wait_ge(ov["added"], 6)
            pool.wait_ge(down_done, NE)
            gather_rows(y_rows, 914, rows_back)
            pool.dma_start(gain_f, at(final_norm, 0, [[0, 128], [1, D]])).then_inc(gain_f_in, 16)
            for t in range(2):
                pool.wait_ge(normalised, t + 1)
                pool.dma_start(y_prompt[0, 128 * t:128 * t + 128, :], ysb[:, t, :]).then_inc(out_done, 16)
            pool.wait_ge(normalised, 3)
            pool.dma_start(y_sample.rearrange("a b n -> (a b) n"), ysb[0:64, 2, :]).then_inc(out_done, 16)
            pool.wait_ge(out_done, 64)
            pool.wait_ge(v_out, 16)
            pool.wait_ge(kv_out, 16 * 6)


_INS = ['x_prompt', 'x_sample', 'cache_kv', 'state_win_kv', 'page_table', 'p_prompt', 'p_sample', 'rel_bias',
        'norm_mix', 'w_in', 'v_norm', 'w_spatial', 'b_spatial', 'pe_cmp', 'w_phi1', 'w_phi2', 'w_branch', 'w_out',
        'norm_ffn', 'w_router_group', 'b_router_group', 'w_router_expert', 'b_router_expert',
        'w_exp_gate', 'w_exp_up', 'w_exp_down', 'norm_ple', 'w_ple_gate', 'w_ple_proj', 'final_norm']
_OUTS = [('y_prompt', (1, NP, D)), ('y_sample', (NB, NQ, D)), ('kv_rows_prompt', (1, 1, NP, 4, G, DH)),
         ('kv_rows_sample', (1, NB, NQ, 4, G, DH)), ('win_prompt', (1, 1, NP, 2, G, DH)),
         ('win_sample', (1, NB, PAST, 2, G, DH)), ('chunk_v_sample', (1, NB, NQ, D))]


def kernel(**inputs):
    import concourse.bacc as bacc
    from concourse.bass_utils import run_bass_kernel_spmd

    nc = bacc.Bacc("TRN2", target_bir_lowering=False, num_devices=1)
    consts, hot, other = shape_constants()
    arrays, args = {}, []
    for name, a in [(n, inputs[n]) for n in _INS] + [("consts", consts), ("hot", hot), ("other", other)]:
        a = np.ascontiguousarray(a)
        arrays[f"in_{name}_dram"] = a
        args.append(nc.dram_tensor(f"in_{name}_dram", a.shape, mybir.dt.from_np(a.dtype), kind="ExternalInput").ap())
    for name, shape in _OUTS:
        args.append(nc.dram_tensor(f"out_{name}_dram", shape, F32, kind="ExternalOutput").ap())
    build(nc, *args)
    r = run_bass_kernel_spmd(nc, [arrays], core_ids=[0])
    return tuple(r.results[0][f"out_{name}_dram"] for name, _ in _OUTS)
```
